# Optimizing a Trainium2 kernel written in Bass

```python
import jax, jax.numpy as jnp
from jax import lax
import numpy as np

D_MODEL = 1024
BATCH = 1
SEQ = 1024
DEPTH = 1

PLE_DIM = 256
BLOCK = 128
EPS = 1e-6
ROPE_THETA = 10000.0
RET_HEADS = 4
RET_DK = 128
RET_DV = 128
RET_QKW = RET_HEADS * RET_DK
RET_VW = RET_HEADS * RET_DV
SGU_GROUPS = 4
SGU_GROUP_CH = 128
SGU_WIDTH = SGU_GROUPS * SGU_GROUP_CH
ATT_HEADS = 8
ATT_KV_HEADS = 2
ATT_DH = 64
ATT_GROUP = ATT_HEADS // ATT_KV_HEADS
ATT_QW = ATT_HEADS * ATT_DH
ATT_KVW = ATT_KV_HEADS * ATT_DH
WINDOW = 128
NEG_INF = -1e30
PEER_HEADS = 8
PEER_KEYS = 128
PEER_EXPERTS = PEER_KEYS * PEER_KEYS
PEER_QDIM = 256
PEER_TOPK = 16
IN_WIDTHS = (RET_QKW, RET_QKW, RET_VW, RET_VW,
             SGU_WIDTH, SGU_WIDTH,
             ATT_QW, ATT_KVW, ATT_KVW,
             D_MODEL, D_MODEL, D_MODEL)
D_IN = sum(IN_WIDTHS)

kernel_name = 'hybrid_retention_sgu_swa_peer_encoder'

def rms_norm(x, g):
    xf = x.astype(jnp.float32)
    y = xf * lax.rsqrt(jnp.mean(xf * xf, axis=-1, keepdims=True) + EPS)
    return (y * g.astype(jnp.float32)).astype(x.dtype)

def rope_tables(seq, dim):
    inv = 1.0 / (ROPE_THETA ** (jnp.arange(0, dim, 2, dtype=jnp.float32) / dim))
    ang = jnp.arange(seq, dtype=jnp.float32)[:, None] * inv[None, :]
    return jnp.cos(ang), jnp.sin(ang)

def apply_rope(x, cos, sin):
    x1, x2 = jnp.split(x.astype(jnp.float32), 2, axis=-1)
    c = cos[None, :, None, :]
    s = sin[None, :, None, :]
    return jnp.concatenate([x1 * c - x2 * s, x2 * c + x1 * s], axis=-1).astype(x.dtype)

def split_columns(z):
    offs = [int(o) for o in np.cumsum(IN_WIDTHS)[:-1]]
    return jnp.split(z, offs, axis=-1)

def retention_chunkwise(q, k, v, log_gamma, strict):
    B, H, S, dk = q.shape
    dv = v.shape[-1]
    C = BLOCK
    N = S // C
    qc = q.reshape(B, H, N, C, dk)
    kc = k.reshape(B, H, N, C, dk)
    vc = v.reshape(B, H, N, C, dv)
    idx = jnp.arange(C, dtype=jnp.float32)
    diff = idx[:, None] - idx[None, :]
    mask = (diff > 0) if strict else (diff >= 0)
    lg = log_gamma[:, None, None]
    decay = jnp.where(mask[None], jnp.exp(lg * jnp.maximum(diff, 0.0)[None]), 0.0)
    scores = jnp.einsum('bhncd,bhnjd->bhncj', qc, kc) * decay[None, :, None]
    out_inner = jnp.einsum('bhncj,bhnje->bhnce', scores, vc)
    k_w = jnp.exp(log_gamma[:, None] * (C - 1 - idx)[None, :])
    kv = jnp.einsum('bhncd,hc,bhnce->bhnde', kc, k_w, vc)
    chunk_decay = jnp.exp(log_gamma * C)[None, :, None, None]

    def step(state, kv_n):
        return state * chunk_decay + kv_n, state

    _, prev = lax.scan(step, jnp.zeros((B, H, dk, dv), jnp.float32), jnp.moveaxis(kv, 2, 0))
    prev = jnp.moveaxis(prev, 0, 2)
    q_w = jnp.exp(log_gamma[:, None] * (idx + 1.0)[None, :])
    out_cross = jnp.einsum('bhncd,hc,bhnde->bhnce', qc, q_w, prev)
    return (out_inner + out_cross).reshape(B, H, S, dv)

def retention_branch(q, k, v, g, decay_logit, gn_gain, cos, sin):
    B, S, _ = q.shape
    q = apply_rope(q.reshape(B, S, RET_HEADS, RET_DK), cos, sin)
    k = apply_rope(k.reshape(B, S, RET_HEADS, RET_DK), cos, sin)
    v = v.reshape(B, S, RET_HEADS, RET_DV)
    qh = jnp.transpose(q, (0, 2, 1, 3)).astype(jnp.float32)
    kh = jnp.transpose(k, (0, 2, 1, 3)).astype(jnp.float32) * (RET_DK ** -0.5)
    vh = jnp.transpose(v, (0, 2, 1, 3)).astype(jnp.float32)
    log_g = jax.nn.log_sigmoid(decay_logit.astype(jnp.float32))
    fwd = retention_chunkwise(qh, kh, vh, log_g[0], strict=False)
    bwd = retention_chunkwise(qh[:, :, ::-1], kh[:, :, ::-1], vh[:, :, ::-1], log_g[1], strict=True)[:, :, ::-1]
    y = jnp.transpose(fwd + bwd, (0, 2, 1, 3))
    y = y * lax.rsqrt(jnp.mean(y * y, axis=-1, keepdims=True) + EPS)
    y = (y * gn_gain.astype(jnp.float32).reshape(RET_HEADS, RET_DV)).reshape(B, S, RET_VW)
    return (jax.nn.silu(g.astype(jnp.float32)) * y).astype(q.dtype)

def sgu_branch(u, v, ln_g, ln_b, w_s, b_s):
    B, S, _ = u.shape
    N = S // BLOCK
    uf = jax.nn.gelu(u.astype(jnp.float32), approximate=False)
    vf = jax.nn.gelu(v.astype(jnp.float32), approximate=False)
    mu = jnp.mean(vf, axis=-1, keepdims=True)
    var = jnp.mean(jnp.square(vf - mu), axis=-1, keepdims=True)
    vf = (vf - mu) * lax.rsqrt(var + EPS) * ln_g.astype(jnp.float32) + ln_b.astype(jnp.float32)
    vf = vf.reshape(B, N, BLOCK, SGU_GROUPS, SGU_GROUP_CH)
    mixed = jnp.einsum('gij,bnjgc->bnigc', w_s.astype(jnp.float32), vf)
    mixed = mixed + jnp.transpose(b_s.astype(jnp.float32))[None, None, :, :, None]
    return (uf * mixed.reshape(B, S, SGU_WIDTH)).astype(u.dtype)

def window_attention(q, k, v, q_gain, k_gain, sink, cos, sin):
    B, S, _ = q.shape
    N = S // BLOCK
    q = apply_rope(rms_norm(q.reshape(B, S, ATT_HEADS, ATT_DH), q_gain), cos, sin)
    k = apply_rope(rms_norm(k.reshape(B, S, ATT_KV_HEADS, ATT_DH), k_gain), cos, sin)
    v = v.reshape(B, S, ATT_KV_HEADS, ATT_DH)
    pad = ((0, 0), (BLOCK, BLOCK), (0, 0), (0, 0))
    kp = jnp.pad(k, pad).reshape(B, N + 2, BLOCK, ATT_KV_HEADS, ATT_DH)
    vp = jnp.pad(v, pad).reshape(B, N + 2, BLOCK, ATT_KV_HEADS, ATT_DH)
    kb = jnp.concatenate([kp[:, :-2], kp[:, 1:-1], kp[:, 2:]], axis=2)
    vb = jnp.concatenate([vp[:, :-2], vp[:, 1:-1], vp[:, 2:]], axis=2)
    qb = q.reshape(B, N, BLOCK, ATT_KV_HEADS, ATT_GROUP, ATT_DH)
    s = jnp.einsum('bnikgd,bnjkd->bnkgij', qb.astype(jnp.float32), kb.astype(jnp.float32)) * (ATT_DH ** -0.5)
    qpos = jnp.arange(BLOCK)[:, None] + BLOCK
    kpos = jnp.arange(3 * BLOCK)[None, :]
    abs_k = jnp.arange(N)[:, None, None] * BLOCK - BLOCK + kpos[None]
    valid = (jnp.abs(qpos - kpos)[None] <= WINDOW) & (abs_k >= 0) & (abs_k < S)
    s = jnp.where(valid[None, :, None, None], s, NEG_INF)
    sk = sink.astype(jnp.float32).reshape(ATT_KV_HEADS, ATT_GROUP)[None, None, :, :, None, None]
    m = jnp.maximum(jnp.max(s, axis=-1, keepdims=True), sk)
    e = jnp.exp(s - m)
    prob = e / (jnp.sum(e, axis=-1, keepdims=True) + jnp.exp(sk - m))
    o = jnp.einsum('bnkgij,bnjkd->bnikgd', prob, vb.astype(jnp.float32))
    return o.reshape(B, S, ATT_QW).astype(q.dtype)

def peer_ffn(xn, wq, sub_keys, u_tab, v_tab):
    B, S, D = xn.shape
    xb = xn.reshape(-1, BLOCK, D)
    kf = sub_keys.astype(jnp.float32)

    def block(xt):
        T = xt.shape[0]
        q = (xt @ wq).astype(jnp.float32).reshape(T, PEER_HEADS, 2, PEER_QDIM // 2)
        s = jnp.einsum('thpc,hpkc->thpk', q, kf)
        s1, i1 = lax.top_k(s[:, :, 0], PEER_TOPK)
        s2, i2 = lax.top_k(s[:, :, 1], PEER_TOPK)
        cand_s = (s1[..., :, None] + s2[..., None, :]).reshape(T, PEER_HEADS, PEER_TOPK * PEER_TOPK)
        cand_e = (i1[..., :, None] * PEER_KEYS + i2[..., None, :]).reshape(T, PEER_HEADS, PEER_TOPK * PEER_TOPK)
        top_s, sel = lax.top_k(cand_s, PEER_TOPK)
        eid = jnp.take_along_axis(cand_e, sel, axis=-1)
        gate = jax.nn.softmax(top_s, axis=-1)
        act = jax.nn.gelu(jnp.einsum('thkd,td->thk', u_tab[eid], xt).astype(jnp.float32), approximate=False)
        w = (gate * act).astype(xt.dtype)
        return jnp.einsum('thk,thkd->td', w, v_tab[eid])

    return lax.map(block, xb).reshape(B, S, D)

def setup_inputs(seed: int = 0) -> dict:
    key = jax.random.key(seed)
    ks = jax.random.split(key, 26)
    nrm = lambda k, shp, sc: jax.random.normal(k, shp, jnp.float32) * sc
    gain = lambda k, shp: 1.0 + 0.05 * jax.random.normal(k, shp, jnp.float32)
    base_decay = jnp.log(2.0 ** (5.0 + jnp.arange(RET_HEADS, dtype=jnp.float32)) - 1.0)
    return {
        'x': nrm(ks[0], (BATCH, SEQ, D_MODEL), 1.0),
        'p': nrm(ks[1], (DEPTH, BATCH, SEQ, PLE_DIM), 1.0),
        'norm_mix': gain(ks[2], (DEPTH, D_MODEL)),
        'w_in': nrm(ks[3], (DEPTH, D_MODEL, D_IN), D_MODEL ** -0.5),
        'ret_decay': base_decay[None, None, :] + nrm(ks[4], (DEPTH, 2, RET_HEADS), 0.1),
        'ret_norm': gain(ks[5], (DEPTH, RET_VW)),
        'sgu_ln_g': gain(ks[6], (DEPTH, SGU_WIDTH)),
        'sgu_ln_b': nrm(ks[7], (DEPTH, SGU_WIDTH), 0.05),
        'sgu_w': nrm(ks[8], (DEPTH, SGU_GROUPS, BLOCK, BLOCK), BLOCK ** -0.5),
        'sgu_b': 1.0 + nrm(ks[9], (DEPTH, SGU_GROUPS, BLOCK), 0.1),
        'att_q_norm': gain(ks[10], (DEPTH, ATT_DH)),
        'att_k_norm': gain(ks[11], (DEPTH, ATT_DH)),
        'att_sink': nrm(ks[12], (DEPTH, ATT_HEADS), 0.5),
        'w_proj_ret': nrm(ks[13], (DEPTH, RET_VW, D_MODEL), RET_VW ** -0.5),
        'w_proj_sgu': nrm(ks[14], (DEPTH, SGU_WIDTH, D_MODEL), SGU_WIDTH ** -0.5),
        'w_proj_att': nrm(ks[15], (DEPTH, ATT_QW, D_MODEL), ATT_QW ** -0.5),
        'w_out': nrm(ks[16], (DEPTH, D_MODEL, D_MODEL), D_MODEL ** -0.5),
        'norm_ffn': gain(ks[17], (DEPTH, D_MODEL)),
        'peer_wq': nrm(ks[18], (DEPTH, D_MODEL, PEER_HEADS * PEER_QDIM), D_MODEL ** -0.5),
        'peer_keys': nrm(ks[19], (DEPTH, PEER_HEADS, 2, PEER_KEYS, PEER_QDIM // 2), (PEER_QDIM // 2) ** -0.5),
        'peer_u': nrm(ks[20], (DEPTH, PEER_EXPERTS, D_MODEL), D_MODEL ** -0.5),
        'peer_v': nrm(ks[21], (DEPTH, PEER_EXPERTS, D_MODEL), PEER_HEADS ** -0.5),
        'norm_ple': gain(ks[22], (DEPTH, D_MODEL)),
        'ple_gate': nrm(ks[23], (DEPTH, D_MODEL, D_MODEL), D_MODEL ** -0.5),
        'ple_proj': nrm(ks[24], (DEPTH, PLE_DIM, D_MODEL), PLE_DIM ** -0.5),
    }

def reference(x, p, norm_mix, w_in, ret_decay, ret_norm, sgu_ln_g, sgu_ln_b, sgu_w, sgu_b,
              att_q_norm, att_k_norm, att_sink, w_proj_ret, w_proj_sgu, w_proj_att, w_out,
              norm_ffn, peer_wq, peer_keys, peer_u, peer_v, norm_ple, ple_gate, ple_proj):
    S = x.shape[1]
    cos_r, sin_r = rope_tables(S, RET_DK)
    cos_a, sin_a = rope_tables(S, ATT_DH)
    h = x
    for i in range(DEPTH):
        xn = rms_norm(h, norm_mix[i])
        (q_r, k_r, v_r, g_r, u_s, v_s, q_a, k_a, v_a,
         gate_r, gate_s, gate_a) = split_columns(xn @ w_in[i])
        y_r = retention_branch(q_r, k_r, v_r, g_r, ret_decay[i], ret_norm[i], cos_r, sin_r)
        y_s = sgu_branch(u_s, v_s, sgu_ln_g[i], sgu_ln_b[i], sgu_w[i], sgu_b[i])
        y_a = window_attention(q_a, k_a, v_a, att_q_norm[i], att_k_norm[i], att_sink[i], cos_a, sin_a)
        merged = (jax.nn.sigmoid(gate_r) * (y_r @ w_proj_ret[i])
                  + jax.nn.sigmoid(gate_s) * (y_s @ w_proj_sgu[i])
                  + jax.nn.sigmoid(gate_a) * (y_a @ w_proj_att[i]))
        h = h + merged @ w_out[i]
        h = h + peer_ffn(rms_norm(h, norm_ffn[i]), peer_wq[i], peer_keys[i], peer_u[i], peer_v[i])
        h = h + jax.nn.sigmoid(rms_norm(h, norm_ple[i]) @ ple_gate[i]) * (p[i] @ ple_proj[i])
    return h


_drawn_inputs = setup_inputs


def setup_inputs(seed=0):
    import zlib

    import numpy as np

    out = dict(_drawn_inputs(seed))
    spreads = {}
    factors = {'att_q_norm': 6.827, 'att_k_norm': 6.717, 'att_sink': 8.0, 'norm_ple': 6.931}
    for name, (base, spread) in spreads.items():
        noise = np.random.default_rng([zlib.crc32(name.encode()), seed]).standard_normal(out[name].shape)
        drawn = base * np.exp(spread * noise) if base else spread * noise
        out[name] = __import__('jax').numpy.asarray(drawn.astype(out[name].dtype))
    for name, factor in factors.items():
        out[name] = (out[name] * factor).astype(out[name].dtype)
    return out
```

```python
from contextlib import ExitStack

import numpy as np
import concourse.bass as bass
from concourse import mybir
from concourse.alu_op_type import AluOpType as ALU

F32 = mybir.dt.float32
U32 = mybir.dt.uint32
ACT = mybir.ActivationFunctionType
AX = mybir.AxisListType

P = 128
S, D = 1024, 1024
T = S // P
DC = D // P
EPS = 1e-6
RH, RD = 4, 128
RW = RH * RD
G, GC = 4, 128
AH, AKV, AD = 8, 2, 64
AW, AKW = AH * AD, AKV * AD
WIN = 3 * P
NEG = -1e30
PH, PK, PC, TOPK = 8, 128, 128, 16
NSEL = PH * TOPK
CAND = TOPK * TOPK
PLE = 256
HB = 512
NR = 4 * (RD // 2)
NA = 2 * (AD // 2)

FIRST = 1
SLOTS = 8
CHUNKS = NSEL // SLOTS


class Semaphores:

    def __init__(self):
        self.taken = []

    def new(self, nc, name):
        self.taken.append((name, nc.alloc_semaphore(name)))
        return self.taken[-1][1]

    def prime(self, nc):
        for name, semaphore in self.taken:
            if not name.rstrip("0123456789").endswith(("_in", "_step")):
                nc.gpsimd.sem_inc(semaphore, FIRST)
        nc.all_engine_barrier()

    def clear(self, nc):
        nc.clear_and_free_semaphores([semaphore for _, semaphore in self.taken])
        nc.all_engine_barrier()
        self.taken = []


class Order:

    def __init__(self, eng, sem):
        self.eng, self.sem, self.n = eng, sem, 0

    def __call__(self, ins):
        ins.then_inc(self.sem, 1)
        self.n += 1
        self.eng.wait_ge(self.sem, self.n)

    def hold(self):
        self.eng.sem_inc(self.sem, 1)
        self.n += 1

    def turn(self):
        self.hold()
        self.eng.sem_clear(self.sem)
        self.n = 0


def ring(eng, ins, sem, value):
    ins.then_inc(sem, 1)
    eng.wait_ge(sem, value + FIRST)


def wide(ap, n):
    return ap.unsqueeze(2).to_broadcast([ap.shape[0], ap.shape[1], n])


def over(ap, n):
    return ap.unsqueeze(1).to_broadcast([ap.shape[0], n, ap.shape[1]])


def matmuls(pe, out, pairs):
    for n, (lhsT, rhs) in enumerate(pairs):
        last = pe.matmul(out, lhsT, rhs, start=(n == 0), stop=(n == len(pairs) - 1))
    return last


def rotate(order, eng, out, x, cos, sin, scratch, heads, half, finish):
    v = lambda ap: ap.rearrange("p (h a d) -> p h a d", h=heads, a=2)
    a, b = scratch
    hv = lambda ap, k: v(ap)[:, :, k, :]
    c, s = over(cos, heads), over(sin, heads)
    for k in range(2):
        order(eng.tensor_tensor(hv(a, k), hv(x, k), c, ALU.mult))
        order(eng.tensor_tensor(hv(b, k), hv(x, 1 - k), s, ALU.mult))
    order(eng.tensor_tensor(hv(out, 0), hv(a, 0), hv(b, 0), ALU.subtract))
    finish(eng.tensor_tensor(hv(out, 1), hv(a, 1), hv(b, 1), ALU.add))


def setup(nc, A, R):
    with ExitStack() as ctx:
        sem = lambda n: R["semaphores"].new(nc, n)
        sb = lambda n, s: ctx.enter_context(nc.sbuf_tensor(n, s, F32))
        params_in, lg_step, act_done, lg_ready = sem("params_in"), sem("lg_step"), sem("act_done"), sem("lg_ready")
        exponents_ready, exp_done, zeroed = sem("exponents_ready"), sem("exp_done"), sem("zeroed")
        K = 2 * RH
        x, e, u, lnu, z, one, lg = (sb(f"lg_{n}", [P, K]) for n in ("x", "e", "u", "ln", "z", "one", "log"))
        ex = sb("lg_exponents", [P, 5 * K])
        dm = sb("lg_distances", [P, RH, P])
        dm2 = sb("lg_distances2", [P, RH, P])
        diff = sb("lg_diff", [P, 2, P])
        col = sb("lg_col", [P, 4])
        R["semaphores"].prime(nc)
        block = ctx.enter_context(nc.Block())
        loads = [(R["ident"], A["ident"]), (R["col_mix"], A["norm_mix_col"]), (R["col_ret"], A["ret_norm_col"]),
                 (R["col_ple"], A["norm_ple_col"]), (R["sink"], A["att_sink"].partition_broadcast(P)), (x, A["ret_decay"].partition_broadcast(P)),
                 (diff, A["distance"]), (col, A["exponent_col"]), (R["iota16"], A["iota16"])]

        @block.sync
        def _(sp):
            for dst, src in loads:
                sp.dma_start(dst[:], src).then_inc(params_in, 16)
            sp.wait_ge(params_in, 16 * len(loads))

        @block.scalar
        def _(act):
            act.wait_ge(lg_ready, 1 + FIRST)
            act.activation(e[:], z[:], ACT.Exp).then_inc(act_done, 1)
            act.wait_ge(lg_ready, 2 + FIRST)
            act.activation(lnu[:], u[:], ACT.Ln).then_inc(act_done, 1)
            act.wait_ge(exponents_ready, 1 + FIRST)
            act.activation(R["decays"][:], ex[:], ACT.Exp).then_inc(exp_done, 1)
            act.activation(R["decay_mask"][:], dm[:], ACT.Exp).then_inc(exp_done, 1)

        @block.vector
        def _(dve):
            step = Order(dve, lg_step)
            step(dve.memset(R["eps"][:], EPS))
            dve.wait_ge(params_in, 16 * len(loads))
            step(dve.tensor_scalar(z[:], x[:], -1.0, None, ALU.mult))
            step(dve.tensor_tensor(z[:], z[:], x[:], ALU.min))
            ring(dve, dve.tensor_scalar(x[:], x[:], 0.0, None, ALU.min), lg_ready, 1)
            dve.wait_ge(act_done, 1 + FIRST)
            ring(dve, dve.tensor_scalar(u[:], e[:], 1.0, None, ALU.add), lg_ready, 2)
            step(dve.tensor_scalar(z[:], u[:], -1.0, None, ALU.add))
            step(dve.tensor_scalar(one[:], z[:], 0.0, None, ALU.is_equal))
            step(dve.tensor_tensor(z[:], z[:], one[:], ALU.add))
            dve.wait_ge(act_done, 2 + FIRST)
            step(dve.tensor_tensor(lnu[:], lnu[:], e[:], ALU.mult))
            step(dve.tensor_tensor(e[:], e[:], one[:], ALU.mult))
            step(dve.reciprocal(z[:], z[:]))
            step(dve.tensor_tensor(lnu[:], lnu[:], z[:], ALU.mult))
            step(dve.tensor_tensor(lnu[:], lnu[:], e[:], ALU.add))
            step(dve.tensor_tensor(lg[:], x[:], lnu[:], ALU.subtract))
            for j in range(4):
                step(dve.tensor_scalar(ex[:, j * K:(j + 1) * K], lg[:], col[:, j:j + 1], None, ALU.mult))
            step(dve.tensor_scalar(ex[:, 4 * K:5 * K], lg[:], float(P), None, ALU.mult))
            for h in range(RH):
                step(dve.tensor_scalar(dm[:, h, :], diff[:, 0, :], lg[:, h:h + 1], None, ALU.mult))
                step(dve.tensor_scalar(dm2[:, h, :], diff[:, 1, :], lg[:, RH + h:RH + h + 1], None, ALU.mult))
            ring(dve, dve.tensor_tensor(dm[:], dm[:], dm2[:], ALU.add), exponents_ready, 1)
            dve.wait_ge(exp_done, 2 + FIRST)
            step(dve.memset(R["ka_t"][:], 0.0))
            step(dve.memset(R["va"][:], 0.0))
            step(dve.memset(R["state_f"][:, 0, :], 0.0))


def keys_stage(nc, A, R, X):
    NW = 2 * RW + 2 * AKW
    with ExitStack() as ctx:
        sem = lambda n: R["semaphores"].new(nc, "k_" + n)
        sb = lambda n, s: ctx.enter_context(nc.sbuf_tensor("k_" + n, s, F32))
        pb = lambda n, s: ctx.enter_context(nc.psum_tensor("k_" + n, s, F32))
        w = sb("w", [P, DC, NW])
        x, xs, junk = sb("x", [P, 2, D]), sb("xs", [P, D]), sb("junk", [P, D])
        xnt = sb("xnt", [P, 2, DC, P])
        tab = sb("tab", [P, 2, NR + NA])
        gain = sb("gain", [P, AD])
        rms, rstd = sb("rms", [P, 2]), sb("rstd", [P, 1])
        k, ra, rb = sb("k", [P, RW]), sb("ra", [P, RW]), sb("rb", [P, RW])
        v, kt = sb("v", [P, 2, RW]), sb("kt", [P, 2, RW])
        kf, kb = sb("kf", [P, RW]), sb("kb", [P, RW])
        ka, ksq, kss = sb("ka", [P, AKW]), sb("ksq", [P, AKW]), sb("kss", [P, 4])
        p_xt = pb("p_xt", [P, D])
        p_k, p_v, p_a, p_kt, p_f, p_b = (pb(f"p_{n}", [P, HB]) for n in ("k", "v", "a", "kt", "f", "b"))
        w_in, gain_in = sem("w_in"), sem("gain_in")
        x_in, tab_in = [sem(f"x_in{b}") for b in range(2)], [sem(f"tab_in{b}") for b in range(2)]
        xnt_out, v_out, kt_out = ([sem(f"{n}_out{b}") for b in range(2)] for n in ("xnt", "v", "kt"))
        rms_ready, xs_ready, xt_done, xnt_ready = sem("rms_ready"), sem("xs_ready"), sem("xt_done"), sem("xnt_ready")
        k_done, v_done, a_done = sem("k_done"), sem("v_done"), sem("a_done")
        v_ready, va_ready, k_ready, kt_done, kt_ready = sem("v_ready"), sem("va_ready"), sem("k_ready"), sem("kt_done"), sem("kt_ready")
        kf_ready, kb_ready, f_done, b_done, b_saved, f_state = (sem(n) for n in ("kf_ready", "kb_ready", "f_done", "b_done", "b_saved", "f_state"))
        ksq_ready, kss_ready, krms_ready, ka_ready, kat_done, kat_ready = (
            sem(n) for n in ("ksq_ready", "kss_ready", "krms_ready", "ka_ready", "kat_done", "kat_ready"))
        dve_step, square_ready = sem("dve_step"), sem("square_ready")
        R["semaphores"].prime(nc)
        block = ctx.enter_context(nc.Block())

        @block.sync
        def _(sp):
            sp.dma_start(w[:], A["w_keys"]).then_inc(w_in, 16)
            sp.dma_start(gain[:], A["att_k_norm"].partition_broadcast(P)).then_inc(gain_in, 16)
            with sp.Fori(0, T // 2) as i:
                for b in range(2):
                    t = i * 2 + b
                    sp.wait_ge(xs_ready, i * 2 + FIRST)
                    sp.dma_start(x[:, b, :], A["x"][t]).then_inc(x_in[b], 16)
                    sp.wait_ge(ka_ready, i * 2 + FIRST)
                    sp.dma_start(tab[:, b, :], A["rotary"][t]).then_inc(tab_in[b], 16)
                for b in range(2):
                    t = i * 2 + b
                    sp.wait_ge(xnt_ready, t + 1 + FIRST)
                    sp.dma_start(X["xnt"][t], xnt[:, b, :, :]).then_inc(xnt_out[b], 16)
                    sp.wait_ge(v_ready, t + 1 + FIRST)
                    sp.dma_start(X["v"][t], v[:, b, :]).then_inc(v_out[b], 16)
                    sp.wait_ge(kt_ready, t + 1 + FIRST)
                    sp.dma_start(X["kt"][t], kt[:, b, :]).then_inc(kt_out[b], 16)
            for b in range(2):
                for s in (xnt_out, v_out, kt_out):
                    sp.wait_ge(s[b], 16 * (T // 2) + FIRST)

        @block.scalar
        def _(act):
            act.preload_act_table(ACT.Sqrt)
            with act.Fori(0, T // 2) as i:
                for b in range(2):
                    t = i * 2 + b
                    act.wait_ge(x_in[b], i * 16 + 16)
                    ring(act, act.activation(junk[:], x[:, b, :], ACT.Square, accum_out=rms[:, 0:1]), square_ready, t + 1)
                    act.wait_ge(xs_ready, t + FIRST)
                    ring(act, act.activation(rms[:, 1:2], rms[:, 0:1], ACT.Sqrt, scale=1.0 / D, bias=R["eps"][:]), rms_ready, t + 1)
                    act.wait_ge(v_done, t + 1 + FIRST)
                    act.wait_ge(v_out[b], i * 16 + FIRST)
                    act.wait_ge(b_done, t + FIRST)
                    ring(act, act.copy(v[:, b, :], p_v[:]), v_ready, t + 1)
                    act.wait_ge(a_done, t + 1 + FIRST)
                    act.wait_ge(kss_ready, t + FIRST)
                    ring(act, act.activation(ksq[:], p_a[:, 0:AKW], ACT.Square), ksq_ready, t + 1)
                    ring(act, act.copy(R["va"][:, t + 1, :], p_a[:, AKW:2 * AKW]), va_ready, t + 1)
                    act.wait_ge(kss_ready, t + 1 + FIRST)
                    ring(act, act.activation(kss[:, 2:4], kss[:, 0:2], ACT.Sqrt, scale=1.0 / AD, bias=R["eps"][:]), krms_ready, t + 1)
                    act.wait_ge(kt_done, t + 1 + FIRST)
                    act.wait_ge(kt_out[b], i * 16 + FIRST)
                    ring(act, act.copy(kt[:, b, :], p_kt[:]), kt_ready, t + 1)
                    act.wait_ge(b_done, t + 1 + FIRST)
                    ring(act, act.copy(R["state_b"][:, t, :], p_b[:]), b_saved, t + 1)
                    act.wait_ge(kat_done, t + 1 + FIRST)
                    ring(act, act.copy(R["ka_t"][:, t + 1, :], p_a[:, 2 * AKW:2 * AKW + P]), kat_ready, t + 1)

        @block.vector
        def _(dve):
            step = Order(dve, dve_step)
            dve.wait_ge(gain_in, 16)
            with dve.Fori(0, T // 2) as i:
                for b in range(2):
                    t = i * 2 + b
                    step.turn()
                    dve.wait_ge(rms_ready, t + 1 + FIRST)
                    step(dve.reciprocal(rstd[:], rms[:, 1:2]))
                    dve.wait_ge(xt_done, t + FIRST)
                    ring(dve, dve.tensor_scalar(xs[:], x[:, b, :], rstd[:, 0:1], None, ALU.mult), xs_ready, t + 1)
                    dve.wait_ge(xt_done, t + 1 + FIRST)
                    dve.wait_ge(xnt_out[b], i * 16 + FIRST)
                    ring(dve, dve.tensor_tensor(xnt[:, b, :, :], p_xt[:].rearrange("p (c n) -> p c n", c=DC),
                                                wide(R["col_mix"][:], P), ALU.mult), xnt_ready, t + 1)
                    dve.wait_ge(tab_in[b], i * 16 + 16)
                    dve.wait_ge(k_done, t + 1 + FIRST)
                    dve.wait_ge(b_done, t + FIRST)
                    q2 = NR // 2
                    rotate(step, dve, k[:], p_k[:], tab[:, b, q2:q2 + RD // 2], tab[:, b, q2 + RD // 2:NR], (ra[:], rb[:]), RH, RD // 2,
                           lambda ins: ring(dve, ins, k_ready, t + 1))
                    hv = lambda ap: ap.rearrange("p (h d) -> p h d", h=RH)
                    ring(dve, dve.tensor_tensor(hv(kf[:]), hv(k[:]), wide(R["decays"][:, 0:RH], RD), ALU.mult), kf_ready, t + 1)
                    ring(dve, dve.tensor_tensor(hv(kb[:]), hv(k[:]), wide(R["decays"][:, 8 + RH:8 + 2 * RH], RD), ALU.mult), kb_ready, t + 1)
                    kv = lambda ap: ap.rearrange("p (h d) -> p h d", h=AKV)
                    dve.wait_ge(ksq_ready, t + 1 + FIRST)
                    dve.wait_ge(krms_ready, t + FIRST)
                    ring(dve, dve.tensor_reduce(kss[:, 0:2], kv(ksq[:]), AX.X, ALU.add), kss_ready, t + 1)
                    dve.wait_ge(krms_ready, t + 1 + FIRST)
                    step(dve.reciprocal(kss[:, 2:4], kss[:, 2:4]))
                    step(dve.tensor_tensor(kv(ra[:, 0:AKW]), kv(p_a[:, 0:AKW]), wide(kss[:, 2:4], AD), ALU.mult))
                    step(dve.tensor_tensor(kv(ra[:, 0:AKW]), kv(ra[:, 0:AKW]), over(gain[:], AKV), ALU.mult))
                    dve.wait_ge(kat_done, t + FIRST)
                    rotate(step, dve, ka[:], ra[:, 0:AKW], tab[:, b, NR:NR + AD // 2], tab[:, b, NR + AD // 2:NR + NA],
                           (ra[:, AKW:2 * AKW], rb[:, 0:AKW]), AKV, AD // 2, lambda ins: ring(dve, ins, ka_ready, t + 1))
                    st = lambda n: hv(R["state_f"][:, n, :])
                    dve.wait_ge(f_done, t + 1 + FIRST)
                    step(dve.tensor_tensor(st(t + 1), st(t), wide(R["decays"][:, 32:32 + RH], RD), ALU.mult))
                    ring(dve, dve.tensor_tensor(st(t + 1), st(t + 1), hv(p_f[:]), ALU.add), f_state, t + 1)
            step.turn()
            dve.wait_ge(b_saved, T + FIRST)
            sb_ = lambda n: hv(R["state_b"][:, n, :])
            step(dve.memset(R["state_b"][:, T, :], 0.0))
            for t in range(T - 2, -1, -1):
                step(dve.tensor_tensor(hv(ra[:]), sb_(t + 2), wide(R["decays"][:, 32 + RH:32 + 2 * RH], RD), ALU.mult))
                step(dve.tensor_tensor(sb_(t + 1), sb_(t + 1), hv(ra[:]), ALU.add))

        @block.tensor
        def _(pe):
            pe.wait_ge(w_in, 16)
            with pe.Fori(0, T // 2) as i:
                for b in range(2):
                    t = i * 2 + b
                    pe.wait_ge(xs_ready, t + 1 + FIRST)
                    pe.wait_ge(xnt_ready, t + FIRST)
                    for c in range(DC):
                        last = pe.transpose(p_xt[:, c * P:(c + 1) * P], xs[:, c * P:(c + 1) * P], R["ident"][:])
                    last.then_inc(xt_done, 1)
                    pe.wait_ge(xnt_ready, t + 1 + FIRST)
                    cut = lambda a, n, out: matmuls(pe, out, [(xnt[:, b, c, :], w[:, c, a:a + n]) for c in range(DC)])
                    pe.wait_ge(k_ready, t + FIRST)
                    cut(0, RW, p_k[:]).then_inc(k_done, 1)
                    pe.wait_ge(v_ready, t + FIRST)
                    cut(RW, RW, p_v[:]).then_inc(v_done, 1)
                    pe.wait_ge(ka_ready, t + FIRST)
                    pe.wait_ge(va_ready, t + FIRST)
                    pe.wait_ge(kat_ready, t + FIRST)
                    cut(2 * RW, 2 * AKW, p_a[:, 0:2 * AKW]).then_inc(a_done, 1)
                    pe.wait_ge(k_ready, t + 1 + FIRST)
                    pe.wait_ge(kt_ready, t + FIRST)
                    for h in range(RH):
                        last = pe.transpose(p_kt[:, h * P:(h + 1) * P], k[:, h * P:(h + 1) * P], R["ident"][:])
                    last.then_inc(kt_done, 1)
                    pe.wait_ge(v_ready, t + 1 + FIRST)
                    pe.wait_ge(kf_ready, t + 1 + FIRST)
                    pe.wait_ge(f_state, t + FIRST)
                    for h in range(RH):
                        hs = slice(h * P, (h + 1) * P)
                        last = pe.matmul(p_f[:, hs], kf[:, hs], v[:, b, hs], start=True, stop=True)
                    last.then_inc(f_done, 1)
                    pe.wait_ge(kb_ready, t + 1 + FIRST)
                    pe.wait_ge(b_saved, t + FIRST)
                    for h in range(RH):
                        hs = slice(h * P, (h + 1) * P)
                        last = pe.matmul(p_b[:, hs], kb[:, hs], v[:, b, hs], start=True, stop=True)
                    last.then_inc(b_done, 1)
                    pe.wait_ge(ka_ready, t + 1 + FIRST)
                    pe.wait_ge(va_ready, t + 1 + FIRST)
                    pe.transpose(p_a[:, 2 * AKW:2 * AKW + P], ka[:], R["ident"][:]).then_inc(kat_done, 1)


def branches_stage(nc, A, R, X):
    NW = RW + RW + 2 * G * GC + AW
    Q_A, Q_R, V_S, U_S, G_R = (n * HB for n in range(5))
    with ExitStack() as ctx:
        sem = lambda n: R["semaphores"].new(nc, "b_" + n)
        sb = lambda n, s: ctx.enter_context(nc.sbuf_tensor("b_" + n, s, F32))
        pb = lambda n: ctx.enter_context(nc.psum_tensor("b_" + n, [P, HB], F32))
        w = sb("w", [P, DC, NW])
        w_mix, ln_g, ln_b = sb("w_mix", [P, G, P]), sb("ln_g", [P, G * GC]), sb("ln_b", [P, G * GC])
        b_mix, gain = sb("b_mix", [P, G]), sb("gain", [P, AD])
        xnt = sb("xnt", [P, 2, DC, P])
        kt, v, tab = sb("kt", [P, RW]), sb("v", [P, RW]), sb("tab", [P, NR + NA])
        mask = sb("mask", [P, WIN])
        qr, ta, tb, tc = (sb(n, [P, RW]) for n in ("qr", "ta", "tb", "tc"))
        qt, st, silu = (sb(n, [P, RW]) for n in ("qt", "st", "silu"))
        small = sb("small", [P, 24])
        vg, ug = sb("vg", [P, G * GC]), sb("ug", [P, G * GC])
        bn, mv = sb("bn", [P, 6]), sb("mv", [P, 4])
        qa, qsq = sb("qa", [P, AW]), sb("qsq", [P, AW])
        qat, win = sb("qat", [P, AW]), sb("win", [P, WIN])
        sc = sb("sc", [P, AH, WIN])
        att = sb("att", [P, 4 * AH])
        pt = sb("pt", [P, 2, WIN])
        yt = sb("yt", [P, 3 * RW])
        p0, p1, p2, p3, p4, p5, p6, p7 = (pb(f"p{n}") for n in range(8))
        par_in, tab_in, kt_in, v_in, mask_in, yt_out = (sem(n) for n in ("par_in", "tab_in", "kt_in", "v_in", "mask_in", "yt_out"))
        xnt_in = [sem(f"xnt_in{b}") for b in range(2)]
        names = ("qa_done qr_done vs_done us_done gr_done qt_done st_done inner_done cross_f_done cross_b_done mix_done qat_done "
                 "score_done pt_done pv_done yr_t_done ys_t_done ya_t_done "
                 "qr_ready st_ready y_summed yr_ready vn_ready ys_ready qss_ready qa_ready ss_ready var_ready masked max_ready den_ready ya_ready ys_t_ready "
                 "qsq_ready qrms_ready qt_ready silu_ready vg_ready ug_ready rms_ready std_ready qat_ready win_ready exp_ready sinks_ready pt_ready yr_t_ready ya_t_ready "
                 "dve_step act_done").split()
        Z = {n: sem(n) for n in names}
        R["semaphores"].prime(nc)
        block = ctx.enter_context(nc.Block())
        par = [(w, A["w_branches"]), (w_mix, A["sgu_w_t"]), (ln_g, A["sgu_ln_g"].partition_broadcast(P)), (ln_b, A["sgu_ln_b"].partition_broadcast(P)),
               (b_mix, A["sgu_b_col"]), (gain, A["att_q_norm"].partition_broadcast(P))]

        @block.sync
        def _(sp):
            for dst, src in par:
                sp.dma_start(dst[:], src).then_inc(par_in, 16)
            with sp.Fori(0, T // 2) as i:
                for b in range(2):
                    t = i * 2 + b
                    sp.wait_ge(Z["gr_done"], i * 2 + FIRST)
                    sp.dma_start(xnt[:, b, :, :], X["xnt"][t]).then_inc(xnt_in[b], 16)
                for b in range(2):
                    t = i * 2 + b
                    sp.wait_ge(Z["qr_ready"], t + FIRST)
                    sp.wait_ge(Z["qa_ready"], t + FIRST)
                    sp.dma_start(tab[:], A["rotary"][t]).then_inc(tab_in, 16)
                    sp.wait_ge(Z["st_done"], t + FIRST)
                    sp.dma_start(kt[:], X["kt"][t]).then_inc(kt_in, 16)
                    sp.wait_ge(Z["inner_done"], t + FIRST)
                    sp.dma_start(v[:], X["v"][t]).then_inc(v_in, 16)
                    sp.wait_ge(Z["masked"], t * AH + FIRST)
                    sp.dma_start(mask[:], A["window_mask"][t]).then_inc(mask_in, 16)
                    sp.wait_ge(Z["ya_t_ready"], t + 1 + FIRST)
                    sp.wait_ge(Z["yr_t_ready"], t + 1 + FIRST)
                    sp.wait_ge(Z["ys_t_ready"], t + 1 + FIRST)
                    sp.dma_start(X["yt"][t], yt[:]).then_inc(yt_out, 16)
            sp.wait_ge(yt_out, 16 * T + FIRST)

        @block.tensor
        def _(pe):
            pe.wait_ge(par_in, 16 * len(par))
            tr = lambda out, x: [pe.transpose(out[:, c * P:(c + 1) * P], x[:, c * P:(c + 1) * P], R["ident"][:]) for c in range(4)][-1]
            with pe.Fori(0, T // 2) as i:
                for b in range(2):
                    t = i * 2 + b
                    cut = lambda a, out: matmuls(pe, out[:], [(xnt[:, b, c, :], w[:, c, a:a + HB]) for c in range(DC)])
                    pe.wait_ge(xnt_in[b], i * 16 + 16)
                    pe.wait_ge(Z["ya_t_ready"], t + FIRST)
                    cut(Q_A, p0).then_inc(Z["qa_done"], 1)
                    pe.wait_ge(Z["ya_ready"], t + FIRST)
                    cut(Q_R, p1).then_inc(Z["qr_done"], 1)
                    pe.wait_ge(Z["ys_t_ready"], t + FIRST)
                    cut(V_S, p2).then_inc(Z["vs_done"], 1)
                    pe.wait_ge(Z["qr_ready"], t + 1 + FIRST)
                    tr(p5, qr).then_inc(Z["qt_done"], 1)
                    pe.wait_ge(Z["qa_ready"], t + 1 + FIRST)
                    tr(p0, qa).then_inc(Z["qat_done"], 1)
                    cut(U_S, p3).then_inc(Z["us_done"], 1)
                    pe.wait_ge(Z["qt_ready"], t + 1 + FIRST)
                    pe.wait_ge(kt_in, t * 16 + 16)
                    for h in range(RH):
                        hs = slice(h * P, (h + 1) * P)
                        last = pe.matmul(p6[:, hs], kt[:, hs], qt[:, hs], start=True, stop=True)
                    last.then_inc(Z["st_done"], 1)
                    pe.wait_ge(Z["yr_t_ready"], t + FIRST)
                    cut(G_R, p4).then_inc(Z["gr_done"], 1)
                    pe.wait_ge(Z["st_ready"], t + 1 + FIRST)
                    pe.wait_ge(v_in, t * 16 + 16)
                    for out, done, left, right in ((p5, "inner_done", st, lambda hs: v[:, hs]), (p7, "cross_f_done", qt, lambda hs: R["state_f"][:, t, hs]),
                                                   (p6, "cross_b_done", qt, lambda hs: R["state_b"][:, t + 1, hs])):
                        for h in range(RH):
                            hs = slice(h * P, (h + 1) * P)
                            last = pe.matmul(out[:, hs], left[:, hs], right(hs), start=True, stop=True)
                        last.then_inc(Z[done], 1)
                    pe.wait_ge(Z["vn_ready"], t + 1 + FIRST)
                    for g in range(G):
                        gs = slice(g * GC, (g + 1) * GC)
                        last = pe.matmul(p2[:, gs], w_mix[:, g, :], vg[:, gs], start=True, stop=True)
                    last.then_inc(Z["mix_done"], 1)
                    pe.wait_ge(Z["yr_ready"], t + 1 + FIRST)
                    tr(p4, ta).then_inc(Z["yr_t_done"], 1)
                    pe.wait_ge(Z["qat_ready"], t + 1 + FIRST)
                    pe.wait_ge(Z["win_ready"], t + 1 + FIRST)
                    pe.wait_ge(Z["y_summed"], t + 1 + FIRST)
                    for n in range(AH):
                        c, half = n // 2, slice(AD * (n % 2), AD * (n % 2) + AD)
                        if n >= 2:
                            pe.wait_ge(Z["masked"], t * AH + n - 1 + FIRST)
                        pe.matmul((p5, p6)[n % 2][:, 0:WIN], qat[half, c * P:(c + 1) * P], win[half, :], start=True, stop=True).then_inc(Z["score_done"], 1)
                    pe.wait_ge(Z["ys_ready"], t + 1 + FIRST)
                    tr(p2, ug).then_inc(Z["ys_t_done"], 1)
                    for n in range(AH):
                        k0 = AD * (n % 2)
                        pe.wait_ge(Z["exp_ready"], t * AH + n + 1 + FIRST)
                        if n >= 2:
                            pe.wait_ge(Z["pt_ready"], t * AH + n - 1 + FIRST)
                        for j in range(3):
                            last = pe.transpose((p7, p0)[n % 2][:, j * P:(j + 1) * P], sc[:, n, j * P:(j + 1) * P], R["ident"][:])
                        last.then_inc(Z["pt_done"], 1)
                        pe.wait_ge(Z["pt_ready"], t * AH + n + 1 + FIRST)
                        for j in range(3):
                            last = pe.matmul(p1[:, n * AD:(n + 1) * AD], pt[:, n % 2, j * P:(j + 1) * P], R["va"][:, t + j, k0:k0 + AD],
                                             start=(j == 0), stop=(j == 2))
                        last.then_inc(Z["pv_done"], 1)
                    pe.wait_ge(Z["ya_ready"], t + 1 + FIRST)
                    tr(p0, qsq).then_inc(Z["ya_t_done"], 1)

        @block.scalar
        def _(act):
            with act.Fori(0, T // 2) as i:
                for b in range(2):
                    t = i * 2 + b
                    to = lambda ins, name: ring(act, ins, Z[name], t + 1)
                    act.wait_ge(Z["qa_done"], t + 1 + FIRST)
                    act.wait_ge(Z["ya_t_done"], t + FIRST)
                    to(act.activation(qsq[:], p0[:], ACT.Square), "qsq_ready")
                    act.wait_ge(Z["qss_ready"], t + 1 + FIRST)
                    to(act.activation(small[:, 8:16], small[:, 0:8], ACT.Sqrt, scale=1.0 / AD, bias=R["eps"][:]), "qrms_ready")
                    act.wait_ge(Z["score_done"], t * AH + FIRST)
                    to(act.copy(win[:], R["ka_t"][:].rearrange("p t n -> p (t n)")[:, bass.ds(t * P, WIN)]), "win_ready")
                    act.wait_ge(Z["qt_done"], t + 1 + FIRST)
                    act.wait_ge(Z["cross_b_done"], t + FIRST)
                    to(act.copy(qt[:], p5[:]), "qt_ready")
                    act.wait_ge(Z["qat_done"], t + 1 + FIRST)
                    to(act.copy(qat[:], p0[:]), "qat_ready")
                    act.wait_ge(Z["vs_done"], t + 1 + FIRST)
                    act.wait_ge(Z["mix_done"], t + FIRST)
                    to(act.activation(vg[:], p2[:], ACT.Gelu), "vg_ready")
                    act.wait_ge(Z["us_done"], t + 1 + FIRST)
                    act.wait_ge(Z["ys_t_done"], t + FIRST)
                    to(act.activation(ug[:], p3[:], ACT.Gelu), "ug_ready")
                    act.wait_ge(Z["gr_done"], t + 1 + FIRST)
                    act.wait_ge(Z["yr_ready"], t + FIRST)
                    to(act.activation(silu[:], p4[:], ACT.Silu), "silu_ready")
                    act.wait_ge(Z["var_ready"], t + 1 + FIRST)
                    to(act.activation(mv[:, 2:3], mv[:, 1:2], ACT.Sqrt, scale=1.0, bias=R["eps"][:]), "std_ready")
                    act.wait_ge(Z["ss_ready"], t + 1 + FIRST)
                    to(act.activation(small[:, 20:24], small[:, 16:20], ACT.Sqrt, scale=1.0 / RD, bias=R["eps"][:]), "rms_ready")
                    act.wait_ge(Z["max_ready"], t + 1 + FIRST)
                    for n in range(AH):
                        ring(act, act.activation(sc[:, n, :], sc[:, n, :], ACT.Exp, bias=att[:, AH + n:AH + n + 1], scale=1.0,
                                                 accum_out=att[:, 2 * AH + n:2 * AH + n + 1]), Z["exp_ready"], t * AH + n + 1)
                    to(act.activation(att[:, 3 * AH:4 * AH], att[:, 3 * AH:4 * AH], ACT.Exp), "sinks_ready")
                    act.wait_ge(yt_out, t * 16 + FIRST)
                    act.wait_ge(Z["ya_t_done"], t + 1 + FIRST)
                    to(act.copy(yt[:, 2 * RW:3 * RW], p0[:]), "ya_t_ready")

        @block.vector
        def _(dve):
            step = Order(dve, Z["dve_step"])
            dve.wait_ge(par_in, 16 * len(par))
            hv = lambda ap: ap.rearrange("p (h d) -> p h d", h=RH)
            av = lambda ap: ap.rearrange("p (h d) -> p h d", h=AH)
            with dve.Fori(0, T // 2) as i:
                for b in range(2):
                    t = i * 2 + b
                    step.turn()
                    to = lambda ins, name: ring(dve, ins, Z[name], t + 1)
                    tt = dve.tensor_tensor
                    dve.wait_ge(Z["qsq_ready"], t + 1 + FIRST)
                    to(dve.tensor_reduce(small[:, 0:8], av(qsq[:]), AX.X, ALU.add), "qss_ready")
                    dve.wait_ge(Z["qrms_ready"], t + 1 + FIRST)
                    step(dve.reciprocal(small[:, 8:16], small[:, 8:16]))
                    dve.wait_ge(Z["yr_t_done"], t + FIRST)
                    step(tt(av(tc[:]), av(p0[:]), wide(small[:, 8:16], AD), ALU.mult))
                    step(tt(av(tc[:]), av(tc[:]), over(gain[:], AH), ALU.mult))
                    dve.wait_ge(tab_in, t * 16 + 16)
                    dve.wait_ge(Z["qat_done"], t + FIRST)
                    rotate(step, dve, qa[:], tc[:], tab[:, NR:NR + AD // 2], tab[:, NR + AD // 2:NR + NA], (ta[:], tb[:]), AH, AD // 2,
                           lambda ins: to(ins, "qa_ready"))
                    dve.wait_ge(Z["qr_done"], t + 1 + FIRST)
                    dve.wait_ge(Z["qt_done"], t + FIRST)
                    rotate(step, dve, qr[:], p1[:], tab[:, 0:RD // 2], tab[:, RD // 2:RD], (ta[:], tb[:]), RH, RD // 2,
                           lambda ins: to(ins, "qr_ready"))
                    dve.wait_ge(Z["vg_ready"], t + 1 + FIRST)
                    step(dve.bn_stats(bn[:], vg[:]))
                    to(dve.bn_aggr(mv[:, 0:2], bn[:]), "var_ready")
                    dve.wait_ge(Z["st_done"], t + 1 + FIRST)
                    dve.wait_ge(Z["inner_done"], t + FIRST)
                    to(tt(st[:], p6[:], R["decay_mask"][:].rearrange("p h n -> p (h n)"), ALU.mult), "st_ready")
                    dve.wait_ge(Z["std_ready"], t + 1 + FIRST)
                    step(dve.reciprocal(mv[:, 3:4], mv[:, 2:3]))
                    step(dve.tensor_scalar(vg[:], vg[:], mv[:, 0:1], mv[:, 3:4], ALU.subtract, ALU.mult))
                    step(tt(vg[:], vg[:], ln_g[:], ALU.mult))
                    to(tt(vg[:], vg[:], ln_b[:], ALU.add), "vn_ready")
                    dve.wait_ge(Z["cross_f_done"], t + 1 + FIRST)
                    step(tt(hv(ta[:]), hv(p7[:]), wide(R["decays"][:, 16:16 + RH], RD), ALU.mult))
                    step(tt(ta[:], ta[:], p5[:], ALU.add))
                    dve.wait_ge(Z["cross_b_done"], t + 1 + FIRST)
                    step(tt(hv(tb[:]), hv(p6[:]), wide(R["decays"][:, 24 + RH:24 + 2 * RH], RD), ALU.mult))
                    to(tt(ta[:], ta[:], tb[:], ALU.add), "y_summed")
                    step(tt(tb[:], ta[:], ta[:], ALU.mult))
                    to(dve.tensor_reduce(small[:, 16:20], hv(tb[:]), AX.X, ALU.add), "ss_ready")
                    dve.wait_ge(Z["rms_ready"], t + 1 + FIRST)
                    step(dve.reciprocal(small[:, 20:24], small[:, 20:24]))
                    dve.wait_ge(Z["silu_ready"], t + 1 + FIRST)
                    step(tt(hv(tb[:]), hv(silu[:]), wide(small[:, 20:24], RD), ALU.mult))
                    to(tt(ta[:], ta[:], tb[:], ALU.mult), "yr_ready")
                    dve.wait_ge(Z["mix_done"], t + 1 + FIRST)
                    step(tt(hv(tb[:]), hv(p2[:]), wide(b_mix[:], GC), ALU.add))
                    dve.wait_ge(Z["ug_ready"], t + 1 + FIRST)
                    to(tt(ug[:], ug[:], tb[:], ALU.mult), "ys_ready")
                    dve.wait_ge(Z["yr_t_done"], t + 1 + FIRST)
                    dve.wait_ge(yt_out, t * 16 + FIRST)
                    to(tt(hv(yt[:, 0:RW]), hv(p4[:]), wide(R["col_ret"][:], P), ALU.mult), "yr_t_ready")
                    dve.wait_ge(mask_in, t * 16 + 16)
                    dve.wait_ge(Z["pt_done"], t * AH + FIRST)
                    for n in range(AH):
                        dve.wait_ge(Z["score_done"], t * AH + n + 1 + FIRST)
                        ring(dve, dve.scalar_tensor_tensor(out=sc[:, n, :], in0=(p5, p6)[n % 2][:, 0:WIN], scalar=AD ** -0.5, in1=mask[:],
                                                           op0=ALU.mult, op1=ALU.add), Z["masked"], t * AH + n + 1)
                    step(dve.tensor_reduce(att[:, 0:AH], sc[:], AX.X, ALU.max))
                    step(tt(att[:, 0:AH], att[:, 0:AH], R["sink"][:], ALU.max))
                    step(tt(att[:, 3 * AH:4 * AH], R["sink"][:], att[:, 0:AH], ALU.subtract))
                    to(dve.tensor_scalar(att[:, AH:2 * AH], att[:, 0:AH], -1.0, None, ALU.mult), "max_ready")
                    dve.wait_ge(Z["ys_t_done"], t + 1 + FIRST)
                    to(dve.tensor_copy(yt[:, RW:2 * RW], p2[:]), "ys_t_ready")
                    for n in range(AH):
                        dve.wait_ge(Z["pt_done"], t * AH + n + 1 + FIRST)
                        dve.wait_ge(Z["pv_done"], t * AH + max(n - 1, 0) + FIRST)
                        ring(dve, dve.tensor_copy(pt[:, n % 2, :], (p7, p0)[n % 2][:, 0:WIN]), Z["pt_ready"], t * AH + n + 1)
                    dve.wait_ge(Z["sinks_ready"], t + 1 + FIRST)
                    step(tt(att[:, 2 * AH:3 * AH], att[:, 2 * AH:3 * AH], att[:, 3 * AH:4 * AH], ALU.add))
                    step(dve.reciprocal(att[:, 2 * AH:3 * AH], att[:, 2 * AH:3 * AH]))
                    dve.wait_ge(Z["pv_done"], t * AH + AH + FIRST)
                    to(tt(av(qsq[:]), av(p1[:]), wide(att[:, 2 * AH:3 * AH], AD), ALU.mult), "ya_ready")


def merge_stage(nc, A, R, X):
    with ExitStack() as ctx:
        sem = lambda n: R["semaphores"].new(nc, "m_" + n)
        sb = lambda n, s: ctx.enter_context(nc.sbuf_tensor("m_" + n, s, F32))
        pb = lambda n: ctx.enter_context(nc.psum_tensor("m_" + n, [P, HB], F32))
        wg, wp = sb("wg", [P, DC, 3 * D]), sb("wp", [P, 4, 3 * D])
        xnt, yt = sb("xnt", [P, 2, DC, P]), sb("yt", [P, 3 * RW])
        sg, part, merged, mt = sb("sg", [P, 2, HB]), sb("part", [P, HB]), sb("merged", [P, D]), sb("mt", [P, D])
        p_g, p_p, p_t = [pb(f"p_g{n}") for n in range(2)], [pb(f"p_p{n}") for n in range(2)], [pb(f"p_t{n}") for n in range(2)]
        w_in, yt_in, mt_out = sem("w_in"), sem("yt_in"), sem("mt_out")
        xnt_in = [sem(f"xnt_in{b}") for b in range(2)]
        gate_done, proj_done, sg_ready, merged_part, merged_ready, mt_done, mt_ready, dve_step = (
            sem(n) for n in ("gate_done", "proj_done", "sg_ready", "merged_part", "merged_ready", "mt_done", "mt_ready", "dve_step"))
        R["semaphores"].prime(nc)
        block = ctx.enter_context(nc.Block())
        U = 6

        @block.sync
        def _(sp):
            for dst, src in ((wg, A["w_gates"]), (wp, A["w_proj"])):
                sp.dma_start(dst[:], src).then_inc(w_in, 16)
            with sp.Fori(0, T // 2) as i:
                for b in range(2):
                    t = i * 2 + b
                    sp.wait_ge(proj_done, i * 2 * U + FIRST)
                    sp.dma_start(xnt[:, b, :, :], X["xnt"][t]).then_inc(xnt_in[b], 16)
                for b in range(2):
                    t = i * 2 + b
                    sp.wait_ge(proj_done, t * U + FIRST)
                    sp.dma_start(yt[:], X["yt"][t]).then_inc(yt_in, 16)
                    sp.wait_ge(mt_ready, t + 1 + FIRST)
                    sp.dma_start(X["mt"][t], mt[:]).then_inc(mt_out, 16)
            sp.wait_ge(mt_out, 16 * T + FIRST)

        @block.tensor
        def _(pe):
            pe.wait_ge(w_in, 32)
            with pe.Fori(0, T // 2) as i:
                for b in range(2):
                    t = i * 2 + b
                    pe.wait_ge(xnt_in[b], i * 16 + 16)
                    pe.wait_ge(yt_in, t * 16 + 16)
                    for n in range(U):
                        half, br = divmod(n, 3)
                        cols = slice(br * D + half * HB, br * D + (half + 1) * HB)
                        u = t * U + n
                        if n >= 2:
                            pe.wait_ge(merged_part, u - 1 + FIRST)
                        else:
                            pe.wait_ge(merged_part, t * U + FIRST)
                        matmuls(pe, p_g[n % 2][:], [(xnt[:, b, c, :], wg[:, c, cols]) for c in range(DC)]).then_inc(gate_done, 1)
                        matmuls(pe, p_p[n % 2][:], [(yt[:, br * RW + c * P:br * RW + (c + 1) * P], wp[:, c, cols]) for c in range(4)]).then_inc(proj_done, 1)
                    pe.wait_ge(mt_ready, t + FIRST)
                    for half in range(2):
                        pe.wait_ge(merged_part, t * U + 3 * half + 3 + FIRST)
                        for c in range(4):
                            cs = slice(half * HB + c * P, half * HB + (c + 1) * P)
                            last = pe.transpose(p_t[half][:, c * P:(c + 1) * P], merged[:, cs], R["ident"][:])
                        last.then_inc(mt_done, 1)

        @block.scalar
        def _(act):
            with act.Fori(0, T // 2) as i:
                for b in range(2):
                    t = i * 2 + b
                    for n in range(U):
                        u = t * U + n
                        act.wait_ge(gate_done, u + 1 + FIRST)
                        act.wait_ge(merged_part, t * U + max(n - 1, 0) + FIRST)
                        ring(act, act.activation(sg[:, n % 2, :], p_g[n % 2][:], ACT.Sigmoid), sg_ready, u + 1)
                    act.wait_ge(mt_out, t * 16 + FIRST)
                    for half in range(2):
                        act.wait_ge(mt_done, t * 2 + half + 1 + FIRST)
                        ins = act.copy(mt[:, half * HB:(half + 1) * HB], p_t[half][:])
                    ins.then_inc(mt_ready, 1)

        @block.vector
        def _(dve):
            step = Order(dve, dve_step)
            with dve.Fori(0, T // 2) as i:
                for b in range(2):
                    t = i * 2 + b
                    step.turn()
                    dve.wait_ge(mt_done, t * 2 + FIRST)
                    for n in range(U):
                        half, br = divmod(n, 3)
                        u = t * U + n
                        m = merged[:, half * HB:(half + 1) * HB]
                        dve.wait_ge(sg_ready, u + 1 + FIRST)
                        dve.wait_ge(proj_done, u + 1 + FIRST)
                        if br == 0:
                            ring(dve, dve.tensor_tensor(m, p_p[n % 2][:], sg[:, n % 2, :], ALU.mult), merged_part, u + 1)
                        else:
                            step(dve.tensor_tensor(part[:], p_p[n % 2][:], sg[:, n % 2, :], ALU.mult))
                            ring(dve, dve.tensor_tensor(m, m, part[:], ALU.add), merged_part, u + 1)


def route_stage(nc, A, R, X):
    with ExitStack() as ctx:
        sem = lambda n: R["semaphores"].new(nc, "r_" + n)
        sb = lambda n, s, d=F32: ctx.enter_context(nc.sbuf_tensor("r_" + n, s, d))
        wo, wq, keys = sb("wo", [P, DC, D]), sb("wq", [P, DC, 2 * PH * PC]), sb("keys", [P, 2 * PH, PK])
        gain = sb("gain", [P, D])
        mt, x, h, xn, xnt = sb("mt", [P, D]), sb("x", [P, D]), sb("h", [P, D]), sb("xn", [P, D]), sb("xnt", [P, D])
        qt, s = sb("qt", [P, 2 * PH, P]), sb("s", [P, 2 * PH, PK])
        rms = sb("rms", [P, 3])
        top, top_at, top_f = sb("top", [P, 2 * PH, TOPK]), sb("top_at", [P, 2 * PH, TOPK], U32), sb("top_f", [P, 2 * PH, TOPK])
        best, best_at = sb("best", [P, PH, TOPK]), sb("best_at", [P, PH, TOPK], U32)
        part_u, part_f = sb("part_u", [P, 2, NSEL], U32), sb("part_f", [P, 2, NSEL])
        row = sb("row", [P, 2, NSEL])
        soft, total = sb("soft", [P, PH, TOPK]), sb("total", [P, PH])
        cand, pick = qt[:].rearrange("p a b -> p (a b)"), s[:].rearrange("p a b -> p (a b)")
        ps = ctx.enter_context(nc.psum_tensor("r_ps", [P, 4 * HB], F32))
        pq = ctx.enter_context(nc.psum_tensor("r_pq", [P, 4 * HB], F32))
        par_in, mt_in, x_in, h_out, xn_out = (sem(n) for n in ("par_in", "mt_in", "x_in", "h_out", "xn_out"))
        names = "h_done xt_done q_done s_done h_ready xn_ready xt_ready cand_used gate_logits chosen square_ready rms_ready q_ready s_ready gate_exp dve_step".split()
        Z = {n: sem(n) for n in names}
        R["semaphores"].prime(nc)
        block = ctx.enter_context(nc.Block())
        par = [(wo, A["w_out"]), (wq, A["peer_wq"]), (keys, A["peer_keys_t"]), (gain, A["norm_ffn"].partition_broadcast(P))]

        @block.sync
        def _(sp):
            for dst, src in par:
                sp.dma_start(dst[:], src).then_inc(par_in, 16)
            with sp.Fori(0, T) as t:
                sp.wait_ge(Z["h_done"], t + FIRST)
                sp.dma_start(mt[:], X["mt"][t]).then_inc(mt_in, 16)
                sp.wait_ge(Z["h_ready"], t + FIRST)
                sp.dma_start(x[:], A["x"][t]).then_inc(x_in, 16)
                sp.wait_ge(Z["h_ready"], t + 1 + FIRST)
                sp.dma_start(X["h"][t], h[:]).then_inc(h_out, 16)
                sp.wait_ge(Z["xn_ready"], t + 1 + FIRST)
                sp.dma_start(X["xn"][t], xn[:]).then_inc(xn_out, 16)
            sp.wait_ge(h_out, 16 * T + FIRST)
            sp.wait_ge(xn_out, 16 * T + FIRST)

        @block.tensor
        def _(pe):
            pe.wait_ge(par_in, 16 * len(par))
            with pe.Fori(0, T) as t:
                pe.wait_ge(mt_in, t * 16 + 16)
                pe.wait_ge(Z["s_ready"], t + FIRST)
                for half in range(2):
                    last = matmuls(pe, ps[:, half * HB:(half + 1) * HB], [(mt[:, c * P:(c + 1) * P], wo[:, c, half * HB:(half + 1) * HB]) for c in range(DC)])
                last.then_inc(Z["h_done"], 1)
                pe.wait_ge(Z["xn_ready"], t + 1 + FIRST)
                for c in range(DC):
                    last = pe.transpose(ps[:, D + c * P:D + (c + 1) * P], xn[:, c * P:(c + 1) * P], R["ident"][:])
                last.then_inc(Z["xt_done"], 1)
                pe.wait_ge(Z["xt_ready"], t + 1 + FIRST)
                for g in range(4):
                    for n in range(4 * g, 4 * g + 4):
                        last = matmuls(pe, pq[:, n * P:(n + 1) * P], [(wq[:, c, n * PC:(n + 1) * PC], xnt[:, c * P:(c + 1) * P]) for c in range(DC)])
                    last.then_inc(Z["q_done"], 1)
                for g in range(4):
                    pe.wait_ge(Z["q_ready"], t * 4 + g + 1 + FIRST)
                    for n in range(4 * g, 4 * g + 4):
                        last = pe.matmul(ps[:, n * PK:(n + 1) * PK], qt[:, n, :], keys[:, n, :], start=True, stop=True)
                last.then_inc(Z["s_done"], 1)

        @block.scalar
        def _(act):
            with act.Fori(0, T) as t:
                act.wait_ge(Z["h_ready"], t + 1 + FIRST)
                act.wait_ge(Z["xt_done"], t + FIRST)
                ring(act, act.activation(xnt[:], h[:], ACT.Square, accum_out=rms[:, 0:1]), Z["square_ready"], t + 1)
                ring(act, act.activation(rms[:, 1:2], rms[:, 0:1], ACT.Sqrt, scale=1.0 / D, bias=R["eps"][:]), Z["rms_ready"], t + 1)
                act.wait_ge(Z["cand_used"], t + FIRST)
                for g in range(4):
                    act.wait_ge(Z["q_done"], t * 4 + g + 1 + FIRST)
                    ring(act, act.copy(qt[:, 4 * g:4 * g + 4, :].rearrange("p a b -> p (a b)"), pq[:, g * HB:(g + 1) * HB]), Z["q_ready"], t * 4 + g + 1)
                act.wait_ge(Z["s_done"], t + 1 + FIRST)
                ring(act, act.copy(s[:].rearrange("p a b -> p (a b)"), ps[:]), Z["s_ready"], t + 1)
                act.wait_ge(Z["gate_logits"], t + 1 + FIRST)
                ring(act, act.activation(soft[:], soft[:], ACT.Exp), Z["gate_exp"], t + 1)

        @block.vector
        def _(dve):
            step = Order(dve, Z["dve_step"])
            dve.wait_ge(par_in, 16 * len(par))
            tt = dve.tensor_tensor

            def top16(scores, values, at):
                for k in range(2):
                    out, where = values[:, 8 * k:8 * k + 8], at[:, 8 * k:8 * k + 8]
                    step(dve.max(out, scores))
                    step(dve.max_index(where, out, scores))
                    if k == 0:
                        step(dve.match_replace(out=scores, in_to_replace=out, in_values=scores, imm_value=-3e38))

            with dve.Fori(0, T) as t:
                step.turn()
                to = lambda ins, name: ring(dve, ins, Z[name], t + 1)
                dve.wait_ge(Z["h_done"], t + 1 + FIRST)
                dve.wait_ge(x_in, t * 16 + 16)
                dve.wait_ge(h_out, t * 16 + FIRST)
                to(tt(h[:], ps[:, 0:D], x[:], ALU.add), "h_ready")
                dve.wait_ge(Z["rms_ready"], t + 1 + FIRST)
                step(dve.reciprocal(rms[:, 2:3], rms[:, 1:2]))
                dve.wait_ge(xn_out, t * 16 + FIRST)
                dve.wait_ge(Z["xt_done"], t + FIRST)
                to(dve.scalar_tensor_tensor(out=xn[:], in0=h[:], scalar=rms[:, 2:3], in1=gain[:], op0=ALU.mult, op1=ALU.mult), "xn_ready")
                dve.wait_ge(Z["xt_done"], t + 1 + FIRST)
                dve.wait_ge(Z["q_done"], t * 4 + FIRST)
                to(dve.tensor_copy(xnt[:], ps[:, D:2 * D]), "xt_ready")
                dve.wait_ge(Z["s_ready"], t + 1 + FIRST)
                step.hold()
                for n in range(2 * PH):
                    top16(s[:, n, :], top[:, n, :], top_at[:, n, :])
                hp = top[:].rearrange("p (h two) k -> p h two k", two=2)
                grid = lambda ap: ap.rearrange("p (h a b) -> p h a b", h=PH, a=TOPK)
                four = [P, PH, TOPK, TOPK]
                first, second = hp[:, :, 0, :].unsqueeze(3).to_broadcast(four), hp[:, :, 1, :].unsqueeze(2).to_broadcast(four)
                step(tt(grid(cand), first, second, ALU.add))
                for n in range(PH):
                    top16(cand[:, n * CAND:(n + 1) * CAND], best[:, n, :], best_at[:, n, :])
                to(tt(soft[:], best[:], best[:, :, 0:1].to_broadcast([P, PH, TOPK]), ALU.subtract), "gate_logits")
                flat = lambda ap: ap.rearrange("p h k -> p (h k)")
                step(dve.tensor_scalar(part_u[:, 0, :], flat(best_at[:]), 4, None, ALU.logical_shift_right))
                step(dve.tensor_scalar(part_u[:, 1, :], flat(best_at[:]), 15, None, ALU.bitwise_and))
                step(dve.tensor_copy(part_f[:], part_u[:]))
                step(dve.tensor_copy(top_f[:], top_at[:]))
                hf = top_f[:].rearrange("p (h two) k -> p h two k", two=2)
                for k in range(2):
                    rank = part_f[:, k, :].rearrange("p (h k) -> p h k", h=PH).unsqueeze(3).to_broadcast(four)
                    ranks = R["iota16"][:].unsqueeze(1).unsqueeze(1).to_broadcast(four)
                    step(tt(grid(pick), rank, ranks, ALU.is_equal))
                    step(tt(grid(pick), grid(pick), hf[:, :, k, :].unsqueeze(2).to_broadcast(four), ALU.mult))
                    step(dve.tensor_reduce(row[:, k, :].rearrange("p (h k) -> p h k", h=PH), grid(pick), AX.X, ALU.add))
                step(dve.scalar_tensor_tensor(out=row[:, 0, :], in0=row[:, 0, :], scalar=float(PK), in1=row[:, 1, :], op0=ALU.mult, op1=ALU.add))
                step(dve.tensor_copy(R["expert"][:, bass.ds(t * NSEL, NSEL)], row[:, 0, :]))
                dve.wait_ge(Z["gate_exp"], t + 1 + FIRST)
                step(dve.tensor_reduce(total[:], soft[:], AX.X, ALU.add))
                step(dve.reciprocal(total[:], total[:]))
                to(tt(R["gate"][:, bass.ds(t * NSEL, NSEL)].rearrange("p (h k) -> p h k", h=PH), soft[:], wide(total[:], TOPK), ALU.mult), "cand_used")


def experts_stage(nc, A, R, X):
    C = T * CHUNKS
    with ExitStack() as ctx:
        sem = lambda n: R["semaphores"].new(nc, "e_" + n)
        sb = lambda n, s, d=F32: ctx.enter_context(nc.sbuf_tensor("e_" + n, s, d))
        pb = lambda n, s: ctx.enter_context(nc.psum_tensor("e_" + n, s, F32))
        rows = sb("rows", [P, SLOTS, 2 * D])
        at = sb("at", [P, 2, SLOTS], U32)
        wg, wp = sb("wg", [P, DC, D]), sb("wp", [P, 2, D])
        xn = sb("xn", [P, T, D])
        prod, acc = sb("prod", [P, 2, D]), sb("acc", [P, 2, D])
        dots, wts = sb("dots", [P, SLOTS]), sb("wts", [P, SLOTS])
        h, pt = sb("h", [P, D]), sb("pt", [P, 2, P])
        h2, xs, xst, sg = sb("h2", [P, D]), sb("xs", [P, D]), sb("xst", [P, D]), sb("sg", [P, D])
        rms = sb("rms", [P, 3])
        p_t, p_g, p_p = pb("p_t", [P, D]), pb("p_g", [P, D]), pb("p_p", [P, D])
        par_in, h_in, pt_in, out_done = (sem(n) for n in ("par_in", "h_in", "pt_in", "out_done"))
        row_in = [sem(f"row_in{q}") for q in range(SLOTS)]
        names = ("at_ready dot_done wts_ready acc_done acc_start slot_free h2_ready xs_ready out_ready act_done square_ready rms_ready "
                 "xst_ready sg_ready xt_done gate_done dve_step").split()
        Z = {n: sem(n) for n in names}
        HALF = SLOTS // 2
        R["semaphores"].prime(nc)
        block = ctx.enter_context(nc.Block())
        par = [(wg, A["ple_gate"]), (wp, A["ple_proj"]), (xn, X["xn"].rearrange("t p d -> p t d"))]

        @block.gpsimd
        def _(pool):
            def gather(b, c, free):
                ring(pool, pool.tensor_copy(at[:, b, :], R["expert"][:, bass.ds(c * SLOTS, SLOTS)]), Z["at_ready"], c + 1)
                for q in range(SLOTS):
                    if free:
                        pool.wait_ge(Z["acc_done"], c * SLOTS - SLOTS + q + 1 + FIRST)
                        pool.sem_inc(Z["slot_free"], 1)
                    pool.indirect_dma_start(out=rows[:, q, :], out_offset=None, in_=A["peer_uv"],
                                            in_offset=bass.IndirectOffsetOnAxis(ap=at[:, b, q:q + 1], axis=0)).then_inc(row_in[q], 16)

            gather(0, 0, False)
            gather(1, 1, True)
            with pool.Fori(1, C // 2) as i:
                for b in range(2):
                    gather(b, i * 2 + b, True)

        @block.sync
        def _(sp):
            for dst, src in par:
                sp.dma_start(dst[:], src).then_inc(par_in, 16)
            with sp.Fori(0, T) as t:
                sp.wait_ge(Z["acc_start"], t + FIRST)
                sp.dma_start(h[:], X["h"][t]).then_inc(h_in, 16)
                sp.wait_ge(Z["gate_done"], t + FIRST)
                sp.dma_start(pt[:], A["p_t"][t]).then_inc(pt_in, 16)
                sp.wait_ge(Z["out_ready"], t + 1 + FIRST)
                sp.dma_start(A["out"][t], sg[:]).then_inc(out_done, 16)
            sp.wait_ge(out_done, 16 * T + FIRST)

        @block.vector
        def _(dve):
            step = Order(dve, Z["dve_step"])
            dve.wait_ge(par_in, 16 * len(par))
            with dve.Fori(0, T) as t:
                step.turn()
                to = lambda ins, name: ring(dve, ins, Z[name], t + 1)
                dve.wait_ge(h_in, t * 16 + 16)
                to(dve.tensor_copy(acc[:, 0, :], h[:]), "acc_start")
                step(dve.memset(acc[:, 1, :], 0.0))
                with dve.Fori(0, CHUNKS) as j:
                    c = t * CHUNKS + j
                    for q in range(SLOTS):
                        dve.wait_ge(row_in[q], c * 16 + 16)
                        dve.wait_ge(Z["dot_done"], c * SLOTS + max(q - 1, 0) + FIRST)
                        dve.scalar_tensor_tensor(out=prod[:, q % 2, :], in0=rows[:, q, 0:D], scalar=1.0, in1=xn[:, t, :],
                                                 op0=ALU.mult, op1=ALU.mult, accum_out=dots[:, q:q + 1]).then_inc(Z["dot_done"], 1)
                    for k in range(2):
                        ks = slice(k * HALF, (k + 1) * HALF)
                        dve.wait_ge(Z["act_done"], c * 2 + k + 1 + FIRST)
                        ring(dve, dve.tensor_tensor(wts[:, ks], dots[:, ks], R["gate"][:, bass.ds(c * SLOTS + k * HALF, HALF)], ALU.mult),
                             Z["wts_ready"], c * 2 + k + 1)
                        for q in range(k * HALF, (k + 1) * HALF):
                            dve.wait_ge(Z["acc_done"], c * SLOTS + max(q - 1, 0) + FIRST)
                            dve.scalar_tensor_tensor(out=acc[:, q % 2, :], in0=rows[:, q, D:2 * D], scalar=wts[:, q:q + 1], in1=acc[:, q % 2, :],
                                                     op0=ALU.mult, op1=ALU.add).then_inc(Z["acc_done"], 1)
                dve.wait_ge(Z["acc_done"], (t + 1) * NSEL + FIRST)
                to(dve.tensor_tensor(h2[:], acc[:, 0, :], acc[:, 1, :], ALU.add), "h2_ready")
                dve.wait_ge(Z["rms_ready"], t + 1 + FIRST)
                step(dve.reciprocal(rms[:, 2:3], rms[:, 1:2]))
                to(dve.tensor_scalar(xs[:], h2[:], rms[:, 2:3], None, ALU.mult), "xs_ready")
                dve.wait_ge(Z["sg_ready"], t + 1 + FIRST)
                step(dve.tensor_tensor(sg[:], sg[:], p_p[:], ALU.mult))
                to(dve.tensor_tensor(sg[:], sg[:], h2[:], ALU.add), "out_ready")

        @block.scalar
        def _(act):
            with act.Fori(0, T) as t:
                with act.Fori(0, CHUNKS) as j:
                    c = t * CHUNKS + j
                    for k in range(2):
                        ks = slice(k * HALF, (k + 1) * HALF)
                        act.wait_ge(Z["dot_done"], c * SLOTS + (k + 1) * HALF + FIRST)
                        ring(act, act.activation(dots[:, ks], dots[:, ks], ACT.Gelu), Z["act_done"], c * 2 + k + 1)
                act.wait_ge(Z["h2_ready"], t + 1 + FIRST)
                act.wait_ge(out_done, t * 16 + FIRST)
                ring(act, act.activation(sg[:], h2[:], ACT.Square, accum_out=rms[:, 0:1]), Z["square_ready"], t + 1)
                ring(act, act.activation(rms[:, 1:2], rms[:, 0:1], ACT.Sqrt, scale=1.0 / D, bias=R["eps"][:]), Z["rms_ready"], t + 1)
                act.wait_ge(Z["xt_done"], t + 1 + FIRST)
                for n in range(DC):
                    ring(act, act.mul(xst[:, n * P:(n + 1) * P], p_t[:, n * P:(n + 1) * P], R["col_ple"][:, n:n + 1]), Z["xst_ready"], t * DC + n + 1)
                act.wait_ge(Z["gate_done"], t + 1 + FIRST)
                ring(act, act.activation(sg[:], p_g[:], ACT.Sigmoid), Z["sg_ready"], t + 1)

        @block.tensor
        def _(pe):
            pe.wait_ge(par_in, 16 * len(par))
            with pe.Fori(0, T) as t:
                pe.wait_ge(Z["xs_ready"], t + 1 + FIRST)
                for n in range(DC):
                    last = pe.transpose(p_t[:, n * P:(n + 1) * P], xs[:, n * P:(n + 1) * P], R["ident"][:])
                last.then_inc(Z["xt_done"], 1)
                pe.wait_ge(pt_in, t * 16 + 16)
                pe.wait_ge(Z["xst_ready"], (t + 1) * DC + FIRST)
                for half in range(2):
                    hs = slice(half * HB, (half + 1) * HB)
                    matmuls(pe, p_p[:, hs], [(pt[:, n, :], wp[:, n, hs]) for n in range(2)])
                    last = matmuls(pe, p_g[:, hs], [(xst[:, n * P:(n + 1) * P], wg[:, n, hs]) for n in range(DC)])
                last.then_inc(Z["gate_done"], 1)


SPILLS = {"xnt": [T, P, DC * P], "v": [T, P, RW], "kt": [T, P, RW], "yt": [T, P, 3 * RW], "mt": [T, P, D], "h": [T, P, D], "xn": [T, P, D]}


def build_program(nc, A, X=None):
    if X is None:
        X = {n: nc.dram_tensor(f"kept_{n}", s, F32).ap() for n, s in SPILLS.items()}
    with ExitStack() as ctx:
        R = {"semaphores": Semaphores()}
        for n, s, d in (("ident", [P, P], F32), ("eps", [P, 1], F32), ("col_mix", [P, DC], F32), ("col_ret", [P, RH], F32), ("col_ple", [P, DC], F32),
                        ("sink", [P, AH], F32), ("decays", [P, 40], F32), ("iota16", [P, TOPK], F32), ("expert", [P, T * NSEL], U32), ("gate", [P, T * NSEL], F32)):
            R[n] = ctx.enter_context(nc.sbuf_tensor("all_" + n, s, d))
        with ExitStack() as mixers:
            for n, s in (("decay_mask", [P, RH, P]), ("state_f", [P, T + 1, RW]), ("state_b", [P, T + 1, RW]), ("ka_t", [P, T + 2, P]), ("va", [P, T + 2, AKW])):
                R[n] = mixers.enter_context(nc.sbuf_tensor("mix_" + n, s, F32))
            setup(nc, A, R)
            R["semaphores"].clear(nc)
            keys_stage(nc, A, R, X)
            R["semaphores"].clear(nc)
            branches_stage(nc, A, R, X)
            R["semaphores"].clear(nc)
        merge_stage(nc, A, R, X)
        R["semaphores"].clear(nc)
        route_stage(nc, A, R, X)
        R["semaphores"].clear(nc)
        experts_stage(nc, A, R, X)


def constants():
    def rotary(dim):
        inv = (np.float32(1.0) / (np.float32(10000.0) ** (np.arange(0, dim, 2, dtype=np.float32) / np.float32(dim)))).astype(np.float32)
        ang = np.arange(S, dtype=np.float32)[:, None] * inv[None, :]
        return np.cos(ang).astype(np.float32), np.sin(ang).astype(np.float32)

    (cr, sr), (ca, sa) = rotary(RD), rotary(AD)
    scale = np.float32(RD ** -0.5)
    table = np.concatenate([cr, sr, cr * scale, sr * scale, ca, sa], axis=1).reshape(T, P, NR + NA)
    pos = np.arange(P)
    key = np.arange(WIN)
    near = np.abs(pos[:, None] + P - key[None, :]) <= P
    mask = np.empty((T, P, WIN), np.float32)
    for t in range(T):
        there = (t * P - P + key >= 0) & (t * P - P + key < S)
        mask[t] = np.where(near & there[None, :], 0.0, NEG)
    j, c = pos[:, None], pos[None, :]
    distance = np.stack([np.maximum(c - j, 0), np.maximum(j - c, 0)], axis=1).astype(np.float32)
    exponents = np.stack([P - 1 - pos, pos, pos + 1, P - pos], axis=1).astype(np.float32)
    return {"rotary": table, "window_mask": mask, "distance": distance, "exponent_col": exponents, "ident": np.eye(P, dtype=np.float32),
            "iota16": np.tile(np.arange(TOPK, dtype=np.float32), (P, 1))}


def layout(x, p, norm_mix, w_in, ret_decay, ret_norm, sgu_ln_g, sgu_ln_b, sgu_w, sgu_b, att_q_norm, att_k_norm, att_sink, w_proj_ret, w_proj_sgu,
           w_proj_att, w_out, norm_ffn, peer_wq, peer_keys, peer_u, peer_v, norm_ple, ple_gate, ple_proj):
    c = np.ascontiguousarray
    chunks = lambda w: c(np.asarray(w).reshape(-1, P, w.shape[-1]).transpose(1, 0, 2))
    col = lambda v: c(np.asarray(v).reshape(-1, P).T)
    w = np.asarray(w_in[0])
    offs = np.cumsum([0, RW, RW, RW, RW, G * GC, G * GC, AW, AKW, AKW, D, D, D])
    q_r, k_r, v_r, g_r, u_s, v_s, q_a, k_a, v_a, g0, g1, g2 = (w[:, offs[n]:offs[n + 1]] for n in range(12))
    heads = [n // 2 + (AH // AKV) * (n % 2) for n in range(AH)]
    by_head = [slice(n * AD, (n + 1) * AD) for n in heads]
    q_a = np.concatenate([q_a[:, s] for s in by_head], axis=1)
    wpa = np.concatenate([np.asarray(w_proj_att[0])[s] for s in by_head], axis=0)
    arrays = {
        "x": c(np.asarray(x[0]).reshape(T, P, D)),
        "p_t": c(np.asarray(p[0, 0]).reshape(T, P, 2, P).transpose(0, 3, 2, 1)),
        "w_keys": chunks(np.concatenate([k_r, v_r, k_a, v_a], axis=1)),
        "w_branches": chunks(np.concatenate([q_a, q_r, v_s, u_s, g_r], axis=1)),
        "w_gates": chunks(np.concatenate([g0, g1, g2], axis=1)),
        "w_proj": chunks(np.concatenate([w_proj_ret[0], w_proj_sgu[0], wpa], axis=1)),
        "w_out": chunks(w_out[0]), "peer_wq": chunks(peer_wq[0]), "ple_gate": chunks(ple_gate[0]), "ple_proj": chunks(ple_proj[0]),
        "peer_keys_t": c(np.asarray(peer_keys[0]).reshape(2 * PH, PK, PC).transpose(2, 0, 1)),
        "peer_uv": np.concatenate([peer_u[0], peer_v[0]], axis=1),
        "norm_mix_col": col(norm_mix[0]), "ret_norm_col": col(ret_norm[0]), "norm_ple_col": col(norm_ple[0]), "norm_ffn": np.asarray(norm_ffn[0]),
        "ret_decay": np.asarray(ret_decay[0]).reshape(2 * RH), "att_sink": np.asarray(att_sink[0])[heads],
        "att_q_norm": np.asarray(att_q_norm[0]), "att_k_norm": np.asarray(att_k_norm[0]),
        "sgu_ln_g": np.asarray(sgu_ln_g[0]), "sgu_ln_b": np.asarray(sgu_ln_b[0]),
        "sgu_w_t": c(np.asarray(sgu_w[0]).transpose(2, 0, 1)), "sgu_b_col": c(np.asarray(sgu_b[0]).T),
    }
    return {n: c(a) for n, a in (arrays | constants()).items()}


def kernel(**inputs):
    import concourse.bacc as bacc
    from concourse.bass_utils import run_bass_kernel_spmd

    arrays = layout(**inputs)
    nc = bacc.Bacc("TRN2", target_bir_lowering=False, num_devices=1)
    A = {n: nc.dram_tensor(f"in_{n}", a.shape, mybir.dt.from_np(a.dtype), kind="ExternalInput").ap() for n, a in arrays.items()}
    A["out"] = nc.dram_tensor("out", (T, P, D), F32, kind="ExternalOutput").ap()
    build_program(nc, A)
    r = run_bass_kernel_spmd(nc, [{f"in_{n}": a for n, a in arrays.items()}], core_ids=[0])
    return r.results[0]["out"].reshape(1, S, D)
```

```python
from contextlib import ExitStack

import numpy as np
import concourse.bass as bass
from concourse import mybir
from concourse.alu_op_type import AluOpType as ALU

F32 = mybir.dt.float32
BF16 = mybir.dt.bfloat16
U32 = mybir.dt.uint32
ACT = mybir.ActivationFunctionType
AX = mybir.AxisListType

P = 128
S, D = 1024, 1024
T = S // P
DC = D // P
EPS = 1e-6
RH, RD = 4, 128
RW = RH * RD
G, GC = 4, 128
AH, AKV, AD = 8, 2, 64
AW, AKW = AH * AD, AKV * AD
WIN = 3 * P
NEG = -1e30
PH, PK, PC, TOPK = 8, 128, 128, 16
NSEL = PH * TOPK
CAND = TOPK * TOPK
PLE = 256
HB = 512
NR = 4 * (RD // 2)
NA = 2 * (AD // 2)

FIRST = 1
SLOTS = 8


class Semaphores:

    def __init__(self):
        self.taken = []

    def new(self, nc, name):
        self.taken.append((name, nc.alloc_semaphore(name)))
        return self.taken[-1][1]

    def prime(self, nc):
        for name, semaphore in self.taken:
            if not name.rstrip("0123456789").endswith(("_in", "_step")):
                nc.gpsimd.sem_inc(semaphore, FIRST)
        nc.all_engine_barrier()

    def clear(self, nc):
        nc.clear_and_free_semaphores([semaphore for _, semaphore in self.taken])
        nc.all_engine_barrier()
        self.taken = []


class Order:

    def __init__(self, eng, sem):
        self.eng, self.sem, self.n = eng, sem, 0

    def __call__(self, ins):
        ins.then_inc(self.sem, 1)
        self.n += 1
        self.eng.wait_ge(self.sem, self.n)

    def hold(self):
        self.eng.sem_inc(self.sem, 1)
        self.n += 1

    def turn(self):
        self.hold()
        self.eng.sem_clear(self.sem)
        self.n = 0


def ring(eng, ins, sem, value):
    ins.then_inc(sem, 1)
    eng.wait_ge(sem, value + FIRST)


def wide(ap, n):
    return ap.unsqueeze(2).to_broadcast([ap.shape[0], ap.shape[1], n])


def over(ap, n):
    return ap.unsqueeze(1).to_broadcast([ap.shape[0], n, ap.shape[1]])


def matmuls(pe, out, pairs):
    for n, (lhsT, rhs) in enumerate(pairs):
        last = pe.matmul(out, lhsT, rhs, start=(n == 0), stop=(n == len(pairs) - 1))
    return last


def rotate(order, eng, out, x, cos, sin, scratch, heads, half, finish):
    v = lambda ap: ap.rearrange("p (h a d) -> p h a d", h=heads, a=2)
    a, b = scratch
    hv = lambda ap, k: v(ap)[:, :, k, :]
    c, s = over(cos, heads), over(sin, heads)
    for k in range(2):
        order(eng.tensor_tensor(hv(a, k), hv(x, k), c, ALU.mult))
        order(eng.tensor_tensor(hv(b, k), hv(x, 1 - k), s, ALU.mult))
    order(eng.tensor_tensor(hv(out, 0), hv(a, 0), hv(b, 0), ALU.subtract))
    finish(eng.tensor_tensor(hv(out, 1), hv(a, 1), hv(b, 1), ALU.add))


def setup(nc, A, R):
    with ExitStack() as ctx:
        sem = lambda n: R["semaphores"].new(nc, n)
        sb = lambda n, s: ctx.enter_context(nc.sbuf_tensor(n, s, F32))
        params_in, lg_step, act_done, lg_ready = sem("params_in"), sem("lg_step"), sem("act_done"), sem("lg_ready")
        exponents_ready, exp_done, zeroed = sem("exponents_ready"), sem("exp_done"), sem("zeroed")
        K = 2 * RH
        x, e, u, lnu, z, one, lg = (sb(f"lg_{n}", [P, K]) for n in ("x", "e", "u", "ln", "z", "one", "log"))
        ex = sb("lg_exponents", [P, 5 * K])
        dm = sb("lg_distances", [P, RH, P])
        dm2 = sb("lg_distances2", [P, RH, P])
        diff = sb("lg_diff", [P, 2, P])
        col = sb("lg_col", [P, 4])
        R["semaphores"].prime(nc)
        block = ctx.enter_context(nc.Block())
        loads = [(R["ident"], A["ident"]), (R["col_mix"], A["norm_mix_col"]), (R["col_ret"], A["ret_norm_col"]),
                 (R["col_ple"], A["norm_ple_col"]), (R["sink"], A["att_sink"].partition_broadcast(P)), (x, A["ret_decay"].partition_broadcast(P)),
                 (diff, A["distance"]), (col, A["exponent_col"]), (R["iota16"], A["iota16"])]

        @block.sync
        def _(sp):
            for dst, src in loads:
                sp.dma_start(dst[:], src).then_inc(params_in, 16)
            sp.wait_ge(params_in, 16 * len(loads))

        @block.scalar
        def _(act):
            act.wait_ge(lg_ready, 1 + FIRST)
            act.activation(e[:], z[:], ACT.Exp).then_inc(act_done, 1)
            act.wait_ge(lg_ready, 2 + FIRST)
            act.activation(lnu[:], u[:], ACT.Ln).then_inc(act_done, 1)
            act.wait_ge(exponents_ready, 1 + FIRST)
            act.activation(R["decays"][:], ex[:], ACT.Exp).then_inc(exp_done, 1)
            act.activation(R["decay_mask"][:], dm[:], ACT.Exp).then_inc(exp_done, 1)

        @block.vector
        def _(dve):
            step = Order(dve, lg_step)
            step(dve.memset(R["eps"][:], EPS))
            dve.wait_ge(params_in, 16 * len(loads))
            step(dve.tensor_scalar(z[:], x[:], -1.0, None, ALU.mult))
            step(dve.tensor_tensor(z[:], z[:], x[:], ALU.min))
            ring(dve, dve.tensor_scalar(x[:], x[:], 0.0, None, ALU.min), lg_ready, 1)
            dve.wait_ge(act_done, 1 + FIRST)
            ring(dve, dve.tensor_scalar(u[:], e[:], 1.0, None, ALU.add), lg_ready, 2)
            step(dve.tensor_scalar(z[:], u[:], -1.0, None, ALU.add))
            step(dve.tensor_scalar(one[:], z[:], 0.0, None, ALU.is_equal))
            step(dve.tensor_tensor(z[:], z[:], one[:], ALU.add))
            dve.wait_ge(act_done, 2 + FIRST)
            step(dve.tensor_tensor(lnu[:], lnu[:], e[:], ALU.mult))
            step(dve.tensor_tensor(e[:], e[:], one[:], ALU.mult))
            step(dve.reciprocal(z[:], z[:]))
            step(dve.tensor_tensor(lnu[:], lnu[:], z[:], ALU.mult))
            step(dve.tensor_tensor(lnu[:], lnu[:], e[:], ALU.add))
            step(dve.tensor_tensor(lg[:], x[:], lnu[:], ALU.subtract))
            for j in range(4):
                step(dve.tensor_scalar(ex[:, j * K:(j + 1) * K], lg[:], col[:, j:j + 1], None, ALU.mult))
            step(dve.tensor_scalar(ex[:, 4 * K:5 * K], lg[:], float(P), None, ALU.mult))
            for h in range(RH):
                step(dve.tensor_scalar(dm[:, h, :], diff[:, 0, :], lg[:, h:h + 1], None, ALU.mult))
                step(dve.tensor_scalar(dm2[:, h, :], diff[:, 1, :], lg[:, RH + h:RH + h + 1], None, ALU.mult))
            ring(dve, dve.tensor_tensor(dm[:], dm[:], dm2[:], ALU.add), exponents_ready, 1)
            dve.wait_ge(exp_done, 2 + FIRST)
            step(dve.memset(R["ka_t"][:], 0.0))
            step(dve.memset(R["va"][:], 0.0))
            step(dve.memset(R["state_f"][:, 0, :], 0.0))


def keys_stage(nc, A, R, X):
    NW = 2 * RW + 2 * AKW
    with ExitStack() as ctx:
        sem = lambda n: R["semaphores"].new(nc, "k_" + n)
        sb = lambda n, s: ctx.enter_context(nc.sbuf_tensor("k_" + n, s, F32))
        pb = lambda n, s: ctx.enter_context(nc.psum_tensor("k_" + n, s, F32))
        w = sb("w", [P, DC, NW])
        wp, pt, pp = sb("wp", [P, 2, D]), sb("pt", [P, 2, 2, P]), sb("pp", [P, D])
        x, xs, junk = sb("x", [P, 2, D]), sb("xs", [P, D]), sb("junk", [P, D])
        xnt = sb("xnt", [P, 2, DC, P])
        tab = sb("tab", [P, 2, NR + NA])
        gain = sb("gain", [P, AD])
        rms, rstd = sb("rms", [P, 2]), sb("rstd", [P, 1])
        k, ra, rb = sb("k", [P, RW]), sb("ra", [P, RW]), sb("rb", [P, RW])
        v, kt = sb("v", [P, 2, RW]), sb("kt", [P, 2, RW])
        kf, kb = sb("kf", [P, RW]), sb("kb", [P, RW])
        ka, ksq, kss = sb("ka", [P, AKW]), sb("ksq", [P, AKW]), sb("kss", [P, 4])
        p_xt = pb("p_xt", [P, D])
        p_k, p_v, p_a, p_kt, p_f, p_b = (pb(f"p_{n}", [P, HB]) for n in ("k", "v", "a", "kt", "f", "b"))
        w_in, wp_in, gain_in = sem("w_in"), sem("wp_in"), sem("gain_in")
        pt_in, pp_out, pp_done, pp_ready = [sem(f"pt_in{b}") for b in range(2)], sem("pp_out"), sem("pp_done"), sem("pp_ready")
        x_in, tab_in = [sem(f"x_in{b}") for b in range(2)], [sem(f"tab_in{b}") for b in range(2)]
        xnt_out, v_out, kt_out = ([sem(f"{n}_out{b}") for b in range(2)] for n in ("xnt", "v", "kt"))
        rms_ready, xs_ready, xt_done, xnt_ready = sem("rms_ready"), sem("xs_ready"), sem("xt_done"), sem("xnt_ready")
        k_done, v_done, a_done = sem("k_done"), sem("v_done"), sem("a_done")
        v_ready, va_ready, k_ready, kt_done, kt_ready = sem("v_ready"), sem("va_ready"), sem("k_ready"), sem("kt_done"), sem("kt_ready")
        kf_ready, kb_ready, f_done, b_done, b_saved, f_state = (sem(n) for n in ("kf_ready", "kb_ready", "f_done", "b_done", "b_saved", "f_state"))
        ksq_ready, kss_ready, krms_ready, ka_ready, kat_done, kat_ready = (
            sem(n) for n in ("ksq_ready", "kss_ready", "krms_ready", "ka_ready", "kat_done", "kat_ready"))
        dve_step, square_ready = sem("dve_step"), sem("square_ready")
        R["semaphores"].prime(nc)
        block = ctx.enter_context(nc.Block())

        @block.sync
        def _(sp):
            sp.dma_start(w[:], A["w_keys"]).then_inc(w_in, 16)
            sp.dma_start(wp[:], A["ple_proj"]).then_inc(wp_in, 16)
            sp.dma_start(gain[:], A["att_k_norm"].partition_broadcast(P)).then_inc(gain_in, 16)
            with sp.Fori(0, T // 2) as i:
                for b in range(2):
                    t = i * 2 + b
                    sp.wait_ge(xs_ready, i * 2 + FIRST)
                    sp.dma_start(x[:, b, :], A["x"][t]).then_inc(x_in[b], 16)
                    sp.wait_ge(ka_ready, i * 2 + FIRST)
                    sp.dma_start(tab[:, b, :], A["rotary"][t]).then_inc(tab_in[b], 16)
                    sp.wait_ge(pp_done, i * 2 + FIRST)
                    sp.dma_start(pt[:, b, :, :], A["p_t"][t]).then_inc(pt_in[b], 16)
                for b in range(2):
                    t = i * 2 + b
                    sp.wait_ge(xnt_ready, t + 1 + FIRST)
                    sp.dma_start(X["xnt"][t], xnt[:, b, :, :]).then_inc(xnt_out[b], 16)
                    sp.wait_ge(v_ready, t + 1 + FIRST)
                    sp.dma_start(X["v"][t], v[:, b, :]).then_inc(v_out[b], 16)
                    sp.wait_ge(pp_ready, t + 1 + FIRST)
                    sp.dma_start(X["pp"][t], pp[:]).then_inc(pp_out, 16)
                    sp.wait_ge(kt_ready, t + 1 + FIRST)
                    sp.dma_start(X["kt"][t], kt[:, b, :]).then_inc(kt_out[b], 16)
            sp.wait_ge(pp_out, 16 * T + FIRST)
            for b in range(2):
                for s in (xnt_out, v_out, kt_out):
                    sp.wait_ge(s[b], 16 * (T // 2) + FIRST)

        @block.scalar
        def _(act):
            act.preload_act_table(ACT.Sqrt)
            with act.Fori(0, T // 2) as i:
                for b in range(2):
                    t = i * 2 + b
                    act.wait_ge(x_in[b], i * 16 + 16)
                    ring(act, act.activation(junk[:], x[:, b, :], ACT.Square, accum_out=rms[:, 0:1]), square_ready, t + 1)
                    act.wait_ge(xs_ready, t + FIRST)
                    ring(act, act.activation(rms[:, 1:2], rms[:, 0:1], ACT.Sqrt, scale=1.0 / D, bias=R["eps"][:]), rms_ready, t + 1)
                    act.wait_ge(v_done, t + 1 + FIRST)
                    act.wait_ge(v_out[b], i * 16 + FIRST)
                    act.wait_ge(b_done, t + FIRST)
                    ring(act, act.copy(v[:, b, :], p_v[:]), v_ready, t + 1)
                    act.wait_ge(pp_done, t + 1 + FIRST)
                    act.wait_ge(pp_out, t * 16 + FIRST)
                    ring(act, act.copy(pp[:], p_xt[:]), pp_ready, t + 1)
                    act.wait_ge(a_done, t + 1 + FIRST)
                    act.wait_ge(kss_ready, t + FIRST)
                    ring(act, act.activation(ksq[:], p_a[:, 0:AKW], ACT.Square), ksq_ready, t + 1)
                    ring(act, act.copy(R["va"][:, t + 1, :], p_a[:, AKW:2 * AKW]), va_ready, t + 1)
                    act.wait_ge(kss_ready, t + 1 + FIRST)
                    ring(act, act.activation(kss[:, 2:4], kss[:, 0:2], ACT.Sqrt, scale=1.0 / AD, bias=R["eps"][:]), krms_ready, t + 1)
                    act.wait_ge(kt_done, t + 1 + FIRST)
                    act.wait_ge(kt_out[b], i * 16 + FIRST)
                    ring(act, act.copy(kt[:, b, :], p_kt[:]), kt_ready, t + 1)
                    act.wait_ge(b_done, t + 1 + FIRST)
                    ring(act, act.copy(R["state_b"][:, t, :], p_b[:]), b_saved, t + 1)
                    act.wait_ge(kat_done, t + 1 + FIRST)
                    ring(act, act.copy(R["ka_t"][:, t + 1, :], p_a[:, 2 * AKW:2 * AKW + P]), kat_ready, t + 1)

        @block.vector
        def _(dve):
            step = Order(dve, dve_step)
            dve.wait_ge(gain_in, 16)
            with dve.Fori(0, T // 2) as i:
                for b in range(2):
                    t = i * 2 + b
                    step.turn()
                    dve.wait_ge(rms_ready, t + 1 + FIRST)
                    step(dve.reciprocal(rstd[:], rms[:, 1:2]))
                    dve.wait_ge(xt_done, t + FIRST)
                    ring(dve, dve.tensor_scalar(xs[:], x[:, b, :], rstd[:, 0:1], None, ALU.mult), xs_ready, t + 1)
                    dve.wait_ge(xt_done, t + 1 + FIRST)
                    dve.wait_ge(xnt_out[b], i * 16 + FIRST)
                    ring(dve, dve.tensor_tensor(xnt[:, b, :, :], p_xt[:].rearrange("p (c n) -> p c n", c=DC),
                                                wide(R["col_mix"][:], P), ALU.mult), xnt_ready, t + 1)
                    dve.wait_ge(tab_in[b], i * 16 + 16)
                    dve.wait_ge(k_done, t + 1 + FIRST)
                    dve.wait_ge(b_done, t + FIRST)
                    q2 = NR // 2
                    rotate(step, dve, k[:], p_k[:], tab[:, b, q2:q2 + RD // 2], tab[:, b, q2 + RD // 2:NR], (ra[:], rb[:]), RH, RD // 2,
                           lambda ins: ring(dve, ins, k_ready, t + 1))
                    hv = lambda ap: ap.rearrange("p (h d) -> p h d", h=RH)
                    ring(dve, dve.tensor_tensor(hv(kf[:]), hv(k[:]), wide(R["decays"][:, 0:RH], RD), ALU.mult), kf_ready, t + 1)
                    ring(dve, dve.tensor_tensor(hv(kb[:]), hv(k[:]), wide(R["decays"][:, 8 + RH:8 + 2 * RH], RD), ALU.mult), kb_ready, t + 1)
                    kv = lambda ap: ap.rearrange("p (h d) -> p h d", h=AKV)
                    dve.wait_ge(ksq_ready, t + 1 + FIRST)
                    dve.wait_ge(krms_ready, t + FIRST)
                    ring(dve, dve.tensor_reduce(kss[:, 0:2], kv(ksq[:]), AX.X, ALU.add), kss_ready, t + 1)
                    dve.wait_ge(krms_ready, t + 1 + FIRST)
                    step(dve.reciprocal(kss[:, 2:4], kss[:, 2:4]))
                    step(dve.tensor_tensor(kv(ra[:, 0:AKW]), kv(p_a[:, 0:AKW]), wide(kss[:, 2:4], AD), ALU.mult))
                    step(dve.tensor_tensor(kv(ra[:, 0:AKW]), kv(ra[:, 0:AKW]), over(gain[:], AKV), ALU.mult))
                    dve.wait_ge(kat_done, t + FIRST)
                    rotate(step, dve, ka[:], ra[:, 0:AKW], tab[:, b, NR:NR + AD // 2], tab[:, b, NR + AD // 2:NR + NA],
                           (ra[:, AKW:2 * AKW], rb[:, 0:AKW]), AKV, AD // 2, lambda ins: ring(dve, ins, ka_ready, t + 1))
                    st = lambda n: hv(R["state_f"][:, n, :])
                    dve.wait_ge(f_done, t + 1 + FIRST)
                    step(dve.tensor_tensor(st(t + 1), st(t), wide(R["decays"][:, 32:32 + RH], RD), ALU.mult))
                    ring(dve, dve.tensor_tensor(st(t + 1), st(t + 1), hv(p_f[:]), ALU.add), f_state, t + 1)
            step.turn()
            dve.wait_ge(b_saved, T + FIRST)
            sb_ = lambda n: hv(R["state_b"][:, n, :])
            step(dve.memset(R["state_b"][:, T, :], 0.0))
            for t in range(T - 2, -1, -1):
                step(dve.tensor_tensor(hv(ra[:]), sb_(t + 2), wide(R["decays"][:, 32 + RH:32 + 2 * RH], RD), ALU.mult))
                step(dve.tensor_tensor(sb_(t + 1), sb_(t + 1), hv(ra[:]), ALU.add))

        @block.tensor
        def _(pe):
            pe.wait_ge(w_in, 16)
            with pe.Fori(0, T // 2) as i:
                for b in range(2):
                    t = i * 2 + b
                    pe.wait_ge(xs_ready, t + 1 + FIRST)
                    pe.wait_ge(pp_ready, t + FIRST)
                    for c in range(DC):
                        last = pe.transpose(p_xt[:, c * P:(c + 1) * P], xs[:, c * P:(c + 1) * P], R["ident"][:])
                    last.then_inc(xt_done, 1)
                    pe.wait_ge(xnt_ready, t + 1 + FIRST)
                    cut = lambda a, n, out: matmuls(pe, out, [(xnt[:, b, c, :], w[:, c, a:a + n]) for c in range(DC)])
                    pe.wait_ge(k_ready, t + FIRST)
                    cut(0, RW, p_k[:]).then_inc(k_done, 1)
                    pe.wait_ge(v_ready, t + FIRST)
                    cut(RW, RW, p_v[:]).then_inc(v_done, 1)
                    pe.wait_ge(pt_in[b], i * 16 + 16)
                    pe.wait_ge(wp_in, 16)
                    for half in range(2):
                        hs = slice(half * HB, (half + 1) * HB)
                        last = matmuls(pe, p_xt[:, hs], [(pt[:, b, n, :], wp[:, n, hs]) for n in range(2)])
                    last.then_inc(pp_done, 1)
                    pe.wait_ge(ka_ready, t + FIRST)
                    pe.wait_ge(va_ready, t + FIRST)
                    pe.wait_ge(kat_ready, t + FIRST)
                    cut(2 * RW, 2 * AKW, p_a[:, 0:2 * AKW]).then_inc(a_done, 1)
                    pe.wait_ge(k_ready, t + 1 + FIRST)
                    pe.wait_ge(kt_ready, t + FIRST)
                    for h in range(RH):
                        last = pe.transpose(p_kt[:, h * P:(h + 1) * P], k[:, h * P:(h + 1) * P], R["ident"][:])
                    last.then_inc(kt_done, 1)
                    pe.wait_ge(v_ready, t + 1 + FIRST)
                    pe.wait_ge(kf_ready, t + 1 + FIRST)
                    pe.wait_ge(f_state, t + FIRST)
                    for h in range(RH):
                        hs = slice(h * P, (h + 1) * P)
                        last = pe.matmul(p_f[:, hs], kf[:, hs], v[:, b, hs], start=True, stop=True)
                    last.then_inc(f_done, 1)
                    pe.wait_ge(kb_ready, t + 1 + FIRST)
                    pe.wait_ge(b_saved, t + FIRST)
                    for h in range(RH):
                        hs = slice(h * P, (h + 1) * P)
                        last = pe.matmul(p_b[:, hs], kb[:, hs], v[:, b, hs], start=True, stop=True)
                    last.then_inc(b_done, 1)
                    pe.wait_ge(ka_ready, t + 1 + FIRST)
                    pe.wait_ge(va_ready, t + 1 + FIRST)
                    pe.transpose(p_a[:, 2 * AKW:2 * AKW + P], ka[:], R["ident"][:]).then_inc(kat_done, 1)


def branches_stage(nc, A, R, X):
    NW = RW + RW + 2 * G * GC + AW
    Q_A, Q_R, V_S, U_S, G_R = (n * HB for n in range(5))
    with ExitStack() as ctx:
        sem = lambda n: R["semaphores"].new(nc, "b_" + n)
        sb = lambda n, s: ctx.enter_context(nc.sbuf_tensor("b_" + n, s, F32))
        pb = lambda n: ctx.enter_context(nc.psum_tensor("b_" + n, [P, HB], F32))
        w = sb("w", [P, DC, NW])
        w_mix, ln_g, ln_b = sb("w_mix", [P, G, P]), sb("ln_g", [P, G * GC]), sb("ln_b", [P, G * GC])
        b_mix, gain = sb("b_mix", [P, G]), sb("gain", [P, AD])
        xnt = sb("xnt", [P, 2, DC, P])
        kt, v, tab = sb("kt", [P, RW]), sb("v", [P, RW]), sb("tab", [P, NR + NA])
        mask = sb("mask", [P, WIN])
        qr, ta, tb, tc = (sb(n, [P, RW]) for n in ("qr", "ta", "tb", "tc"))
        qt, st, silu = (sb(n, [P, RW]) for n in ("qt", "st", "silu"))
        small = sb("small", [P, 24])
        vg, ug = sb("vg", [P, G * GC]), sb("ug", [P, G * GC])
        bn, mv = sb("bn", [P, 6]), sb("mv", [P, 4])
        qa, qsq = sb("qa", [P, AW]), sb("qsq", [P, AW])
        qat, win = sb("qat", [P, AW]), sb("win", [P, WIN])
        sc = sb("sc", [P, AH, WIN])
        att = sb("att", [P, 4 * AH])
        pt = sb("pt", [P, 2, WIN])
        yt = sb("yt", [P, 3 * RW])
        p0, p1, p2, p3, p4, p5, p6, p7 = (pb(f"p{n}") for n in range(8))
        par_in, tab_in, kt_in, v_in, mask_in, yt_out = (sem(n) for n in ("par_in", "tab_in", "kt_in", "v_in", "mask_in", "yt_out"))
        xnt_in = [sem(f"xnt_in{b}") for b in range(2)]
        names = ("qa_done qr_done vs_done us_done gr_done qt_done st_done inner_done cross_f_done cross_b_done mix_done qat_done "
                 "score_done pt_done pv_done yr_t_done ys_t_done ya_t_done "
                 "qr_ready st_ready y_summed yr_ready vn_ready ys_ready qss_ready qa_ready ss_ready var_ready masked max_ready den_ready ya_ready ys_t_ready "
                 "qsq_ready qrms_ready qt_ready silu_ready vg_ready ug_ready rms_ready std_ready qat_ready win_ready exp_ready sinks_ready pt_ready yr_t_ready ya_t_ready "
                 "dve_step act_done").split()
        Z = {n: sem(n) for n in names}
        R["semaphores"].prime(nc)
        block = ctx.enter_context(nc.Block())
        par = [(w, A["w_branches"]), (w_mix, A["sgu_w_t"]), (ln_g, A["sgu_ln_g"].partition_broadcast(P)), (ln_b, A["sgu_ln_b"].partition_broadcast(P)),
               (b_mix, A["sgu_b_col"]), (gain, A["att_q_norm"].partition_broadcast(P))]

        @block.sync
        def _(sp):
            for dst, src in par:
                sp.dma_start(dst[:], src).then_inc(par_in, 16)
            with sp.Fori(0, T // 2) as i:
                for b in range(2):
                    t = i * 2 + b
                    sp.wait_ge(Z["gr_done"], i * 2 + FIRST)
                    sp.dma_start(xnt[:, b, :, :], X["xnt"][t]).then_inc(xnt_in[b], 16)
                for b in range(2):
                    t = i * 2 + b
                    sp.wait_ge(Z["qr_ready"], t + FIRST)
                    sp.wait_ge(Z["qa_ready"], t + FIRST)
                    sp.dma_start(tab[:], A["rotary"][t]).then_inc(tab_in, 16)
                    sp.wait_ge(Z["st_done"], t + FIRST)
                    sp.dma_start(kt[:], X["kt"][t]).then_inc(kt_in, 16)
                    sp.wait_ge(Z["inner_done"], t + FIRST)
                    sp.dma_start(v[:], X["v"][t]).then_inc(v_in, 16)
                    sp.wait_ge(Z["masked"], t * AH + FIRST)
                    sp.dma_start(mask[:], A["window_mask"][t]).then_inc(mask_in, 16)
                    sp.wait_ge(Z["ya_t_ready"], t + 1 + FIRST)
                    sp.wait_ge(Z["yr_t_ready"], t + 1 + FIRST)
                    sp.wait_ge(Z["ys_t_ready"], t + 1 + FIRST)
                    sp.dma_start(X["yt"][t], yt[:]).then_inc(yt_out, 16)
            sp.wait_ge(yt_out, 16 * T + FIRST)

        @block.tensor
        def _(pe):
            pe.wait_ge(par_in, 16 * len(par))
            tr = lambda out, x: [pe.transpose(out[:, c * P:(c + 1) * P], x[:, c * P:(c + 1) * P], R["ident"][:]) for c in range(4)][-1]
            with pe.Fori(0, T // 2) as i:
                for b in range(2):
                    t = i * 2 + b
                    cut = lambda a, out: matmuls(pe, out[:], [(xnt[:, b, c, :], w[:, c, a:a + HB]) for c in range(DC)])
                    pe.wait_ge(xnt_in[b], i * 16 + 16)
                    pe.wait_ge(Z["ya_t_ready"], t + FIRST)
                    cut(Q_A, p0).then_inc(Z["qa_done"], 1)
                    pe.wait_ge(Z["ya_ready"], t + FIRST)
                    cut(Q_R, p1).then_inc(Z["qr_done"], 1)
                    pe.wait_ge(Z["ys_t_ready"], t + FIRST)
                    cut(V_S, p2).then_inc(Z["vs_done"], 1)
                    pe.wait_ge(Z["qr_ready"], t + 1 + FIRST)
                    tr(p5, qr).then_inc(Z["qt_done"], 1)
                    pe.wait_ge(Z["qa_ready"], t + 1 + FIRST)
                    tr(p0, qa).then_inc(Z["qat_done"], 1)
                    cut(U_S, p3).then_inc(Z["us_done"], 1)
                    pe.wait_ge(Z["qt_ready"], t + 1 + FIRST)
                    pe.wait_ge(kt_in, t * 16 + 16)
                    for h in range(RH):
                        hs = slice(h * P, (h + 1) * P)
                        last = pe.matmul(p6[:, hs], kt[:, hs], qt[:, hs], start=True, stop=True)
                    last.then_inc(Z["st_done"], 1)
                    pe.wait_ge(Z["yr_t_ready"], t + FIRST)
                    cut(G_R, p4).then_inc(Z["gr_done"], 1)
                    pe.wait_ge(Z["st_ready"], t + 1 + FIRST)
                    pe.wait_ge(v_in, t * 16 + 16)
                    for out, done, left, right in ((p5, "inner_done", st, lambda hs: v[:, hs]), (p7, "cross_f_done", qt, lambda hs: R["state_f"][:, t, hs]),
                                                   (p6, "cross_b_done", qt, lambda hs: R["state_b"][:, t + 1, hs])):
                        for h in range(RH):
                            hs = slice(h * P, (h + 1) * P)
                            last = pe.matmul(out[:, hs], left[:, hs], right(hs), start=True, stop=True)
                        last.then_inc(Z[done], 1)
                    pe.wait_ge(Z["vn_ready"], t + 1 + FIRST)
                    for g in range(G):
                        gs = slice(g * GC, (g + 1) * GC)
                        last = pe.matmul(p2[:, gs], w_mix[:, g, :], vg[:, gs], start=True, stop=True)
                    last.then_inc(Z["mix_done"], 1)
                    pe.wait_ge(Z["yr_ready"], t + 1 + FIRST)
                    tr(p4, ta).then_inc(Z["yr_t_done"], 1)
                    pe.wait_ge(Z["qat_ready"], t + 1 + FIRST)
                    pe.wait_ge(Z["win_ready"], t + 1 + FIRST)
                    pe.wait_ge(Z["y_summed"], t + 1 + FIRST)
                    for n in range(AH):
                        c, half = n // 2, slice(AD * (n % 2), AD * (n % 2) + AD)
                        if n >= 2:
                            pe.wait_ge(Z["masked"], t * AH + n - 1 + FIRST)
                        pe.matmul((p5, p6)[n % 2][:, 0:WIN], qat[half, c * P:(c + 1) * P], win[half, :], start=True, stop=True).then_inc(Z["score_done"], 1)
                    pe.wait_ge(Z["ys_ready"], t + 1 + FIRST)
                    tr(p2, ug).then_inc(Z["ys_t_done"], 1)
                    for n in range(AH):
                        k0 = AD * (n % 2)
                        pe.wait_ge(Z["exp_ready"], t * AH + n + 1 + FIRST)
                        if n >= 2:
                            pe.wait_ge(Z["pt_ready"], t * AH + n - 1 + FIRST)
                        for j in range(3):
                            last = pe.transpose((p7, p0)[n % 2][:, j * P:(j + 1) * P], sc[:, n, j * P:(j + 1) * P], R["ident"][:])
                        last.then_inc(Z["pt_done"], 1)
                        pe.wait_ge(Z["pt_ready"], t * AH + n + 1 + FIRST)
                        for j in range(3):
                            last = pe.matmul(p1[:, n * AD:(n + 1) * AD], pt[:, n % 2, j * P:(j + 1) * P], R["va"][:, t + j, k0:k0 + AD],
                                             start=(j == 0), stop=(j == 2))
                        last.then_inc(Z["pv_done"], 1)
                    pe.wait_ge(Z["ya_ready"], t + 1 + FIRST)
                    tr(p0, qsq).then_inc(Z["ya_t_done"], 1)

        @block.scalar
        def _(act):
            with act.Fori(0, T // 2) as i:
                for b in range(2):
                    t = i * 2 + b
                    to = lambda ins, name: ring(act, ins, Z[name], t + 1)
                    act.wait_ge(Z["qa_done"], t + 1 + FIRST)
                    act.wait_ge(Z["ya_t_done"], t + FIRST)
                    to(act.activation(qsq[:], p0[:], ACT.Square), "qsq_ready")
                    act.wait_ge(Z["qss_ready"], t + 1 + FIRST)
                    to(act.activation(small[:, 8:16], small[:, 0:8], ACT.Sqrt, scale=1.0 / AD, bias=R["eps"][:]), "qrms_ready")
                    act.wait_ge(Z["score_done"], t * AH + FIRST)
                    to(act.copy(win[:], R["ka_t"][:].rearrange("p t n -> p (t n)")[:, bass.ds(t * P, WIN)]), "win_ready")
                    act.wait_ge(Z["qt_done"], t + 1 + FIRST)
                    act.wait_ge(Z["cross_b_done"], t + FIRST)
                    to(act.copy(qt[:], p5[:]), "qt_ready")
                    act.wait_ge(Z["qat_done"], t + 1 + FIRST)
                    to(act.copy(qat[:], p0[:]), "qat_ready")
                    act.wait_ge(Z["vs_done"], t + 1 + FIRST)
                    act.wait_ge(Z["mix_done"], t + FIRST)
                    to(act.activation(vg[:], p2[:], ACT.Gelu), "vg_ready")
                    act.wait_ge(Z["us_done"], t + 1 + FIRST)
                    act.wait_ge(Z["ys_t_done"], t + FIRST)
                    to(act.activation(ug[:], p3[:], ACT.Gelu), "ug_ready")
                    act.wait_ge(Z["gr_done"], t + 1 + FIRST)
                    act.wait_ge(Z["yr_ready"], t + FIRST)
                    to(act.activation(silu[:], p4[:], ACT.Silu), "silu_ready")
                    act.wait_ge(Z["var_ready"], t + 1 + FIRST)
                    to(act.activation(mv[:, 2:3], mv[:, 1:2], ACT.Sqrt, scale=1.0, bias=R["eps"][:]), "std_ready")
                    act.wait_ge(Z["ss_ready"], t + 1 + FIRST)
                    to(act.activation(small[:, 20:24], small[:, 16:20], ACT.Sqrt, scale=1.0 / RD, bias=R["eps"][:]), "rms_ready")
                    act.wait_ge(Z["max_ready"], t + 1 + FIRST)
                    for n in range(AH):
                        ring(act, act.activation(sc[:, n, :], sc[:, n, :], ACT.Exp, bias=att[:, AH + n:AH + n + 1], scale=1.0,
                                                 accum_out=att[:, 2 * AH + n:2 * AH + n + 1]), Z["exp_ready"], t * AH + n + 1)
                    to(act.activation(att[:, 3 * AH:4 * AH], att[:, 3 * AH:4 * AH], ACT.Exp), "sinks_ready")
                    act.wait_ge(yt_out, t * 16 + FIRST)
                    act.wait_ge(Z["ya_t_done"], t + 1 + FIRST)
                    to(act.copy(yt[:, 2 * RW:3 * RW], p0[:]), "ya_t_ready")

        @block.vector
        def _(dve):
            step = Order(dve, Z["dve_step"])
            dve.wait_ge(par_in, 16 * len(par))
            hv = lambda ap: ap.rearrange("p (h d) -> p h d", h=RH)
            av = lambda ap: ap.rearrange("p (h d) -> p h d", h=AH)
            with dve.Fori(0, T // 2) as i:
                for b in range(2):
                    t = i * 2 + b
                    step.turn()
                    to = lambda ins, name: ring(dve, ins, Z[name], t + 1)
                    tt = dve.tensor_tensor
                    dve.wait_ge(Z["qsq_ready"], t + 1 + FIRST)
                    to(dve.tensor_reduce(small[:, 0:8], av(qsq[:]), AX.X, ALU.add), "qss_ready")
                    dve.wait_ge(Z["qrms_ready"], t + 1 + FIRST)
                    step(dve.reciprocal(small[:, 8:16], small[:, 8:16]))
                    dve.wait_ge(Z["yr_t_done"], t + FIRST)
                    step(tt(av(tc[:]), av(p0[:]), wide(small[:, 8:16], AD), ALU.mult))
                    step(tt(av(tc[:]), av(tc[:]), over(gain[:], AH), ALU.mult))
                    dve.wait_ge(tab_in, t * 16 + 16)
                    dve.wait_ge(Z["qat_done"], t + FIRST)
                    rotate(step, dve, qa[:], tc[:], tab[:, NR:NR + AD // 2], tab[:, NR + AD // 2:NR + NA], (ta[:], tb[:]), AH, AD // 2,
                           lambda ins: to(ins, "qa_ready"))
                    dve.wait_ge(Z["qr_done"], t + 1 + FIRST)
                    dve.wait_ge(Z["qt_done"], t + FIRST)
                    rotate(step, dve, qr[:], p1[:], tab[:, 0:RD // 2], tab[:, RD // 2:RD], (ta[:], tb[:]), RH, RD // 2,
                           lambda ins: to(ins, "qr_ready"))
                    dve.wait_ge(Z["vg_ready"], t + 1 + FIRST)
                    step(dve.bn_stats(bn[:], vg[:]))
                    to(dve.bn_aggr(mv[:, 0:2], bn[:]), "var_ready")
                    dve.wait_ge(Z["st_done"], t + 1 + FIRST)
                    dve.wait_ge(Z["inner_done"], t + FIRST)
                    to(tt(st[:], p6[:], R["decay_mask"][:].rearrange("p h n -> p (h n)"), ALU.mult), "st_ready")
                    dve.wait_ge(Z["std_ready"], t + 1 + FIRST)
                    step(dve.reciprocal(mv[:, 3:4], mv[:, 2:3]))
                    step(dve.tensor_scalar(vg[:], vg[:], mv[:, 0:1], mv[:, 3:4], ALU.subtract, ALU.mult))
                    step(tt(vg[:], vg[:], ln_g[:], ALU.mult))
                    to(tt(vg[:], vg[:], ln_b[:], ALU.add), "vn_ready")
                    dve.wait_ge(Z["cross_f_done"], t + 1 + FIRST)
                    step(tt(hv(ta[:]), hv(p7[:]), wide(R["decays"][:, 16:16 + RH], RD), ALU.mult))
                    step(tt(ta[:], ta[:], p5[:], ALU.add))
                    dve.wait_ge(Z["cross_b_done"], t + 1 + FIRST)
                    step(tt(hv(tb[:]), hv(p6[:]), wide(R["decays"][:, 24 + RH:24 + 2 * RH], RD), ALU.mult))
                    to(tt(ta[:], ta[:], tb[:], ALU.add), "y_summed")
                    step(tt(tb[:], ta[:], ta[:], ALU.mult))
                    to(dve.tensor_reduce(small[:, 16:20], hv(tb[:]), AX.X, ALU.add), "ss_ready")
                    dve.wait_ge(Z["rms_ready"], t + 1 + FIRST)
                    step(dve.reciprocal(small[:, 20:24], small[:, 20:24]))
                    dve.wait_ge(Z["silu_ready"], t + 1 + FIRST)
                    step(tt(hv(tb[:]), hv(silu[:]), wide(small[:, 20:24], RD), ALU.mult))
                    to(tt(ta[:], ta[:], tb[:], ALU.mult), "yr_ready")
                    dve.wait_ge(Z["mix_done"], t + 1 + FIRST)
                    step(tt(hv(tb[:]), hv(p2[:]), wide(b_mix[:], GC), ALU.add))
                    dve.wait_ge(Z["ug_ready"], t + 1 + FIRST)
                    to(tt(ug[:], ug[:], tb[:], ALU.mult), "ys_ready")
                    dve.wait_ge(Z["yr_t_done"], t + 1 + FIRST)
                    dve.wait_ge(yt_out, t * 16 + FIRST)
                    to(tt(hv(yt[:, 0:RW]), hv(p4[:]), wide(R["col_ret"][:], P), ALU.mult), "yr_t_ready")
                    dve.wait_ge(mask_in, t * 16 + 16)
                    dve.wait_ge(Z["pt_done"], t * AH + FIRST)
                    for n in range(AH):
                        dve.wait_ge(Z["score_done"], t * AH + n + 1 + FIRST)
                        ring(dve, dve.scalar_tensor_tensor(out=sc[:, n, :], in0=(p5, p6)[n % 2][:, 0:WIN], scalar=AD ** -0.5, in1=mask[:],
                                                           op0=ALU.mult, op1=ALU.add), Z["masked"], t * AH + n + 1)
                    step(dve.tensor_reduce(att[:, 0:AH], sc[:], AX.X, ALU.max))
                    step(tt(att[:, 0:AH], att[:, 0:AH], R["sink"][:], ALU.max))
                    step(tt(att[:, 3 * AH:4 * AH], R["sink"][:], att[:, 0:AH], ALU.subtract))
                    to(dve.tensor_scalar(att[:, AH:2 * AH], att[:, 0:AH], -1.0, None, ALU.mult), "max_ready")
                    dve.wait_ge(Z["ys_t_done"], t + 1 + FIRST)
                    to(dve.tensor_copy(yt[:, RW:2 * RW], p2[:]), "ys_t_ready")
                    for n in range(AH):
                        dve.wait_ge(Z["pt_done"], t * AH + n + 1 + FIRST)
                        dve.wait_ge(Z["pv_done"], t * AH + max(n - 1, 0) + FIRST)
                        ring(dve, dve.tensor_copy(pt[:, n % 2, :], (p7, p0)[n % 2][:, 0:WIN]), Z["pt_ready"], t * AH + n + 1)
                    dve.wait_ge(Z["sinks_ready"], t + 1 + FIRST)
                    step(tt(att[:, 2 * AH:3 * AH], att[:, 2 * AH:3 * AH], att[:, 3 * AH:4 * AH], ALU.add))
                    step(dve.reciprocal(att[:, 2 * AH:3 * AH], att[:, 2 * AH:3 * AH]))
                    dve.wait_ge(Z["pv_done"], t * AH + AH + FIRST)
                    to(tt(av(qsq[:]), av(p1[:]), wide(att[:, 2 * AH:3 * AH], AD), ALU.mult), "ya_ready")


def merge_stage(nc, A, R, X):
    with ExitStack() as ctx:
        sem = lambda n: R["semaphores"].new(nc, "m_" + n)
        sb = lambda n, s: ctx.enter_context(nc.sbuf_tensor("m_" + n, s, F32))
        pb = lambda n, s=(P, HB): ctx.enter_context(nc.psum_tensor("m_" + n, list(s), F32))
        wg, wp, wo = sb("wg", [P, DC, 3 * D]), sb("wp", [P, 4, 3 * D]), sb("wo", [P, DC, D])
        xnt, yt, gain = sb("xnt", [P, DC, P]), sb("yt", [P, 3 * RW]), sb("gain", [P, D])
        sg, merged, mt, h = sb("sg", [P, 2, HB]), sb("merged", [P, D]), sb("mt", [P, D]), sb("h", [P, D])
        rms = sb("rms", [P, 3])
        p_g, p_p, p_t, part, p_o = [pb(f"p_g{n}") for n in range(2)], [pb(f"p_p{n}") for n in range(2)], pb("p_t"), pb("part"), pb("p_o", (P, D))
        yt_in, xnt_in, x_in, wo_in, h_out, xn_out = (sem(n) for n in ("yt_in", "xnt_in", "x_in", "wo_in", "h_out", "xn_out"))
        w_in = [sem(f"w{n}_in") for n in range(6)]
        gate_done, proj_done, sg_ready, merged_part, mt_done, mt_ready, dve_step = (
            sem(n) for n in ("gate_done", "proj_done", "sg_ready", "merged_part", "mt_done", "mt_ready", "dve_step"))
        h_done, h_ready, square_ready, rms_ready, xn_ready = (sem(n) for n in ("h_done", "h_ready", "square_ready", "rms_ready", "xn_ready"))
        R["semaphores"].prime(nc)
        block = ctx.enter_context(nc.Block())
        U = 6

        def columns(n):
            half, br = divmod(n, 3)
            return slice(br * D + half * HB, br * D + (half + 1) * HB)

        @block.sync
        def _(sp):
            def load_tile(t):
                sp.wait_ge(proj_done, t * U + FIRST)
                sp.dma_start(xnt[:], X["xnt"][t].rearrange("p (c n) -> p c n", c=DC)).then_inc(xnt_in, 16)
                sp.dma_start(yt[:], X["yt"][t]).then_inc(yt_in, 16)
                sp.wait_ge(xn_ready, t + FIRST)
                sp.wait_ge(h_out, t * 16 + FIRST)
                sp.dma_start(h[:], A["x"][t]).then_inc(x_in, 16)

            load_tile(0)
            for n in range(U):
                sp.dma_start(wg[:, :, columns(n)], A["w_gates"][:, :, columns(n)]).then_inc(w_in[n], 16)
                sp.dma_start(wp[:, :, columns(n)], A["w_proj"][:, :, columns(n)]).then_inc(w_in[n], 16)
            sp.dma_start(wo[:], A["w_out"]).then_inc(wo_in, 16)
            sp.dma_start(gain[:], A["norm_ffn"].partition_broadcast(P)).then_inc(wo_in, 16)
            with sp.Fori(1, T) as t:
                load_tile(t)

        @block.tensor
        def _(pe):
            def transpose_half(half, t):
                for c in range(4):
                    last = pe.transpose(p_t[:, c * P:(c + 1) * P], merged[:, half * HB + c * P:half * HB + (c + 1) * P], R["ident"][:])
                last.then_inc(mt_done, 1)

            with pe.Fori(0, T) as t:
                pe.wait_ge(xnt_in, t * 16 + 16)
                pe.wait_ge(yt_in, t * 16 + 16)
                for n in range(U):
                    pe.wait_ge(w_in[n], 32)
                    pe.wait_ge(merged_part, t * U + max(n - 1, 0) + FIRST)
                    matmuls(pe, p_g[n % 2][:], [(xnt[:, c, :], wg[:, c, columns(n)]) for c in range(DC)]).then_inc(gate_done, 1)
                    br = n % 3
                    matmuls(pe, p_p[n % 2][:], [(yt[:, br * RW + c * P:br * RW + (c + 1) * P], wp[:, c, columns(n)]) for c in range(4)]).then_inc(proj_done, 1)
                    if n == U - 2:
                        pe.wait_ge(merged_part, t * U + 3 + FIRST)
                        pe.wait_ge(mt_ready, t * 2 + FIRST)
                        transpose_half(0, t)
                pe.wait_ge(wo_in, 32)
                pe.wait_ge(mt_ready, t * 2 + 1 + FIRST)
                pe.wait_ge(h_ready, t + FIRST)
                for c in range(4):
                    for half in range(2):
                        pe.matmul(p_o[:, half * HB:(half + 1) * HB], mt[:, c * P:(c + 1) * P], wo[:, c, half * HB:(half + 1) * HB], start=(c == 0), stop=False)
                pe.wait_ge(merged_part, t * U + U + FIRST)
                transpose_half(1, t)
                pe.wait_ge(mt_ready, t * 2 + 2 + FIRST)
                for c in range(4, 8):
                    for half in range(2):
                        last = pe.matmul(p_o[:, half * HB:(half + 1) * HB], mt[:, c * P:(c + 1) * P], wo[:, c, half * HB:(half + 1) * HB], start=False, stop=(c == 7))
                last.then_inc(h_done, 1)

        @block.scalar
        def _(act):
            def keep_half(t, half):
                act.wait_ge(mt_done, t * 2 + half + 1 + FIRST)
                act.wait_ge(xn_out, t * 16 + FIRST)
                ring(act, act.copy(mt[:, half * HB:(half + 1) * HB], p_t[:]), mt_ready, t * 2 + half + 1)

            with act.Fori(0, T) as t:
                for n in range(U):
                    u = t * U + n
                    act.wait_ge(gate_done, u + 1 + FIRST)
                    act.wait_ge(merged_part, t * U + max(n - 1, 0) + FIRST)
                    ring(act, act.activation(sg[:, n % 2, :], p_g[n % 2][:], ACT.Sigmoid), sg_ready, u + 1)
                    if n == U - 1:
                        keep_half(t, 0)
                keep_half(t, 1)
                act.wait_ge(h_ready, t + 1 + FIRST)
                ring(act, act.activation(merged[:], h[:], ACT.Square, accum_out=rms[:, 0:1]), square_ready, t + 1)
                act.dma_start(X["h"][t], h[:]).then_inc(h_out, 16)
                ring(act, act.activation(rms[:, 1:2], rms[:, 0:1], ACT.Sqrt, scale=1.0 / D, bias=R["eps"][:]), rms_ready, t + 1)
                act.wait_ge(xn_ready, t + 1 + FIRST)
                act.dma_start(X["xn"][t], mt[:]).then_inc(xn_out, 16)
            act.wait_ge(h_out, 16 * T + FIRST)
            act.wait_ge(xn_out, 16 * T + FIRST)

        @block.vector
        def _(dve):
            step = Order(dve, dve_step)
            dve.wait_ge(wo_in, 32)
            with dve.Fori(0, T) as t:
                step.turn()
                for n in range(U):
                    half, br = divmod(n, 3)
                    u = t * U + n
                    m = merged[:, half * HB:(half + 1) * HB]
                    dve.wait_ge(sg_ready, u + 1 + FIRST)
                    dve.wait_ge(proj_done, u + 1 + FIRST)
                    if br == 0:
                        ring(dve, dve.tensor_tensor(m, p_p[n % 2][:], sg[:, n % 2, :], ALU.mult), merged_part, u + 1)
                    else:
                        step(dve.tensor_tensor(part[:], p_p[n % 2][:], sg[:, n % 2, :], ALU.mult))
                        ring(dve, dve.tensor_tensor(m, m, part[:], ALU.add), merged_part, u + 1)
                dve.wait_ge(h_done, t + 1 + FIRST)
                dve.wait_ge(x_in, t * 16 + 16)
                ring(dve, dve.tensor_tensor(h[:], p_o[:], h[:], ALU.add), h_ready, t + 1)
                dve.wait_ge(rms_ready, t + 1 + FIRST)
                step(dve.reciprocal(rms[:, 2:3], rms[:, 1:2]))
                ring(dve, dve.scalar_tensor_tensor(out=mt[:], in0=h[:], scalar=rms[:, 2:3], in1=gain[:], op0=ALU.mult, op1=ALU.mult), xn_ready, t + 1)


def experts_stage(nc, A, R, X):
    N = TOPK
    GROUPS = N // 2
    HQ = 2 * PC
    with ExitStack() as ctx:
        sem = lambda n: R["semaphores"].new(nc, "e_" + n)
        sb = lambda n, s, d=F32: ctx.enter_context(nc.sbuf_tensor("e_" + n, s, d))
        pb = lambda n, s, d=F32: ctx.enter_context(nc.psum_tensor("e_" + n, s, d))
        rows = sb("rows", [P, SLOTS, 2 * D])
        at = sb("at", [P, 2, N], U32)
        wg, wq, keys = sb("wg", [P, DC, D]), sb("wq", [P, DC, PH * HQ]), sb("keys", [P, 2 * PH, PK])
        xn, xn_next, xnt = sb("xn", [P, D]), sb("xn_next", [P, D]), sb("xnt", [P, D])
        h2 = sb("h2", [P, D])
        hp = sb("hp", [P, D])
        o = sb("o", [P, D])
        expert, gate = sb("expert", [P, NSEL], U32), sb("gate", [P, NSEL])
        dots, wts, rms = sb("dots", [P, N]), sb("wts", [P, N]), sb("rms", [P, 3])
        q, qt, s = sb("q", [P, HQ]), sb("qt", [P, HQ]), sb("s", [P, 2, PK])
        cand, pick = sb("cand", [P, CAND]), sb("pick", [P, CAND])
        top, top_at, top_f = sb("top", [P, 2, TOPK]), sb("top_at", [P, 2, TOPK], U32), sb("top_f", [P, 2, TOPK])
        best, best_at = sb("best", [P, TOPK]), sb("best_at", [P, TOPK], U32)
        part_u, part_f, row = sb("part_u", [P, 2, TOPK], U32), sb("part_f", [P, 2, TOPK]), sb("row", [P, 2, TOPK])
        soft, total = sb("soft", [P, TOPK]), sb("total", [P, 1])
        p_t, acc, acc2 = (pb(n, [P, D]) for n in ("p_t", "acc", "acc2"))
        prod = [sb(f"prod{n}", [P, D], BF16) for n in range(2)]
        p_q, p_s = pb("p_q", [P, 2 * HQ]), pb("p_s", [P, 2, PK])
        par_in, next_in, h_in, pp_in, out_done = (sem(n) for n in ("par_in", "next_in", "h_in", "pp_in", "out_done"))
        row_in = [sem(f"row_in{n}") for n in range(SLOTS)]
        names = ("at_ready slot_free dot_done act_done wts_ready acc_done h2_ready out_ready dve_step "
                 "xt_done xnt_ready xn_ready q_done q_ready qt_done qt_ready s_done s_ready searched logits_ready exp_ready chosen "
                 "square_ready rms_ready rstd_ready h2t_done h2t_ready gate_done sg_ready").split()
        Z = {n: sem(n) for n in names}
        R["semaphores"].prime(nc)
        block = ctx.enter_context(nc.Block())
        par = [(wq, A["peer_wq"]), (keys, A["peer_keys_t"]), (wg, A["ple_gate"])]

        def tiles(eng, tile):
            tile(0, False, True)
            with eng.Fori(1, T - 1) as t:
                tile(t, True, True)
            tile(T - 1, True, False)

        def steps(eng, step):
            step(0)
            step(1)
            with eng.Fori(2, PH - 1) as j:
                step(j)
            step(PH - 1)

        @block.gpsimd
        def _(pool):
            def rows_of(b, c, part, first):
                pool.wait_ge(Z["chosen"], c + 1 + FIRST)
                ring(pool, pool.tensor_copy(at[:, b, :], expert[:, part]), Z["at_ready"], c + 1)
                for n in range(N):
                    if not first or n >= SLOTS:
                        pool.wait_ge(Z["acc_done"], c * N + n - SLOTS + 1 + FIRST)
                    if not (first and 0 < n < SLOTS):
                        pool.sem_inc(Z["slot_free"], 1)
                    pool.indirect_dma_start(out=rows[:, n % SLOTS, :], out_offset=None, in_=A["peer_uv"],
                                            in_offset=bass.IndirectOffsetOnAxis(ap=at[:, b, n:n + 1], axis=0)).then_inc(row_in[n % SLOTS], 16)

            rows_of(0, 0, slice(0, N), True)
            rows_of(1, 1, slice(N, 2 * N), False)
            with pool.Fori(1, PH // 2) as i:
                for b in range(2):
                    rows_of(b, i * 2 + b, bass.ds(i * 2 * N + b * N, N), False)
            with pool.Fori(1, T) as t:
                with pool.Fori(0, PH // 2) as i:
                    for b in range(2):
                        rows_of(b, t * PH + i * 2 + b, bass.ds(i * 2 * N + b * N, N), False)

        @block.sync
        def _(sp):
            sp.dma_start(xn_next[:], X["xn"][0]).then_inc(next_in, 16)
            sp.dma_start(hp[:], X["h"][0]).then_inc(h_in, 16)
            for dst, src in par:
                sp.dma_start(dst[:], src).then_inc(par_in, 16)

            def finish(t):
                sp.dma_start(hp[:], X["pp"][t]).then_inc(pp_in, 16)
                sp.wait_ge(Z["out_ready"], t + 1 + FIRST)
                sp.dma_start(A["out"][t], o[:]).then_inc(out_done, 16)

            def tile(t, finishes, routes):
                if routes:
                    sp.wait_ge(Z["xt_done"], t + 1 + FIRST)
                    sp.wait_ge(Z["xn_ready"], t + 1 + FIRST)
                    sp.dma_start(xn_next[:], X["xn"][t + 1]).then_inc(next_in, 16)
                sp.wait_ge(Z["acc_done"], t * NSEL + 1 + FIRST)
                if finishes:
                    finish(t - 1)
                if routes:
                    sp.dma_start(hp[:], X["h"][t + 1]).then_inc(h_in, 16)

            tiles(sp, tile)
            finish(T - 1)
            sp.wait_ge(out_done, 16 * T + FIRST)

        @block.tensor
        def _(pe):
            pe.wait_ge(par_in, 16 * len(par))

            def transpose_next(t):
                pe.wait_ge(next_in, t * 16 + 16)
                for c in range(DC):
                    last = pe.transpose(p_t[:, c * P:(c + 1) * P], xn_next[:, c * P:(c + 1) * P], R["ident"][:])
                last.then_inc(Z["xt_done"], 1)

            def scores(t, j, cols, pair):
                r = t * PH + j
                pe.wait_ge(Z["xnt_ready"], t + 1 + FIRST)
                pe.wait_ge(Z["q_ready"], r + FIRST)
                matmuls(pe, p_q[:, 0:HQ], [(xnt[:, c * P:(c + 1) * P], wq[:, c, cols]) for c in range(DC)]).then_inc(Z["q_done"], 1)
                pe.wait_ge(Z["q_ready"], r + 1 + FIRST)
                pe.wait_ge(Z["qt_ready"], r + FIRST)
                for k in range(2):
                    last = pe.transpose(p_q[:, HQ + k * PC:HQ + (k + 1) * PC], q[:, k * PC:(k + 1) * PC], R["ident"][:])
                last.then_inc(Z["qt_done"], 1)
                pe.wait_ge(Z["qt_ready"], r + 1 + FIRST)
                pe.wait_ge(Z["s_ready"], r + FIRST)
                for k in range(2):
                    last = pe.matmul(p_s[:, k, :], qt[:, k * PC:(k + 1) * PC], keys[:, pair(k), :], start=True, stop=True)
                last.then_inc(Z["s_done"], 1)

            def heads(t, first, last):
                with pe.Fori(first, last) as j:
                    scores(t, j, bass.ds(j * HQ, HQ), lambda k: j * 2 + k)

            def transpose_sum(t):
                pe.wait_ge(Z["h2_ready"], t + 1 + FIRST)
                for c in range(DC):
                    last = pe.transpose(p_t[:, c * P:(c + 1) * P], h2[:, c * P:(c + 1) * P], R["ident"][:])
                last.then_inc(Z["h2t_done"], 1)

            def gate_product(t):
                pe.wait_ge(Z["h2t_ready"], t + 1 + FIRST)
                for half in range(2):
                    hs = slice(half * HB, (half + 1) * HB)
                    last = matmuls(pe, p_t[:, hs], [(o[:, c * P:(c + 1) * P], wg[:, c, hs]) for c in range(DC)])
                last.then_inc(Z["gate_done"], 1)

            def tile(t, finishes, routes):
                if finishes:
                    pe.wait_ge(Z["sg_ready"], t - 1 + FIRST)
                if routes:
                    if not finishes:
                        pe.wait_ge(Z["xnt_ready"], t + 1 + FIRST)
                    transpose_next(t + 1)
                    scores(t + 1, 0, slice(0, HQ), lambda k: k)
                if finishes:
                    transpose_sum(t - 1)
                    gate_product(t - 1)
                if routes:
                    heads(t + 1, 1, PH)

            transpose_next(0)
            heads(0, 0, PH)
            tiles(pe, tile)
            pe.wait_ge(Z["sg_ready"], T - 1 + FIRST)
            transpose_sum(T - 1)
            gate_product(T - 1)

        @block.scalar
        def _(act):
            def keep_transposed(t):
                act.wait_ge(Z["xt_done"], t + 1 + FIRST)
                act.wait_ge(Z["q_done"], t * PH + FIRST)
                ring(act, act.copy(xnt[:], p_t[:]), Z["xnt_ready"], t + 1)

            def keep_query(r):
                act.wait_ge(Z["q_done"], r + 1 + FIRST)
                act.wait_ge(Z["qt_done"], r + FIRST)
                ring(act, act.copy(q[:], p_q[:, 0:HQ]), Z["q_ready"], r + 1)
                act.wait_ge(Z["qt_done"], r + 1 + FIRST)
                act.wait_ge(Z["s_done"], r + FIRST)
                ring(act, act.copy(qt[:], p_q[:, HQ:2 * HQ]), Z["qt_ready"], r + 1)

            def keep_scores(r):
                act.wait_ge(Z["s_done"], r + 1 + FIRST)
                act.wait_ge(Z["searched"], r + FIRST)
                ring(act, act.copy(s[:], p_s[:]), Z["s_ready"], r + 1)

            def exponentials(r):
                act.wait_ge(Z["logits_ready"], r + 1 + FIRST)
                ring(act, act.activation(soft[:], soft[:], ACT.Exp), Z["exp_ready"], r + 1)

            def next_input(t):
                act.wait_ge(next_in, t * 16 + 16)
                act.wait_ge(Z["dot_done"], t * NSEL + FIRST)
                ring(act, act.copy(xn[:], xn_next[:]), Z["xn_ready"], t + 1)

            def norm(t):
                act.wait_ge(Z["h2_ready"], t + 1 + FIRST)
                act.wait_ge(out_done, t * 16 + FIRST)
                ring(act, act.activation(o[:], h2[:], ACT.Square, accum_out=rms[:, 0:1]), Z["square_ready"], t + 1)
                ring(act, act.activation(rms[:, 1:2], rms[:, 0:1], ACT.Sqrt, scale=1.0 / D, bias=R["eps"][:]), Z["rms_ready"], t + 1)

            def keep_sum(t, part):
                act.wait_ge(Z["h2t_done"], t + 1 + FIRST)
                for c in range(part * DC // 2, (part + 1) * DC // 2):
                    ins = act.mul(o[:, c * P:(c + 1) * P], p_t[:, c * P:(c + 1) * P], R["col_ple"][:, c:c + 1])
                if part:
                    ring(act, ins, Z["h2t_ready"], t + 1)

            def sigmoid(t):
                act.wait_ge(Z["rstd_ready"], t + 1 + FIRST)
                act.wait_ge(Z["gate_done"], t + 1 + FIRST)
                ring(act, act.activation(o[:], p_t[:], ACT.Sigmoid, scale=rms[:, 2:3]), Z["sg_ready"], t + 1)

            def tile(t, finishes, routes):
                def step(j):
                    c, r = t * PH + j, (t + 1) * PH + j
                    for k in range(GROUPS):
                        act.wait_ge(Z["dot_done"], c * N + 2 * k + 2 + FIRST)
                        ring(act, act.activation(dots[:, 2 * k:2 * k + 2], dots[:, 2 * k:2 * k + 2], ACT.Gelu), Z["act_done"], c * GROUPS + k + 1)
                        first, second = isinstance(j, int) and j == 0, isinstance(j, int) and j == 1
                        if k == 0 and routes and first:
                            keep_transposed(t + 1)
                        if k == 1 and finishes and first:
                            norm(t - 1)
                        if k == 2 and routes:
                            keep_query(r)
                        if k == 3 and routes:
                            keep_scores(r)
                        if k in (4, 5) and finishes and first:
                            keep_sum(t - 1, k - 4)
                        if k == 4 and finishes and second:
                            sigmoid(t - 1)
                        if k == 7 and routes:
                            exponentials(r)
                        if k == 7 and routes and isinstance(j, int) and j == PH - 1:
                            next_input(t + 1)

                steps(act, step)

            act.wait_ge(next_in, 16)
            ring(act, act.copy(xn[:], xn_next[:]), Z["xn_ready"], 1)
            keep_transposed(0)
            with act.Fori(0, PH) as j:
                keep_query(j)
                keep_scores(j)
                exponentials(j)
            tiles(act, tile)
            norm(T - 1)
            keep_sum(T - 1, 0)
            keep_sum(T - 1, 1)
            sigmoid(T - 1)

        @block.vector
        def _(dve):
            order = Order(dve, Z["dve_step"])
            tt = dve.tensor_tensor
            grid = lambda ap: ap.rearrange("p (a b) -> p a b", a=TOPK)
            square = [P, TOPK, TOPK]

            def top16(scores, values, where):
                for k in range(2):
                    eight = slice(8 * k, 8 * k + 8)
                    order(dve.max(values[:, eight], scores))
                    order(dve.max_index(where[:, eight], values[:, eight], scores))
                    if k == 0:
                        order(dve.match_replace(out=scores, in_to_replace=values[:, eight], in_values=scores, imm_value=-3e38))

            def search(r, half):
                if half == 0:
                    dve.wait_ge(Z["s_ready"], r + 1 + FIRST)
                order.hold()
                top16(s[:, half, :], top[:, half, :], top_at[:, half, :])

            def pairs(r):
                ring(dve, tt(grid(cand[:]), top[:, 0, :].unsqueeze(2).to_broadcast(square), top[:, 1, :].unsqueeze(1).to_broadcast(square), ALU.add),
                     Z["searched"], r + 1)
                order.hold()
                top16(cand[:], best[:], best_at[:])
                ring(dve, tt(soft[:], best[:], best[:, 0:1].to_broadcast([P, TOPK]), ALU.subtract), Z["logits_ready"], r + 1)

            def choose(r, part):
                order(dve.tensor_scalar(part_u[:, 0, :], best_at[:], 4, None, ALU.logical_shift_right))
                order(dve.tensor_scalar(part_u[:, 1, :], best_at[:], 15, None, ALU.bitwise_and))
                order(dve.tensor_copy(part_f[:], part_u[:]))
                order(dve.tensor_copy(top_f[:], top_at[:]))
                for k in range(2):
                    order(tt(grid(pick[:]), part_f[:, k, :].unsqueeze(2).to_broadcast(square), R["iota16"][:].unsqueeze(1).to_broadcast(square), ALU.is_equal))
                    order(tt(grid(pick[:]), grid(pick[:]), top_f[:, k, :].unsqueeze(1).to_broadcast(square), ALU.mult))
                    order(dve.tensor_reduce(row[:, k, :], grid(pick[:]), AX.X, ALU.add))
                order(dve.scalar_tensor_tensor(out=row[:, 0, :], in0=row[:, 0, :], scalar=float(PK), in1=row[:, 1, :], op0=ALU.mult, op1=ALU.add))
                ring(dve, dve.tensor_copy(expert[:, part], row[:, 0, :]), Z["chosen"], r + 1)
                dve.wait_ge(Z["exp_ready"], r + 1 + FIRST)
                order(dve.tensor_reduce(total[:], soft[:], AX.X, ALU.add))
                order(dve.reciprocal(total[:], total[:]))
                order(tt(gate[:, part], soft[:], total[:].to_broadcast([P, TOPK]), ALU.mult))

            def dot(c, n):
                lap = n // SLOTS
                dve.wait_ge(row_in[n % SLOTS], c * 32 + lap * 16 + 16)
                dve.wait_ge(Z["dot_done"], c * N + max(n - 1, 0) + FIRST)
                dve.scalar_tensor_tensor(out=prod[n % 2][:], in0=rows[:, n % SLOTS, 0:D], scalar=1.0, in1=xn[:], op0=ALU.mult, op1=ALU.mult,
                                         accum_out=dots[:, n:n + 1]).then_inc(Z["dot_done"], 1)

            def weigh(c, k, part, t=None):
                ks = slice(2 * k, 2 * k + 2)
                dve.wait_ge(Z["act_done"], c * GROUPS + k + 1 + FIRST)
                ring(dve, tt(wts[:, ks], dots[:, ks], gate[:, part], ALU.mult), Z["wts_ready"], c * GROUPS + k + 1)
                for n in (2 * k, 2 * k + 1):
                    sum_ = (acc, acc2)[n % 2]
                    row_v, weight = rows[:, n % SLOTS, D:2 * D], wts[:, n:n + 1]
                    dve.wait_ge(Z["acc_done"], c * N + max(n - 1, 0) + FIRST)
                    if t is not None and n == 0:
                        dve.wait_ge(h_in, t * 16 + 16)
                    if t is not None and n == 1:
                        ins = dve.tensor_scalar(sum_[:], row_v, weight, None, ALU.mult)
                    else:
                        ins = dve.scalar_tensor_tensor(out=sum_[:], in0=row_v, scalar=weight, in1=sum_[:] if t is None else hp[:], op0=ALU.mult, op1=ALU.add)
                    ins.then_inc(Z["acc_done"], 1)

            def reciprocal_rms(t):
                dve.wait_ge(Z["rms_ready"], t + 1 + FIRST)
                ring(dve, dve.reciprocal(rms[:, 2:3], rms[:, 1:2]), Z["rstd_ready"], t + 1)

            def output(t):
                dve.wait_ge(Z["sg_ready"], t + 1 + FIRST)
                dve.wait_ge(pp_in, t * 16 + 16)
                order(tt(o[:], o[:], hp[:], ALU.mult))
                ring(dve, tt(o[:], o[:], h2[:], ALU.add), Z["out_ready"], t + 1)

            def tile(t, finishes, routes):
                def step(j):
                    c, r = t * PH + j, (t + 1) * PH + j
                    fixed = isinstance(j, int)
                    cols = (lambda k, n: slice(j * N + k, j * N + k + n)) if fixed else (lambda k, n: bass.ds(j * N + k, n))
                    order.turn()
                    for k in range(GROUPS):
                        if k + 1 < GROUPS:
                            dot(c, 2 * k + 2)
                            dot(c, 2 * k + 3)
                        elif not (fixed and j == PH - 1):
                            dot(c + 1, 0)
                            dot(c + 1, 1)
                        weigh(c, k, cols(2 * k, 2), t if fixed and j == 0 and k == 0 else None)
                        if k == 2 and finishes and fixed and j == 0:
                            reciprocal_rms(t - 1)
                        if k in (4, 5) and routes:
                            search(r, k - 4)
                        if k == 6 and routes:
                            pairs(r)
                        if k == 7 and routes:
                            choose(r, cols(0, TOPK))
                        if k == 7 and finishes and fixed and j == 1:
                            output(t - 1)
                            order.hold()

                dve.wait_ge(Z["xn_ready"], t + 1 + FIRST)
                dot(t * PH, 0)
                dot(t * PH, 1)
                steps(dve, step)
                dve.wait_ge(Z["acc_done"], (t + 1) * NSEL + FIRST)
                order.turn()
                order(dve.tensor_copy(h2[:], acc[:]))
                ring(dve, tt(h2[:], h2[:], acc2[:], ALU.add), Z["h2_ready"], t + 1)

            with dve.Fori(0, PH) as j:
                order.turn()
                search(j, 0)
                search(j, 1)
                pairs(j)
                choose(j, bass.ds(j * N, N))
            tiles(dve, tile)
            reciprocal_rms(T - 1)
            output(T - 1)


SPILLS = {"xnt": [T, P, DC * P], "v": [T, P, RW], "kt": [T, P, RW], "yt": [T, P, 3 * RW], "pp": [T, P, D], "h": [T, P, D], "xn": [T, P, D]}


def build_program(nc, A, X=None):
    if X is None:
        X = {n: nc.dram_tensor(f"kept_{n}", s, F32).ap() for n, s in SPILLS.items()}
    with ExitStack() as ctx:
        R = {"semaphores": Semaphores()}
        for n, s, d in (("ident", [P, P], F32), ("eps", [P, 1], F32), ("col_mix", [P, DC], F32), ("col_ret", [P, RH], F32), ("col_ple", [P, DC], F32),
                        ("sink", [P, AH], F32), ("decays", [P, 40], F32), ("iota16", [P, TOPK], F32)):
            R[n] = ctx.enter_context(nc.sbuf_tensor("all_" + n, s, d))
        with ExitStack() as mixers:
            for n, s in (("decay_mask", [P, RH, P]), ("state_f", [P, T + 1, RW]), ("state_b", [P, T + 1, RW]), ("ka_t", [P, T + 2, P]), ("va", [P, T + 2, AKW])):
                R[n] = mixers.enter_context(nc.sbuf_tensor("mix_" + n, s, F32))
            setup(nc, A, R)
            R["semaphores"].clear(nc)
            keys_stage(nc, A, R, X)
            R["semaphores"].clear(nc)
            branches_stage(nc, A, R, X)
            R["semaphores"].clear(nc)
        merge_stage(nc, A, R, X)
        R["semaphores"].clear(nc)
        experts_stage(nc, A, R, X)


def constants():
    def rotary(dim):
        inv = (np.float32(1.0) / (np.float32(10000.0) ** (np.arange(0, dim, 2, dtype=np.float32) / np.float32(dim)))).astype(np.float32)
        ang = np.arange(S, dtype=np.float32)[:, None] * inv[None, :]
        return np.cos(ang).astype(np.float32), np.sin(ang).astype(np.float32)

    (cr, sr), (ca, sa) = rotary(RD), rotary(AD)
    scale = np.float32(RD ** -0.5)
    table = np.concatenate([cr, sr, cr * scale, sr * scale, ca, sa], axis=1).reshape(T, P, NR + NA)
    pos = np.arange(P)
    key = np.arange(WIN)
    near = np.abs(pos[:, None] + P - key[None, :]) <= P
    mask = np.empty((T, P, WIN), np.float32)
    for t in range(T):
        there = (t * P - P + key >= 0) & (t * P - P + key < S)
        mask[t] = np.where(near & there[None, :], 0.0, NEG)
    j, c = pos[:, None], pos[None, :]
    distance = np.stack([np.maximum(c - j, 0), np.maximum(j - c, 0)], axis=1).astype(np.float32)
    exponents = np.stack([P - 1 - pos, pos, pos + 1, P - pos], axis=1).astype(np.float32)
    return {"rotary": table, "window_mask": mask, "distance": distance, "exponent_col": exponents, "ident": np.eye(P, dtype=np.float32),
            "iota16": np.tile(np.arange(TOPK, dtype=np.float32), (P, 1))}


def layout(x, p, norm_mix, w_in, ret_decay, ret_norm, sgu_ln_g, sgu_ln_b, sgu_w, sgu_b, att_q_norm, att_k_norm, att_sink, w_proj_ret, w_proj_sgu,
           w_proj_att, w_out, norm_ffn, peer_wq, peer_keys, peer_u, peer_v, norm_ple, ple_gate, ple_proj):
    c = np.ascontiguousarray
    chunks = lambda w: c(np.asarray(w).reshape(-1, P, w.shape[-1]).transpose(1, 0, 2))
    col = lambda v: c(np.asarray(v).reshape(-1, P).T)
    w = np.asarray(w_in[0])
    offs = np.cumsum([0, RW, RW, RW, RW, G * GC, G * GC, AW, AKW, AKW, D, D, D])
    q_r, k_r, v_r, g_r, u_s, v_s, q_a, k_a, v_a, g0, g1, g2 = (w[:, offs[n]:offs[n + 1]] for n in range(12))
    heads = [n // 2 + (AH // AKV) * (n % 2) for n in range(AH)]
    by_head = [slice(n * AD, (n + 1) * AD) for n in heads]
    q_a = np.concatenate([q_a[:, s] for s in by_head], axis=1)
    wpa = np.concatenate([np.asarray(w_proj_att[0])[s] for s in by_head], axis=0)
    arrays = {
        "x": c(np.asarray(x[0]).reshape(T, P, D)),
        "p_t": c(np.asarray(p[0, 0]).reshape(T, P, 2, P).transpose(0, 3, 2, 1)),
        "w_keys": chunks(np.concatenate([k_r, v_r, k_a, v_a], axis=1)),
        "w_branches": chunks(np.concatenate([q_a, q_r, v_s, u_s, g_r], axis=1)),
        "w_gates": chunks(np.concatenate([g0, g1, g2], axis=1)),
        "w_proj": chunks(np.concatenate([w_proj_ret[0], w_proj_sgu[0], wpa], axis=1)),
        "w_out": chunks(w_out[0]), "peer_wq": chunks(peer_wq[0]), "ple_gate": chunks(ple_gate[0]), "ple_proj": chunks(ple_proj[0]),
        "peer_keys_t": c(np.asarray(peer_keys[0]).reshape(2 * PH, PK, PC).transpose(2, 0, 1)),
        "peer_uv": np.concatenate([peer_u[0], peer_v[0]], axis=1),
        "norm_mix_col": col(norm_mix[0]), "ret_norm_col": col(ret_norm[0]), "norm_ple_col": col(norm_ple[0]), "norm_ffn": np.asarray(norm_ffn[0]),
        "ret_decay": np.asarray(ret_decay[0]).reshape(2 * RH), "att_sink": np.asarray(att_sink[0])[heads],
        "att_q_norm": np.asarray(att_q_norm[0]), "att_k_norm": np.asarray(att_k_norm[0]),
        "sgu_ln_g": np.asarray(sgu_ln_g[0]), "sgu_ln_b": np.asarray(sgu_ln_b[0]),
        "sgu_w_t": c(np.asarray(sgu_w[0]).transpose(2, 0, 1)), "sgu_b_col": c(np.asarray(sgu_b[0]).T),
    }
    return {n: c(a) for n, a in (arrays | constants()).items()}


def kernel(**inputs):
    import concourse.bacc as bacc
    from concourse.bass_utils import run_bass_kernel_spmd

    arrays = layout(**inputs)
    nc = bacc.Bacc("TRN2", target_bir_lowering=False, num_devices=1)
    A = {n: nc.dram_tensor(f"in_{n}", a.shape, mybir.dt.from_np(a.dtype), kind="ExternalInput").ap() for n, a in arrays.items()}
    A["out"] = nc.dram_tensor("out", (T, P, D), F32, kind="ExternalOutput").ap()
    build_program(nc, A)
    r = run_bass_kernel_spmd(nc, [{f"in_{n}": a for n, a in arrays.items()}], core_ids=[0])
    return r.results[0]["out"].reshape(1, S, D)
```

```python
from contextlib import ExitStack

import numpy as np
import concourse.bass as bass
from concourse import mybir
from concourse.alu_op_type import AluOpType as ALU

F32 = mybir.dt.float32
BF16 = mybir.dt.bfloat16
U32 = mybir.dt.uint32
ACT = mybir.ActivationFunctionType
AX = mybir.AxisListType

P = 128
S, D = 1024, 1024
T = S // P
DC = D // P
assert DC == T
EPS = 1e-6
RH, RD = 4, 128
RW = RH * RD
G, GC = 4, 128
AH, AKV, AD = 8, 2, 64
AW, AKW = AH * AD, AKV * AD
WIN = 3 * P
NEG = -1e30
PH, PK, PC, TOPK = 8, 128, 128, 16
NSEL = PH * TOPK
CAND = TOPK * TOPK
PLE = 256
HB = 512
KEPT = 3
NR = 4 * (RD // 2)
NA = 2 * (AD // 2)

FIRST = 1
SLOTS = 8


class Semaphores:

    def __init__(self):
        self.taken = []

    def new(self, nc, name):
        self.taken.append((name, nc.alloc_semaphore(name)))
        return self.taken[-1][1]

    def prime(self, nc):
        for name, semaphore in self.taken:
            if not name.rstrip("0123456789").endswith(("_in", "_step")):
                nc.gpsimd.sem_inc(semaphore, FIRST)
        nc.all_engine_barrier()

    def clear(self, nc):
        nc.clear_and_free_semaphores([semaphore for _, semaphore in self.taken])
        nc.all_engine_barrier()
        self.taken = []


class Order:

    def __init__(self, eng, sem):
        self.eng, self.sem, self.n = eng, sem, 0

    def __call__(self, ins):
        ins.then_inc(self.sem, 1)
        self.n += 1
        self.eng.wait_ge(self.sem, self.n)

    def hold(self):
        self.eng.sem_inc(self.sem, 1)
        self.n += 1

    def turn(self):
        self.hold()
        self.eng.sem_clear(self.sem)
        self.n = 0


def ring(eng, ins, sem, value):
    ins.then_inc(sem, 1)
    eng.wait_ge(sem, value + FIRST)


def wide(ap, n):
    return ap.unsqueeze(2).to_broadcast([ap.shape[0], ap.shape[1], n])


def over(ap, n):
    return ap.unsqueeze(1).to_broadcast([ap.shape[0], n, ap.shape[1]])


def matmuls(pe, out, pairs):
    for n, (lhsT, rhs) in enumerate(pairs):
        last = pe.matmul(out, lhsT, rhs, start=(n == 0), stop=(n == len(pairs) - 1))
    return last


def rotate(order, eng, out, x, cos, sin, scratch, heads, half, finish):
    v = lambda ap: ap.rearrange("p (h a d) -> p h a d", h=heads, a=2)
    a, b = scratch
    hv = lambda ap, k: v(ap)[:, :, k, :]
    c, s = over(cos, heads), over(sin, heads)
    for k in range(2):
        order(eng.tensor_tensor(hv(a, k), hv(x, k), c, ALU.mult))
        order(eng.tensor_tensor(hv(b, k), hv(x, 1 - k), s, ALU.mult))
    order(eng.tensor_tensor(hv(out, 0), hv(a, 0), hv(b, 0), ALU.subtract))
    finish(eng.tensor_tensor(hv(out, 1), hv(a, 1), hv(b, 1), ALU.add))


class Decays:

    def __init__(self, A, R, sem, sb):
        K = 2 * RH
        self.R, self.K = R, K
        self.Z = {n: sem(n) for n in ("params_in", "lg_ready", "logs_done", "exponents_ready", "exp_done")}
        self.x, self.e, self.u, self.lnu, self.z, self.one, self.lg = (sb(f"lg_{n}", [P, K]) for n in ("x", "e", "u", "ln", "z", "one", "log"))
        self.ex, self.dm, self.dm2 = sb("lg_exponents", [P, 5 * K]), sb("lg_distances", [P, RH, P]), sb("lg_distances2", [P, RH, P])
        self.diff, self.col = sb("lg_diff", [P, 2, P]), sb("lg_col", [P, 4])
        self.loads = [(R["ident"], A["ident"]), (R["col_mix"], A["norm_mix_col"]), (self.x, A["ret_decay"].partition_broadcast(P)),
                      (self.diff, A["distance"]), (self.col, A["exponent_col"]), (R["col_ret"], A["ret_norm_col"]), (R["col_ple"], A["norm_ple_col"]),
                      (R["sink"], A["att_sink"].partition_broadcast(P)), (R["iota16"], A["iota16"])]

    def load(self, sp):
        for dst, src in self.loads:
            sp.dma_start(dst[:], src).then_inc(self.Z["params_in"], 16)

    def loaded(self, eng):
        eng.wait_ge(self.Z["params_in"], 16 * len(self.loads))

    def scalar_part(self, act):
        Z = self.Z
        act.wait_ge(Z["lg_ready"], 1 + FIRST)
        act.activation(self.e[:], self.z[:], ACT.Exp).then_inc(Z["logs_done"], 1)
        act.wait_ge(Z["lg_ready"], 2 + FIRST)
        act.activation(self.lnu[:], self.u[:], ACT.Ln).then_inc(Z["logs_done"], 1)
        act.wait_ge(Z["exponents_ready"], 1 + FIRST)
        act.activation(self.R["decays"][:], self.ex[:], ACT.Exp).then_inc(Z["exp_done"], 1)
        act.activation(self.R["decay_mask"][:], self.dm[:], ACT.Exp).then_inc(Z["exp_done"], 1)

    def vector_part(self, dve, step):
        R, Z, K, x, e, u, lnu, z, one, lg, ex, dm, dm2, diff, col = (
            self.R, self.Z, self.K, self.x, self.e, self.u, self.lnu, self.z, self.one, self.lg, self.ex, self.dm, self.dm2, self.diff, self.col)
        step(dve.tensor_scalar(z[:], x[:], -1.0, None, ALU.mult))
        step(dve.tensor_tensor(z[:], z[:], x[:], ALU.min))
        ring(dve, dve.tensor_scalar(x[:], x[:], 0.0, None, ALU.min), Z["lg_ready"], 1)
        dve.wait_ge(Z["logs_done"], 1 + FIRST)
        ring(dve, dve.tensor_scalar(u[:], e[:], 1.0, None, ALU.add), Z["lg_ready"], 2)
        step(dve.tensor_scalar(z[:], u[:], -1.0, None, ALU.add))
        step(dve.tensor_scalar(one[:], z[:], 0.0, None, ALU.is_equal))
        step(dve.tensor_tensor(z[:], z[:], one[:], ALU.add))
        dve.wait_ge(Z["logs_done"], 2 + FIRST)
        step(dve.tensor_tensor(lnu[:], lnu[:], e[:], ALU.mult))
        step(dve.tensor_tensor(e[:], e[:], one[:], ALU.mult))
        step(dve.reciprocal(z[:], z[:]))
        step(dve.tensor_tensor(lnu[:], lnu[:], z[:], ALU.mult))
        step(dve.tensor_tensor(lnu[:], lnu[:], e[:], ALU.add))
        step(dve.tensor_tensor(lg[:], x[:], lnu[:], ALU.subtract))
        for j in range(4):
            step(dve.tensor_scalar(ex[:, j * K:(j + 1) * K], lg[:], col[:, j:j + 1], None, ALU.mult))
        step(dve.tensor_scalar(ex[:, 4 * K:5 * K], lg[:], float(P), None, ALU.mult))
        for h in range(RH):
            step(dve.tensor_scalar(dm[:, h, :], diff[:, 0, :], lg[:, h:h + 1], None, ALU.mult))
            step(dve.tensor_scalar(dm2[:, h, :], diff[:, 1, :], lg[:, RH + h:RH + h + 1], None, ALU.mult))
        ring(dve, dve.tensor_tensor(dm[:], dm[:], dm2[:], ALU.add), Z["exponents_ready"], 1)
        dve.wait_ge(Z["exp_done"], 2 + FIRST)


def keys_stage(nc, A, R, X):
    NW = 2 * RW + 2 * AKW
    with ExitStack() as ctx:
        sem = lambda n: R["semaphores"].new(nc, "k_" + n)
        sb = lambda n, s: ctx.enter_context(nc.sbuf_tensor("k_" + n, s, F32))
        pb = lambda n, s: ctx.enter_context(nc.psum_tensor("k_" + n, s, F32))
        w, wp = sb("w", [P, DC, NW]), sb("wp", [P, 2, D])
        pt, pp = sb("pt", [P, 2, P]), sb("pp", [P, D])
        x, xs, junk = sb("x", [P, D]), sb("xs", [P, D]), sb("junk", [P, D])
        xnt = sb("xnt", [P, DC, P])
        tab = sb("tab", [P, NR + NA])
        gain = sb("gain", [P, AD])
        rms, rstd = sb("rms", [P, 2]), sb("rstd", [P, 1])
        k, ra, rb = sb("k", [P, RW]), sb("ra", [P, RW]), sb("rb", [P, RW])
        v, kt = sb("v", [P, RW]), sb("kt", [P, RW])
        kf, kb = sb("kf", [P, RW]), sb("kb", [P, RW])
        ka, ksq, kss = sb("ka", [P, AKW]), sb("ksq", [P, AKW]), sb("kss", [P, 4])
        p_xt = pb("p_xt", [P, D])
        p_k, p_v, p_a, p_kt, p_f, p_b = (pb(f"p_{n}", [P, HB]) for n in ("k", "v", "a", "kt", "f", "b"))
        wk_in, wv_in, wa_in, wp_in, gain_in, x_in, tab_in, pt_in = (sem(n) for n in ("wk_in", "wv_in", "wa_in", "wp_in", "gain_in", "x_in", "tab_in", "pt_in"))
        next_w_in, xnt_out, v_out, kt_out, pp_out = (sem(n) for n in ("next_w_in", "xnt_out", "v_out", "kt_out", "pp_out"))
        Z = {n: sem(n) for n in ("rms_ready square_ready xs_ready xt_done xnt_ready k_done v_done a_done pp_done pp_ready v_ready va_ready k_ready kt_done "
                                 "kt_ready kf_ready kb_ready f_done b_done b_saved f_state ksq_ready kss_ready krms_ready ka_ready kat_done kat_ready "
                                 "eps_ready zeroed dve_step").split()}
        decays = Decays(A, R, sem, sb)
        R["semaphores"].prime(nc)
        block = ctx.enter_context(nc.Block())

        def tiles(eng, tile):
            with eng.Fori(0, T - 1) as t:
                tile(t, True)
            tile(T - 1, False)

        @block.sync
        def _(sp):
            def tile(t, more):
                if more:
                    sp.wait_ge(Z["xs_ready"], t + 1 + FIRST)
                    sp.dma_start(x[:], A["x"][t + 1]).then_inc(x_in, 16)
                sp.wait_ge(Z["xnt_ready"], t + 1 + FIRST)
                sp.dma_start(X["xnt"][t], xnt[:]).then_inc(xnt_out, 16)
                sp.wait_ge(Z["v_ready"], t + 1 + FIRST)
                sp.dma_start(X["v"][t], v[:]).then_inc(v_out, 16)
                sp.wait_ge(Z["pp_ready"], t + 1 + FIRST)
                sp.dma_start(X["pp"][t], pp[:]).then_inc(pp_out, 16)
                if more:
                    sp.dma_start(pt[:], A["p_t"][t + 1]).then_inc(pt_in, 16)
                sp.wait_ge(Z["kt_ready"], t + 1 + FIRST)
                sp.dma_start(X["kt"][t], kt[:]).then_inc(kt_out, 16)
                sp.dma_start(R["w_branches"][:, t, :], A["w_branches_kept"][t]).then_inc(next_w_in, 16)
                if more:
                    sp.wait_ge(Z["ka_ready"], t + 1 + FIRST)
                    sp.dma_start(tab[:], A["rotary"][t + 1]).then_inc(tab_in, 16)

            sp.dma_start(x[:], A["x"][0]).then_inc(x_in, 16)
            decays.load(sp)
            sp.dma_start(w[:, :, 0:RW], A["w_keys"][:, :, 0:RW]).then_inc(wk_in, 16)
            sp.dma_start(w[:, :, RW:2 * RW], A["w_keys"][:, :, RW:2 * RW]).then_inc(wv_in, 16)
            sp.dma_start(tab[:], A["rotary"][0]).then_inc(tab_in, 16)
            sp.dma_start(pt[:], A["p_t"][0]).then_inc(pt_in, 16)
            sp.dma_start(wp[:], A["ple_proj"]).then_inc(wp_in, 16)
            sp.dma_start(w[:, :, 2 * RW:NW], A["w_keys"][:, :, 2 * RW:NW]).then_inc(wa_in, 16)
            sp.dma_start(gain[:], A["att_k_norm"].partition_broadcast(P)).then_inc(gain_in, 16)
            tiles(sp, tile)
            sp.wait_ge(next_w_in, 16 * T)
            for s in (pp_out, xnt_out, v_out, kt_out):
                sp.wait_ge(s, 16 * T + FIRST)

        @block.scalar
        def _(act):
            def norm(t):
                act.wait_ge(x_in, t * 16 + 16)
                act.wait_ge(Z["xs_ready"], t + FIRST)
                ring(act, act.activation(junk[:], x[:], ACT.Square, accum_out=rms[:, 0:1]), Z["square_ready"], t + 1)
                ring(act, act.activation(rms[:, 1:2], rms[:, 0:1], ACT.Sqrt, scale=1.0 / D, bias=R["eps"][:]), Z["rms_ready"], t + 1)

            def tile(t, more):
                to = lambda ins, name: ring(act, ins, Z[name], t + 1)
                act.wait_ge(Z["v_done"], t + 1 + FIRST)
                act.wait_ge(v_out, t * 16 + FIRST)
                act.wait_ge(Z["b_done"], t + FIRST)
                to(act.copy(v[:], p_v[:]), "v_ready")
                if more:
                    norm(t + 1)
                act.wait_ge(Z["pp_done"], t + 1 + FIRST)
                act.wait_ge(pp_out, t * 16 + FIRST)
                to(act.copy(pp[:], p_xt[:]), "pp_ready")
                act.wait_ge(Z["a_done"], t + 1 + FIRST)
                act.wait_ge(Z["kss_ready"], t + FIRST)
                to(act.activation(ksq[:], p_a[:, 0:AKW], ACT.Square), "ksq_ready")
                to(act.copy(R["va"][:, t + 1, :], p_a[:, AKW:2 * AKW]), "va_ready")
                act.wait_ge(Z["kss_ready"], t + 1 + FIRST)
                to(act.activation(kss[:, 2:4], kss[:, 0:2], ACT.Sqrt, scale=1.0 / AD, bias=R["eps"][:]), "krms_ready")
                act.wait_ge(Z["kt_done"], t + 1 + FIRST)
                act.wait_ge(kt_out, t * 16 + FIRST)
                to(act.copy(kt[:], p_kt[:]), "kt_ready")
                act.wait_ge(Z["b_done"], t + 1 + FIRST)
                to(act.copy(R["state_b"][:, t, :], p_b[:]), "b_saved")
                act.wait_ge(Z["kat_done"], t + 1 + FIRST)
                to(act.copy(R["ka_t"][:, t + 1, :], p_a[:, 2 * AKW:2 * AKW + P]), "kat_ready")

            act.wait_ge(Z["eps_ready"], 1 + FIRST)
            norm(0)
            decays.scalar_part(act)
            act.wait_ge(Z["zeroed"], 1 + FIRST)
            tiles(act, tile)

        @block.vector
        def _(dve):
            step = Order(dve, Z["dve_step"])
            hv = lambda ap: ap.rearrange("p (h d) -> p h d", h=RH)
            kv = lambda ap: ap.rearrange("p (h d) -> p h d", h=AKV)
            tt = dve.tensor_tensor

            def normed(t):
                dve.wait_ge(Z["rms_ready"], t + 1 + FIRST)
                step(dve.reciprocal(rstd[:], rms[:, 1:2]))
                dve.wait_ge(Z["xt_done"], t + FIRST)
                ring(dve, dve.tensor_scalar(xs[:], x[:], rstd[:, 0:1], None, ALU.mult), Z["xs_ready"], t + 1)

            def keep_transposed(t):
                dve.wait_ge(Z["xt_done"], t + 1 + FIRST)
                dve.wait_ge(Z["a_done"], t + FIRST)
                dve.wait_ge(xnt_out, t * 16 + FIRST)
                ring(dve, tt(xnt[:], p_xt[:].rearrange("p (c n) -> p c n", c=DC), wide(R["col_mix"][:], P), ALU.mult), Z["xnt_ready"], t + 1)

            def tile(t, more):
                step.turn()
                to = lambda ins, name: ring(dve, ins, Z[name], t + 1)
                dve.wait_ge(tab_in, t * 16 + 16)
                dve.wait_ge(Z["k_done"], t + 1 + FIRST)
                dve.wait_ge(Z["b_done"], t + FIRST)
                q2 = NR // 2
                rotate(step, dve, k[:], p_k[:], tab[:, q2:q2 + RD // 2], tab[:, q2 + RD // 2:NR], (ra[:], rb[:]), RH, RD // 2,
                       lambda ins: to(ins, "k_ready"))
                to(tt(hv(kf[:]), hv(k[:]), wide(R["decays"][:, 0:RH], RD), ALU.mult), "kf_ready")
                to(tt(hv(kb[:]), hv(k[:]), wide(R["decays"][:, 8 + RH:8 + 2 * RH], RD), ALU.mult), "kb_ready")
                if more:
                    normed(t + 1)
                dve.wait_ge(Z["ksq_ready"], t + 1 + FIRST)
                dve.wait_ge(Z["krms_ready"], t + FIRST)
                to(dve.tensor_reduce(kss[:, 0:2], kv(ksq[:]), AX.X, ALU.add), "kss_ready")
                dve.wait_ge(Z["krms_ready"], t + 1 + FIRST)
                step(dve.reciprocal(kss[:, 2:4], kss[:, 2:4]))
                step(tt(kv(ra[:, 0:AKW]), kv(p_a[:, 0:AKW]), wide(kss[:, 2:4], AD), ALU.mult))
                step(tt(kv(ra[:, 0:AKW]), kv(ra[:, 0:AKW]), over(gain[:], AKV), ALU.mult))
                dve.wait_ge(Z["kat_done"], t + FIRST)
                rotate(step, dve, ka[:], ra[:, 0:AKW], tab[:, NR:NR + AD // 2], tab[:, NR + AD // 2:NR + NA],
                       (ra[:, AKW:2 * AKW], rb[:, 0:AKW]), AKV, AD // 2, lambda ins: to(ins, "ka_ready"))
                if more:
                    keep_transposed(t + 1)
                st = lambda n: hv(R["state_f"][:, n, :])
                dve.wait_ge(Z["f_done"], t + 1 + FIRST)
                step(tt(st(t + 1), st(t), wide(R["decays"][:, 32:32 + RH], RD), ALU.mult))
                to(tt(st(t + 1), st(t + 1), hv(p_f[:]), ALU.add), "f_state")

            ring(dve, dve.memset(R["eps"][:], EPS), Z["eps_ready"], 1)
            decays.loaded(dve)
            normed(0)
            keep_transposed(0)
            decays.vector_part(dve, step)
            step(dve.memset(R["ka_t"][:], 0.0))
            step(dve.memset(R["va"][:], 0.0))
            dve.memset(R["state_f"][:, 0, :], 0.0).then_inc(Z["zeroed"], 1)
            dve.wait_ge(Z["zeroed"], 1 + FIRST)
            dve.wait_ge(gain_in, 16)
            tiles(dve, tile)

        @block.tensor
        def _(pe):
            def transpose_input(t):
                pe.wait_ge(Z["xs_ready"], t + 1 + FIRST)
                pe.wait_ge(Z["pp_ready"], t + FIRST)
                for c in range(DC):
                    last = pe.transpose(p_xt[:, c * P:(c + 1) * P], xs[:, c * P:(c + 1) * P], R["ident"][:])
                last.then_inc(Z["xt_done"], 1)

            def tile(t, more):
                cut = lambda a, n, out: matmuls(pe, out, [(xnt[:, c, :], w[:, c, a:a + n]) for c in range(DC)])
                pe.wait_ge(Z["xnt_ready"], t + 1 + FIRST)
                pe.wait_ge(wk_in, 16)
                pe.wait_ge(Z["k_ready"], t + FIRST)
                cut(0, RW, p_k[:]).then_inc(Z["k_done"], 1)
                pe.wait_ge(wv_in, 16)
                pe.wait_ge(Z["v_ready"], t + FIRST)
                cut(RW, RW, p_v[:]).then_inc(Z["v_done"], 1)
                pe.wait_ge(pt_in, t * 16 + 16)
                pe.wait_ge(wp_in, 16)
                for half in range(2):
                    hs = slice(half * HB, (half + 1) * HB)
                    last = matmuls(pe, p_xt[:, hs], [(pt[:, n, :], wp[:, n, hs]) for n in range(2)])
                last.then_inc(Z["pp_done"], 1)
                pe.wait_ge(wa_in, 16)
                pe.wait_ge(Z["ka_ready"], t + FIRST)
                pe.wait_ge(Z["va_ready"], t + FIRST)
                pe.wait_ge(Z["kat_ready"], t + FIRST)
                cut(2 * RW, 2 * AKW, p_a[:, 0:2 * AKW]).then_inc(Z["a_done"], 1)
                if more:
                    transpose_input(t + 1)
                pe.wait_ge(Z["k_ready"], t + 1 + FIRST)
                pe.wait_ge(Z["kt_ready"], t + FIRST)
                for h in range(RH):
                    last = pe.transpose(p_kt[:, h * P:(h + 1) * P], k[:, h * P:(h + 1) * P], R["ident"][:])
                last.then_inc(Z["kt_done"], 1)
                pe.wait_ge(Z["v_ready"], t + 1 + FIRST)
                pe.wait_ge(Z["kf_ready"], t + 1 + FIRST)
                pe.wait_ge(Z["f_state"], t + FIRST)
                for h in range(RH):
                    hs = slice(h * P, (h + 1) * P)
                    last = pe.matmul(p_f[:, hs], kf[:, hs], v[:, hs], start=True, stop=True)
                last.then_inc(Z["f_done"], 1)
                pe.wait_ge(Z["kb_ready"], t + 1 + FIRST)
                pe.wait_ge(Z["b_saved"], t + FIRST)
                for h in range(RH):
                    hs = slice(h * P, (h + 1) * P)
                    last = pe.matmul(p_b[:, hs], kb[:, hs], v[:, hs], start=True, stop=True)
                last.then_inc(Z["b_done"], 1)
                pe.wait_ge(Z["ka_ready"], t + 1 + FIRST)
                pe.wait_ge(Z["va_ready"], t + 1 + FIRST)
                pe.transpose(p_a[:, 2 * AKW:2 * AKW + P], ka[:], R["ident"][:]).then_inc(Z["kat_done"], 1)

            decays.loaded(pe)
            transpose_input(0)
            tiles(pe, tile)


def branches_stage(nc, A, R, X):
    Q_A, Q_R, V_S, U_S, G_R = (n * HB for n in range(5))
    with ExitStack() as ctx:
        sem = lambda n: R["semaphores"].new(nc, "b_" + n)
        sb = lambda n, s: ctx.enter_context(nc.sbuf_tensor("b_" + n, s, F32))
        pb = lambda n: ctx.enter_context(nc.psum_tensor("b_" + n, [P, HB], F32))
        w_last = sb("w_last", [P, DC, (5 - KEPT) * HB])
        w_mix, ln_g, ln_b = sb("w_mix", [P, G, P]), sb("ln_g", [P, G * GC]), sb("ln_b", [P, G * GC])
        b_mix, gain = sb("b_mix", [P, G]), sb("gain", [P, AD])
        xnt = sb("xnt", [P, DC, P])
        kt, v, tab = sb("kt", [P, RW]), sb("v", [P, RW]), sb("tab", [P, NR + NA])
        mask = sb("mask", [P, WIN])
        qr, ta, tb = (sb(n, [P, RW]) for n in ("qr", "ta", "tb"))
        qt, st, silu = (sb(n, [P, RW]) for n in ("qt", "st", "silu"))
        small = sb("small", [P, 24])
        vg, ug = sb("vg", [P, G * GC]), sb("ug", [P, G * GC])
        bn, mv = sb("bn", [P, 6]), sb("mv", [P, 4])
        qa, qsq = sb("qa", [P, AW]), sb("qsq", [P, AW])
        qat, win = sb("qat", [P, AW]), sb("win", [P, WIN])
        sc = sb("sc", [P, AH, WIN])
        att = sb("att", [P, 4 * AH])
        pt = sb("pt", [P, 2, WIN])
        yt = sb("yt", [P, 3 * RW])
        p0, p1, p2, p3, p4, p5, p6, p7 = (pb(f"p{n}") for n in range(8))
        par_in, tab_in, kt_in, v_in, mask_in, yt_out = (sem(n) for n in ("par_in", "tab_in", "kt_in", "v_in", "mask_in", "yt_out"))
        xnt_in, w_in, gates_in = sem("xnt_in"), sem("w_in"), sem("gates_in")
        names = ("qa_done qr_done vs_done us_done gr_done qt_done st_done inner_done cross_f_done cross_b_done mix_done qat_done "
                 "score_done pt_done pv_done yr_t_done ys_t_done ya_t_done "
                 "qr_ready st_ready y_summed yr_ready vn_ready ys_ready qss_ready qa_ready ss_ready var_ready masked max_ready den_ready ya_ready ys_t_ready "
                 "qsq_ready qrms_ready qt_ready silu_ready vg_ready ug_ready rms_ready std_ready qat_ready win_ready exp_ready sinks_ready pt_ready yr_t_ready ya_t_ready "
                 "dve_step states_ready").split()
        Z = {n: sem(n) for n in names}
        R["semaphores"].prime(nc)
        block = ctx.enter_context(nc.Block())
        par = [(w_mix, A["sgu_w_t"]), (ln_g, A["sgu_ln_g"].partition_broadcast(P)), (ln_b, A["sgu_ln_b"].partition_broadcast(P)),
               (b_mix, A["sgu_b_col"]), (gain, A["att_q_norm"].partition_broadcast(P))]

        def tiles(eng, tile):
            tile(0, False)
            with eng.Fori(1, T) as t:
                tile(t, True)

        @block.sync
        def _(sp):
            def load(t):
                sp.wait_ge(Z["gr_done"], t + FIRST)
                sp.dma_start(xnt[:], X["xnt"][t].rearrange("p (c n) -> p c n", c=DC)).then_inc(xnt_in, 16)
                sp.wait_ge(Z["qr_ready"], t + FIRST)
                sp.wait_ge(Z["qa_ready"], t + FIRST)
                sp.dma_start(tab[:], A["rotary"][t]).then_inc(tab_in, 16)
                sp.wait_ge(Z["st_done"], t + FIRST)
                sp.dma_start(kt[:], X["kt"][t]).then_inc(kt_in, 16)
                sp.wait_ge(Z["inner_done"], t + FIRST)
                sp.dma_start(v[:], X["v"][t]).then_inc(v_in, 16)
                sp.wait_ge(Z["masked"], t * AH + FIRST)
                sp.dma_start(mask[:], A["window_mask"][t]).then_inc(mask_in, 16)

            def store(t):
                sp.wait_ge(Z["ya_t_ready"], t + 1 + FIRST)
                sp.wait_ge(Z["yr_t_ready"], t + 1 + FIRST)
                sp.wait_ge(Z["ys_t_ready"], t + 1 + FIRST)
                sp.dma_start(X["yt"][t], yt[:]).then_inc(yt_out, 16)

            load(0)
            for dst, src in par:
                sp.dma_start(dst[:], src).then_inc(par_in, 16)
            sp.dma_start(w_last[:], A["w_branches_last"]).then_inc(w_in, 16)
            sp.dma_start(R["w_gates_first"][:], A["w_gates"][:, :, 0:HB]).then_inc(gates_in, 16)
            load(1)
            with sp.Fori(1, T - 1) as t:
                load(t + 1)
                store(t - 1)
            store(T - 2)
            store(T - 1)
            sp.wait_ge(yt_out, 16 * T + FIRST)
            sp.wait_ge(gates_in, 16)

        @block.tensor
        def _(pe):
            tr = lambda out, x: [pe.transpose(out[:, c * P:(c + 1) * P], x[:, c * P:(c + 1) * P], R["ident"][:]) for c in range(4)][-1]

            def cut(column, out, done):
                late = column // HB >= KEPT
                if late:
                    pe.wait_ge(w_in, 16)
                w = lambda c: w_last[:, c, column - KEPT * HB:column - KEPT * HB + HB] if late else R["w_branches"][:, c, column:column + HB]
                matmuls(pe, out[:], [(xnt[:, c, :], w(c)) for c in range(DC)]).then_inc(Z[done], 1)

            def transpose_outputs(t):
                pe.wait_ge(Z["yr_ready"], t + 1 + FIRST)
                tr(p4, ta).then_inc(Z["yr_t_done"], 1)
                pe.wait_ge(Z["ys_ready"], t + 1 + FIRST)
                tr(p2, ug).then_inc(Z["ys_t_done"], 1)

            def transpose_probs(t, heads):
                for n in heads:
                    pe.wait_ge(Z["exp_ready"], t * AH + n + 1 + FIRST)
                    if n >= 2:
                        pe.wait_ge(Z["pt_ready"], t * AH + n - 1 + FIRST)
                    for j in range(3):
                        last = pe.transpose((p7, p6)[n % 2][:, j * P:(j + 1) * P], sc[:, n, j * P:(j + 1) * P], R["ident"][:])
                    last.then_inc(Z["pt_done"], 1)

            def values(t, heads):
                for n in heads:
                    k0 = AD * (n % 2)
                    pe.wait_ge(Z["pt_ready"], t * AH + n + 1 + FIRST)
                    for j in range(3):
                        last = pe.matmul(p5[:, n * AD:(n + 1) * AD], pt[:, n % 2, j * P:(j + 1) * P], R["va"][:, t + j, k0:k0 + AD],
                                         start=(j == 0), stop=(j == 2))
                    last.then_inc(Z["pv_done"], 1)

            def transpose_attended(t):
                pe.wait_ge(Z["ya_ready"], t + 1 + FIRST)
                tr(p7, qsq).then_inc(Z["ya_t_done"], 1)

            def scores(t, heads):
                for n in heads:
                    c, half = n // 2, slice(AD * (n % 2), AD * (n % 2) + AD)
                    if n >= 2:
                        pe.wait_ge(Z["masked"], t * AH + n - 1 + FIRST)
                    pe.matmul((p0, p1)[n % 2][:, 0:WIN], qat[half, c * P:(c + 1) * P], win[half, :], start=True, stop=True).then_inc(Z["score_done"], 1)

            def tile(t, before):
                pe.wait_ge(xnt_in, t * 16 + 16)
                if before:
                    pe.wait_ge(Z["masked"], t * AH - 1 + FIRST)
                cut(Q_A, p0, "qa_done")
                if before:
                    transpose_outputs(t - 1)
                    pe.wait_ge(Z["masked"], t * AH + FIRST)
                cut(Q_R, p1, "qr_done")
                if before:
                    pe.wait_ge(Z["y_summed"], t + FIRST)
                    transpose_probs(t - 1, (0, 1))
                pe.wait_ge(Z["ys_t_ready"], t + FIRST)
                cut(V_S, p2, "vs_done")
                if before:
                    values(t - 1, (0, 1))
                    transpose_probs(t - 1, (2, 3))
                pe.wait_ge(Z["ug_ready"], t + FIRST)
                cut(U_S, p3, "us_done")
                if before:
                    values(t - 1, (2, 3))
                    transpose_probs(t - 1, (4, 5))
                pe.wait_ge(Z["yr_t_ready"], t + FIRST)
                cut(G_R, p4, "gr_done")
                if before:
                    values(t - 1, (4, 5))
                    transpose_probs(t - 1, (6, 7))
                pe.wait_ge(Z["qr_ready"], t + 1 + FIRST)
                tr(p1, qr).then_inc(Z["qt_done"], 1)
                pe.wait_ge(Z["qa_ready"], t + 1 + FIRST)
                tr(p0, qa).then_inc(Z["qat_done"], 1)
                if before:
                    values(t - 1, (6, 7))
                pe.wait_ge(Z["qt_ready"], t + 1 + FIRST)
                pe.wait_ge(kt_in, t * 16 + 16)
                pe.wait_ge(Z["pt_ready"], t * AH + FIRST)
                for h in range(RH):
                    hs = slice(h * P, (h + 1) * P)
                    last = pe.matmul(p6[:, hs], kt[:, hs], qt[:, hs], start=True, stop=True)
                last.then_inc(Z["st_done"], 1)
                pe.wait_ge(Z["vn_ready"], t + 1 + FIRST)
                for g in range(G):
                    gs = slice(g * GC, (g + 1) * GC)
                    last = pe.matmul(p2[:, gs], w_mix[:, g, :], vg[:, gs], start=True, stop=True)
                last.then_inc(Z["mix_done"], 1)
                pe.wait_ge(Z["qat_ready"], t + 1 + FIRST)
                pe.wait_ge(Z["win_ready"], t + 1 + FIRST)
                scores(t, (0, 1))
                if before:
                    transpose_attended(t - 1)
                pe.wait_ge(Z["st_ready"], t + 1 + FIRST)
                pe.wait_ge(v_in, t * 16 + 16)
                for out, done, left, right in ((p5, "inner_done", st, lambda hs: v[:, hs]), (p6, "cross_b_done", qt, lambda hs: R["state_b"][:, t + 1, hs]),
                                               (p7, "cross_f_done", qt, lambda hs: R["state_f"][:, t, hs])):
                    if out is p6:
                        pe.wait_ge(Z["states_ready"], 1 + FIRST)
                    if out is p7:
                        pe.wait_ge(Z["ya_t_ready"], t + FIRST)
                    for h in range(RH):
                        hs = slice(h * P, (h + 1) * P)
                        last = pe.matmul(out[:, hs], left[:, hs], right(hs), start=True, stop=True)
                    last.then_inc(Z[done], 1)
                scores(t, range(2, AH))

            pe.wait_ge(par_in, 16 * len(par))
            tiles(pe, tile)
            transpose_outputs(T - 1)
            pe.wait_ge(Z["y_summed"], T + FIRST)
            transpose_probs(T - 1, (0, 1))
            for n in range(0, AH, 2):
                values(T - 1, (n, n + 1))
                if n + 2 < AH:
                    transpose_probs(T - 1, (n + 2, n + 3))
            transpose_attended(T - 1)

        @block.scalar
        def _(act):
            def exponentials(t):
                act.wait_ge(Z["max_ready"], t + 1 + FIRST)
                for n in range(AH):
                    ring(act, act.activation(sc[:, n, :], sc[:, n, :], ACT.Exp, bias=att[:, AH + n:AH + n + 1], scale=1.0,
                                             accum_out=att[:, 2 * AH + n:2 * AH + n + 1]), Z["exp_ready"], t * AH + n + 1)
                ring(act, act.activation(att[:, 3 * AH:4 * AH], att[:, 3 * AH:4 * AH], ACT.Exp), Z["sinks_ready"], t + 1)
                act.wait_ge(Z["ys_t_done"], t + 1 + FIRST)
                act.wait_ge(yt_out, t * 16 + FIRST)
                ring(act, act.copy(yt[:, RW:2 * RW], p2[:]), Z["ys_t_ready"], t + 1)

            def keep_attended(t):
                act.wait_ge(Z["ya_t_done"], t + 1 + FIRST)
                ring(act, act.copy(yt[:, 2 * RW:3 * RW], p7[:]), Z["ya_t_ready"], t + 1)

            def tile(t, before):
                to = lambda ins, name: ring(act, ins, Z[name], t + 1)
                if before:
                    exponentials(t - 1)
                    act.wait_ge(Z["ya_t_done"], t - 1 + FIRST)
                act.wait_ge(Z["qa_done"], t + 1 + FIRST)
                to(act.activation(qsq[:], p0[:], ACT.Square), "qsq_ready")
                act.wait_ge(Z["qss_ready"], t + 1 + FIRST)
                to(act.activation(small[:, 8:16], small[:, 0:8], ACT.Sqrt, scale=1.0 / AD, bias=R["eps"][:]), "qrms_ready")
                act.wait_ge(Z["score_done"], t * AH + FIRST)
                to(act.copy(win[:], R["ka_t"][:].rearrange("p t n -> p (t n)")[:, bass.ds(t * P, WIN)]), "win_ready")
                act.wait_ge(Z["vs_done"], t + 1 + FIRST)
                act.wait_ge(Z["mix_done"], t + FIRST)
                to(act.activation(vg[:], p2[:], ACT.Gelu), "vg_ready")
                act.wait_ge(Z["var_ready"], t + 1 + FIRST)
                to(act.activation(mv[:, 2:3], mv[:, 1:2], ACT.Sqrt, scale=1.0, bias=R["eps"][:]), "std_ready")
                act.wait_ge(Z["us_done"], t + 1 + FIRST)
                act.wait_ge(Z["ys_t_done"], t + FIRST)
                to(act.activation(ug[:], p3[:], ACT.Gelu), "ug_ready")
                act.wait_ge(Z["gr_done"], t + 1 + FIRST)
                act.wait_ge(Z["yr_ready"], t + FIRST)
                to(act.activation(silu[:], p4[:], ACT.Silu), "silu_ready")
                act.wait_ge(Z["qt_done"], t + 1 + FIRST)
                act.wait_ge(Z["cross_f_done"], t + FIRST)
                to(act.copy(qt[:], p1[:]), "qt_ready")
                act.wait_ge(Z["qat_done"], t + 1 + FIRST)
                to(act.copy(qat[:], p0[:]), "qat_ready")
                if before:
                    keep_attended(t - 1)
                act.wait_ge(Z["ss_ready"], t + 1 + FIRST)
                to(act.activation(small[:, 20:24], small[:, 16:20], ACT.Sqrt, scale=1.0 / RD, bias=R["eps"][:]), "rms_ready")

            tiles(act, tile)
            exponentials(T - 1)
            keep_attended(T - 1)

        @block.vector
        def _(dve):
            step = Order(dve, Z["dve_step"])
            hv = lambda ap: ap.rearrange("p (h d) -> p h d", h=RH)
            av = lambda ap: ap.rearrange("p (h d) -> p h d", h=AH)
            tt = dve.tensor_tensor

            def keep_retained(t):
                dve.wait_ge(Z["yr_t_done"], t + 1 + FIRST)
                dve.wait_ge(yt_out, t * 16 + FIRST)
                ring(dve, tt(hv(yt[:, 0:RW]), hv(p4[:]), wide(R["col_ret"][:], P), ALU.mult), Z["yr_t_ready"], t + 1)

            def keep_probs(t, heads):
                for n in heads:
                    dve.wait_ge(Z["pt_done"], t * AH + n + 1 + FIRST)
                    dve.wait_ge(Z["pv_done"], t * AH + max(n - 1, 0) + FIRST)
                    ring(dve, dve.tensor_copy(pt[:, n % 2, :], (p7, p6)[n % 2][:, 0:WIN]), Z["pt_ready"], t * AH + n + 1)

            def attended(t):
                dve.wait_ge(Z["sinks_ready"], t + 1 + FIRST)
                step(tt(att[:, 2 * AH:3 * AH], att[:, 2 * AH:3 * AH], att[:, 3 * AH:4 * AH], ALU.add))
                step(dve.reciprocal(att[:, 2 * AH:3 * AH], att[:, 2 * AH:3 * AH]))
                dve.wait_ge(Z["pv_done"], t * AH + AH + FIRST)
                ring(dve, tt(av(qsq[:]), av(p5[:]), wide(att[:, 2 * AH:3 * AH], AD), ALU.mult), Z["ya_ready"], t + 1)

            def masked(t, heads):
                for n in heads:
                    dve.wait_ge(Z["score_done"], t * AH + n + 1 + FIRST)
                    ring(dve, dve.scalar_tensor_tensor(out=sc[:, n, :], in0=(p0, p1)[n % 2][:, 0:WIN], scalar=AD ** -0.5, in1=mask[:],
                                                       op0=ALU.mult, op1=ALU.add), Z["masked"], t * AH + n + 1)

            def tile(t, before):
                step.turn()
                to = lambda ins, name: ring(dve, ins, Z[name], t + 1)
                if before:
                    keep_retained(t - 1)
                dve.wait_ge(Z["qsq_ready"], t + 1 + FIRST)
                to(dve.tensor_reduce(small[:, 0:8], av(qsq[:]), AX.X, ALU.add), "qss_ready")
                dve.wait_ge(Z["qrms_ready"], t + 1 + FIRST)
                step(dve.reciprocal(small[:, 8:16], small[:, 8:16]))
                dve.wait_ge(Z["qt_done"], t + FIRST)
                step(tt(av(qr[:]), av(p0[:]), wide(small[:, 8:16], AD), ALU.mult))
                step(tt(av(qr[:]), av(qr[:]), over(gain[:], AH), ALU.mult))
                dve.wait_ge(tab_in, t * 16 + 16)
                dve.wait_ge(Z["qat_done"], t + FIRST)
                rotate(step, dve, qa[:], qr[:], tab[:, NR:NR + AD // 2], tab[:, NR + AD // 2:NR + NA], (ta[:], tb[:]), AH, AD // 2,
                       lambda ins: to(ins, "qa_ready"))
                if before:
                    keep_probs(t - 1, (0, 1))
                dve.wait_ge(Z["qr_done"], t + 1 + FIRST)
                dve.wait_ge(Z["qt_done"], t + FIRST)
                rotate(step, dve, qr[:], p1[:], tab[:, 0:RD // 2], tab[:, RD // 2:RD], (ta[:], tb[:]), RH, RD // 2,
                       lambda ins: to(ins, "qr_ready"))
                if before:
                    keep_probs(t - 1, (2, 3))
                dve.wait_ge(Z["vg_ready"], t + 1 + FIRST)
                step(dve.bn_stats(bn[:], vg[:]))
                to(dve.bn_aggr(mv[:, 0:2], bn[:]), "var_ready")
                dve.wait_ge(Z["std_ready"], t + 1 + FIRST)
                step(dve.reciprocal(mv[:, 3:4], mv[:, 2:3]))
                step(dve.tensor_scalar(vg[:], vg[:], mv[:, 0:1], mv[:, 3:4], ALU.subtract, ALU.mult))
                step(tt(vg[:], vg[:], ln_g[:], ALU.mult))
                to(tt(vg[:], vg[:], ln_b[:], ALU.add), "vn_ready")
                if before:
                    keep_probs(t - 1, (4, 5))
                    keep_probs(t - 1, (6, 7))
                    attended(t - 1)
                dve.wait_ge(Z["st_done"], t + 1 + FIRST)
                dve.wait_ge(Z["inner_done"], t + FIRST)
                to(tt(st[:], p6[:], R["decay_mask"][:].rearrange("p h n -> p (h n)"), ALU.mult), "st_ready")
                dve.wait_ge(mask_in, t * 16 + 16)
                dve.wait_ge(Z["pt_done"], t * AH + FIRST)
                masked(t, (0, 1))
                dve.wait_ge(Z["cross_b_done"], t + 1 + FIRST)
                step(tt(hv(tb[:]), hv(p6[:]), wide(R["decays"][:, 24 + RH:24 + 2 * RH], RD), ALU.mult))
                dve.wait_ge(Z["cross_f_done"], t + 1 + FIRST)
                step(tt(hv(ta[:]), hv(p7[:]), wide(R["decays"][:, 16:16 + RH], RD), ALU.mult))
                step(tt(ta[:], ta[:], p5[:], ALU.add))
                to(tt(ta[:], ta[:], tb[:], ALU.add), "y_summed")
                masked(t, (2, 3))
                step(tt(tb[:], ta[:], ta[:], ALU.mult))
                to(dve.tensor_reduce(small[:, 16:20], hv(tb[:]), AX.X, ALU.add), "ss_ready")
                masked(t, (4, 5))
                dve.wait_ge(Z["mix_done"], t + 1 + FIRST)
                step(tt(hv(tb[:]), hv(p2[:]), wide(b_mix[:], GC), ALU.add))
                dve.wait_ge(Z["ug_ready"], t + 1 + FIRST)
                to(tt(ug[:], ug[:], tb[:], ALU.mult), "ys_ready")
                masked(t, (6, 7))
                step(dve.tensor_reduce(att[:, 0:AH], sc[:], AX.X, ALU.max))
                step(tt(att[:, 0:AH], att[:, 0:AH], R["sink"][:], ALU.max))
                step(tt(att[:, 3 * AH:4 * AH], R["sink"][:], att[:, 0:AH], ALU.subtract))
                to(dve.tensor_scalar(att[:, AH:2 * AH], att[:, 0:AH], -1.0, None, ALU.mult), "max_ready")
                dve.wait_ge(Z["rms_ready"], t + 1 + FIRST)
                step(dve.reciprocal(small[:, 20:24], small[:, 20:24]))
                dve.wait_ge(Z["silu_ready"], t + 1 + FIRST)
                step(tt(hv(tb[:]), hv(silu[:]), wide(small[:, 20:24], RD), ALU.mult))
                to(tt(ta[:], ta[:], tb[:], ALU.mult), "yr_ready")

            sb_ = lambda n: hv(R["state_b"][:, n, :])
            step(dve.memset(R["state_b"][:, T, :], 0.0))
            for t in range(T - 2, -1, -1):
                step(tt(hv(ta[:]), sb_(t + 2), wide(R["decays"][:, 32 + RH:32 + 2 * RH], RD), ALU.mult))
                last = tt(sb_(t + 1), sb_(t + 1), hv(ta[:]), ALU.add)
                if t:
                    step(last)
            ring(dve, last, Z["states_ready"], 1)
            dve.wait_ge(par_in, 16 * len(par))
            tiles(dve, tile)
            keep_retained(T - 1)
            keep_probs(T - 1, range(AH))
            attended(T - 1)


def merge_stage(nc, A, R, X):
    with ExitStack() as ctx:
        sem = lambda n: R["semaphores"].new(nc, "m_" + n)
        sb = lambda n, s: ctx.enter_context(nc.sbuf_tensor("m_" + n, s, F32))
        pb = lambda n, s=(P, HB): ctx.enter_context(nc.psum_tensor("m_" + n, list(s), F32))
        wg, wp, wo = sb("wg", [P, DC, 3 * D - HB]), sb("wp", [P, 4, 3 * D]), sb("wo", [P, DC, D])
        xnt, yt, gain = sb("xnt", [P, DC, P]), sb("yt", [P, 3 * RW]), sb("gain", [P, D])
        sg, merged, mt, h = sb("sg", [P, 2, HB]), sb("merged", [P, D]), sb("mt", [P, D]), sb("h", [P, D])
        rms = sb("rms", [P, 3])
        p_g, p_p, p_t, part, p_o = [pb(f"p_g{n}") for n in range(2)], [pb(f"p_p{n}") for n in range(2)], pb("p_t"), pb("part"), pb("p_o", (P, D))
        yt_in, xnt_in, x_in, wo_in, h_out, xn_out = (sem(n) for n in ("yt_in", "xnt_in", "x_in", "wo_in", "h_out", "xn_out"))
        w_in = [sem(f"w{n}_in") for n in range(6)]
        gate_done, proj_done, sg_ready, merged_part, mt_done, mt_ready, dve_step = (
            sem(n) for n in ("gate_done", "proj_done", "sg_ready", "merged_part", "mt_done", "mt_ready", "dve_step"))
        h_done, h_ready, square_ready, rms_ready, xn_ready = (sem(n) for n in ("h_done", "h_ready", "square_ready", "rms_ready", "xn_ready"))
        R["semaphores"].prime(nc)
        block = ctx.enter_context(nc.Block())
        U = 6

        def columns(n):
            half, br = divmod(n, 3)
            return slice(br * D + half * HB, br * D + (half + 1) * HB)

        def gate_weights(n, c):
            cols = columns(n)
            return wg[:, c, cols.start - HB:cols.stop - HB] if n else R["w_gates_first"][:, c, :]

        @block.sync
        def _(sp):
            def load_tile(t):
                sp.wait_ge(proj_done, t * U + FIRST)
                sp.dma_start(xnt[:], X["xnt"][t].rearrange("p (c n) -> p c n", c=DC)).then_inc(xnt_in, 16)
                sp.dma_start(yt[:], X["yt"][t]).then_inc(yt_in, 16)
                sp.wait_ge(xn_ready, t + FIRST)
                sp.wait_ge(h_out, t * 16 + FIRST)
                sp.dma_start(h[:], A["x"][t]).then_inc(x_in, 16)

            load_tile(0)
            for n in range(U):
                if n:
                    sp.dma_start(gate_weights(n, slice(None)), A["w_gates"][:, :, columns(n)]).then_inc(w_in[n], 16)
                sp.dma_start(wp[:, :, columns(n)], A["w_proj"][:, :, columns(n)]).then_inc(w_in[n], 16)
            sp.dma_start(wo[:], A["w_out"]).then_inc(wo_in, 16)
            sp.dma_start(gain[:], A["norm_ffn"].partition_broadcast(P)).then_inc(wo_in, 16)
            with sp.Fori(1, T) as t:
                load_tile(t)

        @block.tensor
        def _(pe):
            def transpose_half(half, t):
                for c in range(4):
                    last = pe.transpose(p_t[:, c * P:(c + 1) * P], merged[:, half * HB + c * P:half * HB + (c + 1) * P], R["ident"][:])
                last.then_inc(mt_done, 1)

            with pe.Fori(0, T) as t:
                pe.wait_ge(xnt_in, t * 16 + 16)
                pe.wait_ge(yt_in, t * 16 + 16)
                for n in range(U):
                    pe.wait_ge(w_in[n], 32 if n else 16)
                    pe.wait_ge(merged_part, t * U + max(n - 1, 0) + FIRST)
                    matmuls(pe, p_g[n % 2][:], [(xnt[:, c, :], gate_weights(n, c)) for c in range(DC)]).then_inc(gate_done, 1)
                    br = n % 3
                    matmuls(pe, p_p[n % 2][:], [(yt[:, br * RW + c * P:br * RW + (c + 1) * P], wp[:, c, columns(n)]) for c in range(4)]).then_inc(proj_done, 1)
                    if n == U - 2:
                        pe.wait_ge(merged_part, t * U + 3 + FIRST)
                        pe.wait_ge(mt_ready, t * 2 + FIRST)
                        transpose_half(0, t)
                pe.wait_ge(wo_in, 32)
                pe.wait_ge(mt_ready, t * 2 + 1 + FIRST)
                pe.wait_ge(h_ready, t + FIRST)
                for c in range(4):
                    for half in range(2):
                        pe.matmul(p_o[:, half * HB:(half + 1) * HB], mt[:, c * P:(c + 1) * P], wo[:, c, half * HB:(half + 1) * HB], start=(c == 0), stop=False)
                pe.wait_ge(merged_part, t * U + U + FIRST)
                transpose_half(1, t)
                pe.wait_ge(mt_ready, t * 2 + 2 + FIRST)
                for c in range(4, 8):
                    for half in range(2):
                        last = pe.matmul(p_o[:, half * HB:(half + 1) * HB], mt[:, c * P:(c + 1) * P], wo[:, c, half * HB:(half + 1) * HB], start=False, stop=(c == 7))
                last.then_inc(h_done, 1)

        @block.scalar
        def _(act):
            def keep_half(t, half):
                act.wait_ge(mt_done, t * 2 + half + 1 + FIRST)
                act.wait_ge(xn_out, t * 16 + FIRST)
                ring(act, act.copy(mt[:, half * HB:(half + 1) * HB], p_t[:]), mt_ready, t * 2 + half + 1)

            with act.Fori(0, T) as t:
                for n in range(U):
                    u = t * U + n
                    act.wait_ge(gate_done, u + 1 + FIRST)
                    act.wait_ge(merged_part, t * U + max(n - 1, 0) + FIRST)
                    ring(act, act.activation(sg[:, n % 2, :], p_g[n % 2][:], ACT.Sigmoid), sg_ready, u + 1)
                    if n == U - 1:
                        keep_half(t, 0)
                keep_half(t, 1)
                act.wait_ge(h_ready, t + 1 + FIRST)
                ring(act, act.activation(merged[:], h[:], ACT.Square, accum_out=rms[:, 0:1]), square_ready, t + 1)
                act.dma_start(X["h"][t], h[:]).then_inc(h_out, 16)
                ring(act, act.activation(rms[:, 1:2], rms[:, 0:1], ACT.Sqrt, scale=1.0 / D, bias=R["eps"][:]), rms_ready, t + 1)
                act.wait_ge(xn_ready, t + 1 + FIRST)
                act.dma_start(X["xn"][t], mt[:]).then_inc(xn_out, 16)
            act.wait_ge(h_out, 16 * T + FIRST)
            act.wait_ge(xn_out, 16 * T + FIRST)

        @block.vector
        def _(dve):
            step = Order(dve, dve_step)
            with dve.Fori(0, T) as t:
                step.turn()
                for n in range(U):
                    half, br = divmod(n, 3)
                    u = t * U + n
                    m = merged[:, half * HB:(half + 1) * HB]
                    dve.wait_ge(sg_ready, u + 1 + FIRST)
                    dve.wait_ge(proj_done, u + 1 + FIRST)
                    if br == 0:
                        ring(dve, dve.tensor_tensor(m, p_p[n % 2][:], sg[:, n % 2, :], ALU.mult), merged_part, u + 1)
                    else:
                        step(dve.tensor_tensor(part[:], p_p[n % 2][:], sg[:, n % 2, :], ALU.mult))
                        ring(dve, dve.tensor_tensor(m, m, part[:], ALU.add), merged_part, u + 1)
                dve.wait_ge(h_done, t + 1 + FIRST)
                dve.wait_ge(x_in, t * 16 + 16)
                ring(dve, dve.tensor_tensor(h[:], p_o[:], h[:], ALU.add), h_ready, t + 1)
                dve.wait_ge(rms_ready, t + 1 + FIRST)
                step(dve.reciprocal(rms[:, 2:3], rms[:, 1:2]))
                dve.wait_ge(wo_in, 32)
                ring(dve, dve.scalar_tensor_tensor(out=mt[:], in0=h[:], scalar=rms[:, 2:3], in1=gain[:], op0=ALU.mult, op1=ALU.mult), xn_ready, t + 1)


def experts_stage(nc, A, R, X):
    N = TOPK
    GROUPS = N // 2
    HQ = 2 * PC
    LEAD = 3
    with ExitStack() as ctx:
        sem = lambda n: R["semaphores"].new(nc, "e_" + n)
        sb = lambda n, s, d=F32: ctx.enter_context(nc.sbuf_tensor("e_" + n, s, d))
        pb = lambda n, s, d=F32: ctx.enter_context(nc.psum_tensor("e_" + n, s, d))
        rows = sb("rows", [P, SLOTS, 2 * D])
        at = sb("at", [P, 2, N], U32)
        wg, wq, keys = sb("wg", [P, DC, D]), sb("wq", [P, DC, PH * HQ]), sb("keys", [P, 2 * PH, PK])
        xn, xn_next, xnt = sb("xn", [P, D]), sb("xn_next", [P, D]), sb("xnt", [P, D])
        h2 = sb("h2", [P, D])
        hp = sb("hp", [P, D])
        o = sb("o", [P, D])
        expert, gate = sb("expert", [P, NSEL]), sb("gate", [P, NSEL])
        dots, wts, rms = sb("dots", [P, N]), sb("wts", [P, N]), sb("rms", [P, 3])
        q, qt, s = sb("q", [P, HQ]), sb("qt", [P, HQ]), sb("s", [P, 2, PK])
        cand, hot = sb("cand", [P, CAND]), sb("hot", [P, TOPK, 2, TOPK])
        top, top_at, top_f = sb("top", [P, 2, TOPK]), sb("top_at", [P, 2, TOPK], U32), sb("top_f", [P, 2, TOPK])
        best, best_at = sb("best", [P, TOPK]), sb("best_at", [P, TOPK], U32)
        part_u, part_f = sb("part_u", [P, 2, TOPK], U32), sb("part_f", [P, 2, TOPK])
        soft, total = sb("soft", [P, TOPK]), sb("total", [P, 3])
        p_t, acc, acc2 = (pb(n, [P, D]) for n in ("p_t", "acc", "acc2"))
        prod = [sb(f"prod{n}", [P, D], BF16) for n in range(2)]
        p_q, p_s = pb("p_q", [P, 2 * HQ]), pb("p_s", [P, 2, PK])
        par_in, next_in, h_in, pp_in, out_done = (sem(n) for n in ("par_in", "next_in", "h_in", "pp_in", "out_done"))
        first_in, second_in = sem("first_in"), sem("second_in")
        row_in = [sem(f"row_in{n}") for n in range(SLOTS)]
        names = ("at_ready slot_free dot_done act_done wts_ready acc_done h2_ready out_ready dve_step "
                 "xt_done xnt_ready xn_ready q_done q_ready qt_done qt_ready s_done s_ready searched best_ready parts_ready converted "
                 "neg_ready exp_ready sum_ready gate_ready chosen square_ready rms_ready rstd_ready h2t_done h2t_ready gate_done sg_ready").split()
        Z = {n: sem(n) for n in names}
        R["semaphores"].prime(nc)
        block = ctx.enter_context(nc.Block())
        first = [(wq[:, :, 0:HQ], A["peer_wq"][:, :, 0:HQ]), (keys[:], A["peer_keys_t"])]
        second = [(wq[:, :, HQ:LEAD * HQ], A["peer_wq"][:, :, HQ:LEAD * HQ])]
        par = [(wq[:, :, LEAD * HQ:PH * HQ], A["peer_wq"][:, :, LEAD * HQ:PH * HQ]), (wg[:], A["ple_gate"])]

        def tiles(eng, tile):
            tile(0, False, True)
            with eng.Fori(1, T - 1) as t:
                tile(t, True, True)
            tile(T - 1, True, False)

        def steps(eng, step):
            step(0)
            step(1)
            with eng.Fori(2, PH - LEAD) as j:
                step(j)
            for j in range(PH - LEAD, PH):
                step(j)

        def ahead(t, j):
            if isinstance(j, int) and j >= PH - LEAD:
                return j + LEAD - PH, t * PH + j + LEAD
            return j + LEAD, t * PH + j + LEAD

        def part(j, k, n):
            return slice(j * N + k, j * N + k + n) if isinstance(j, int) else bass.ds(j * N + k, n)

        @block.gpsimd
        def _(pool):
            def rows_of(b, c, columns, lead_in):
                pool.wait_ge(Z["chosen"], c + 1 + FIRST)
                ring(pool, pool.tensor_copy(at[:, b, :], expert[:, columns]), Z["at_ready"], c + 1)
                for n in range(N):
                    if not lead_in or n >= SLOTS:
                        pool.wait_ge(Z["acc_done"], c * N + n - SLOTS + 1 + FIRST)
                    if not (lead_in and 0 < n < SLOTS):
                        pool.sem_inc(Z["slot_free"], 1)
                    pool.indirect_dma_start(out=rows[:, n % SLOTS, :], out_offset=None, in_=A["peer_uv"],
                                            in_offset=bass.IndirectOffsetOnAxis(ap=at[:, b, n:n + 1], axis=0)).then_inc(row_in[n % SLOTS], 16)

            rows_of(0, 0, slice(0, N), True)
            rows_of(1, 1, slice(N, 2 * N), False)
            with pool.Fori(1, PH // 2) as i:
                for b in range(2):
                    rows_of(b, i * 2 + b, bass.ds(i * 2 * N + b * N, N), False)
            with pool.Fori(1, T) as t:
                with pool.Fori(0, PH // 2) as i:
                    for b in range(2):
                        rows_of(b, t * PH + i * 2 + b, bass.ds(i * 2 * N + b * N, N), False)

        @block.sync
        def _(sp):
            sp.dma_start(xn_next[:], X["xn"][0]).then_inc(next_in, 16)
            for dst, src in first:
                sp.dma_start(dst, src).then_inc(first_in, 16)
            for dst, src in second:
                sp.dma_start(dst, src).then_inc(second_in, 16)
            sp.dma_start(hp[:], X["h"][0]).then_inc(h_in, 16)
            for dst, src in par:
                sp.dma_start(dst, src).then_inc(par_in, 16)

            def finish(t):
                sp.dma_start(hp[:], X["pp"][t]).then_inc(pp_in, 16)
                sp.wait_ge(Z["out_ready"], t + 1 + FIRST)
                sp.dma_start(A["out"][t], o[:]).then_inc(out_done, 16)

            def tile(t, before, after):
                if after:
                    sp.wait_ge(Z["xt_done"], t + 1 + FIRST)
                    sp.wait_ge(Z["xn_ready"], t + 1 + FIRST)
                    sp.dma_start(xn_next[:], X["xn"][t + 1]).then_inc(next_in, 16)
                sp.wait_ge(Z["acc_done"], t * NSEL + 1 + FIRST)
                if before:
                    finish(t - 1)
                if after:
                    sp.dma_start(hp[:], X["h"][t + 1]).then_inc(h_in, 16)

            tiles(sp, tile)
            finish(T - 1)
            sp.wait_ge(out_done, 16 * T + FIRST)

        @block.tensor
        def _(pe):
            def transpose_next(t):
                pe.wait_ge(next_in, t * 16 + 16)
                for c in range(DC):
                    last = pe.transpose(p_t[:, c * P:(c + 1) * P], xn_next[:, c * P:(c + 1) * P], R["ident"][:])
                last.then_inc(Z["xt_done"], 1)

            def scores(t, j, cols, pair):
                r = t * PH + j
                pe.wait_ge(Z["xnt_ready"], t + 1 + FIRST)
                pe.wait_ge(Z["q_ready"], r + FIRST)
                matmuls(pe, p_q[:, 0:HQ], [(xnt[:, c * P:(c + 1) * P], wq[:, c, cols]) for c in range(DC)]).then_inc(Z["q_done"], 1)
                pe.wait_ge(Z["q_ready"], r + 1 + FIRST)
                pe.wait_ge(Z["qt_ready"], r + FIRST)
                for k in range(2):
                    last = pe.transpose(p_q[:, HQ + k * PC:HQ + (k + 1) * PC], q[:, k * PC:(k + 1) * PC], R["ident"][:])
                last.then_inc(Z["qt_done"], 1)
                pe.wait_ge(Z["qt_ready"], r + 1 + FIRST)
                pe.wait_ge(Z["s_ready"], r + FIRST)
                for k in range(2):
                    last = pe.matmul(p_s[:, k, :], qt[:, k * PC:(k + 1) * PC], keys[:, pair(k), :], start=True, stop=True)
                last.then_inc(Z["s_done"], 1)

            def heads(t, first, last):
                with pe.Fori(first, last) as j:
                    scores(t, j, bass.ds(j * HQ, HQ), lambda k: j * 2 + k)

            def transpose_sum(t):
                pe.wait_ge(Z["h2_ready"], t + 1 + FIRST)
                for c in range(DC):
                    last = pe.transpose(p_t[:, c * P:(c + 1) * P], h2[:, c * P:(c + 1) * P], R["ident"][:])
                last.then_inc(Z["h2t_done"], 1)

            def gate_product(t):
                pe.wait_ge(Z["h2t_ready"], t + 1 + FIRST)
                for half in range(2):
                    hs = slice(half * HB, (half + 1) * HB)
                    last = matmuls(pe, p_t[:, hs], [(o[:, c * P:(c + 1) * P], wg[:, c, hs]) for c in range(DC)])
                last.then_inc(Z["gate_done"], 1)

            def tile(t, before, after):
                scores(t, LEAD, slice(LEAD * HQ, (LEAD + 1) * HQ), lambda k: 2 * LEAD + k)
                if before:
                    transpose_sum(t - 1)
                    gate_product(t - 1)
                heads(t, LEAD + 1, PH)
                if after:
                    if before:
                        pe.wait_ge(Z["sg_ready"], t + FIRST)
                    else:
                        pe.wait_ge(Z["xnt_ready"], t + 1 + FIRST)
                    transpose_next(t + 1)
                    heads(t + 1, 0, LEAD)

            transpose_next(0)
            pe.wait_ge(first_in, 16 * len(first))
            scores(0, 0, slice(0, HQ), lambda k: k)
            pe.wait_ge(second_in, 16 * len(second))
            heads(0, 1, LEAD)
            pe.wait_ge(par_in, 16 * len(par))
            tiles(pe, tile)
            pe.wait_ge(Z["sg_ready"], T - 1 + FIRST)
            transpose_sum(T - 1)
            gate_product(T - 1)

        @block.scalar
        def _(act):
            def keep_transposed(t):
                act.wait_ge(Z["xt_done"], t + 1 + FIRST)
                act.wait_ge(Z["q_done"], t * PH + FIRST)
                ring(act, act.copy(xnt[:], p_t[:]), Z["xnt_ready"], t + 1)

            def keep_query(r):
                act.wait_ge(Z["q_done"], r + 1 + FIRST)
                act.wait_ge(Z["qt_done"], r + FIRST)
                ring(act, act.copy(q[:], p_q[:, 0:HQ]), Z["q_ready"], r + 1)
                act.wait_ge(Z["qt_done"], r + 1 + FIRST)
                act.wait_ge(Z["s_done"], r + FIRST)
                ring(act, act.copy(qt[:], p_q[:, HQ:2 * HQ]), Z["qt_ready"], r + 1)

            def keep_scores(r):
                act.wait_ge(Z["s_done"], r + 1 + FIRST)
                act.wait_ge(Z["searched"], r + FIRST)
                ring(act, act.copy(s[:], p_s[:]), Z["s_ready"], r + 1)

            def convert(r):
                act.wait_ge(Z["parts_ready"], r + 1 + FIRST)
                act.copy(part_f[:], part_u[:])
                act.mul(top_f[:, 0, :], top_at[:, 0, :], float(PK))
                ring(act, act.copy(top_f[:, 1, :], top_at[:, 1, :]), Z["converted"], r + 1)

            def exponentials(r):
                act.wait_ge(Z["best_ready"], r + 1 + FIRST)
                ring(act, act.mul(total[:, 0:1], best[:, 0:1], -1.0), Z["neg_ready"], r + 1)
                ring(act, act.activation(soft[:], best[:], ACT.Exp, bias=total[:, 0:1], scale=1.0, accum_out=total[:, 1:2]), Z["exp_ready"], r + 1)

            def gates(r, columns):
                act.wait_ge(Z["sum_ready"], r + 1 + FIRST)
                ring(act, act.mul(gate[:, columns], soft[:], total[:, 2:3]), Z["gate_ready"], r + 1)

            def next_input(t):
                act.wait_ge(next_in, t * 16 + 16)
                act.wait_ge(Z["dot_done"], t * NSEL + FIRST)
                ring(act, act.copy(xn[:], xn_next[:]), Z["xn_ready"], t + 1)

            def norm(t):
                act.wait_ge(Z["h2_ready"], t + 1 + FIRST)
                act.wait_ge(out_done, t * 16 + FIRST)
                ring(act, act.activation(o[:], h2[:], ACT.Square, accum_out=rms[:, 0:1]), Z["square_ready"], t + 1)
                ring(act, act.activation(rms[:, 1:2], rms[:, 0:1], ACT.Sqrt, scale=1.0 / D, bias=R["eps"][:]), Z["rms_ready"], t + 1)

            def keep_sum(t, part):
                act.wait_ge(Z["h2t_done"], t + 1 + FIRST)
                for c in range(part * DC // 2, (part + 1) * DC // 2):
                    ins = act.mul(o[:, c * P:(c + 1) * P], p_t[:, c * P:(c + 1) * P], R["col_ple"][:, c:c + 1])
                if part:
                    ring(act, ins, Z["h2t_ready"], t + 1)

            def sigmoid(t):
                act.wait_ge(Z["rstd_ready"], t + 1 + FIRST)
                act.wait_ge(Z["gate_done"], t + 1 + FIRST)
                ring(act, act.activation(o[:], p_t[:], ACT.Sigmoid, scale=rms[:, 2:3]), Z["sg_ready"], t + 1)

            def tile(t, before, after):
                def step(j):
                    c = t * PH + j
                    late = isinstance(j, int) and j >= PH - LEAD
                    first, second = isinstance(j, int) and j == 0, isinstance(j, int) and j == 1
                    head, r = ahead(t, j)
                    search = after or not late
                    for k in range(GROUPS):
                        act.wait_ge(Z["dot_done"], c * N + 2 * k + 2 + FIRST)
                        ring(act, act.activation(dots[:, 2 * k:2 * k + 2], dots[:, 2 * k:2 * k + 2], ACT.Gelu), Z["act_done"], c * GROUPS + k + 1)
                        for n in (2 * k, 2 * k + 1):
                            ins = act.mul(wts[:, n:n + 1], dots[:, n:n + 1], gate[:, part(j, n, 1)])
                        ring(act, ins, Z["wts_ready"], c * GROUPS + k + 1)
                        if k == 0 and search and late and head == 0:
                            keep_transposed(t + 1)
                        if k == 0 and before and first:
                            norm(t - 1)
                        if k == 1 and search:
                            keep_query(r)
                        if k == 2 and search:
                            keep_scores(r)
                        if k in (4, 5) and before and first:
                            keep_sum(t - 1, k - 4)
                        if k == 4 and before and second:
                            sigmoid(t - 1)
                        if k == 6 and search:
                            convert(r)
                            exponentials(r)
                        if k == 7 and search:
                            gates(r, part(head, 0, N))
                        if k == 7 and search and late and j == PH - 1:
                            next_input(t + 1)

                steps(act, step)

            act.wait_ge(next_in, 16)
            ring(act, act.copy(xn[:], xn_next[:]), Z["xn_ready"], 1)
            keep_transposed(0)
            for r in range(LEAD):
                keep_query(r)
                keep_scores(r)
                convert(r)
                exponentials(r)
                gates(r, part(r, 0, N))
            tiles(act, tile)
            norm(T - 1)
            keep_sum(T - 1, 0)
            keep_sum(T - 1, 1)
            sigmoid(T - 1)

        @block.vector
        def _(dve):
            order = Order(dve, Z["dve_step"])
            tt = dve.tensor_tensor
            grid = lambda ap: ap.rearrange("p (a b) -> p a b", a=TOPK)
            square, hots = [P, TOPK, TOPK], [P, TOPK, 2, TOPK]

            def top16(scores, values, where):
                for k in range(2):
                    eight = slice(8 * k, 8 * k + 8)
                    order(dve.max(values[:, eight], scores))
                    order(dve.max_index(where[:, eight], values[:, eight], scores))
                    if k == 0:
                        order(dve.match_replace(out=scores, in_to_replace=values[:, eight], in_values=scores, imm_value=-3e38))

            def search(r, half):
                if half == 0:
                    dve.wait_ge(Z["s_ready"], r + 1 + FIRST)
                order.hold()
                top16(s[:, half, :], top[:, half, :], top_at[:, half, :])

            def pairs(r):
                ring(dve, tt(grid(cand[:]), top[:, 0, :].unsqueeze(2).to_broadcast(square), top[:, 1, :].unsqueeze(1).to_broadcast(square), ALU.add),
                     Z["searched"], r + 1)
                dve.wait_ge(Z["gate_ready"], r + FIRST)
                order.hold()
                top16(cand[:], best[:], best_at[:])
                ring(dve, dve.tensor_scalar(part_u[:, 0, :], best_at[:], 4, None, ALU.logical_shift_right), Z["best_ready"], r + 1)
                ring(dve, dve.tensor_scalar(part_u[:, 1, :], best_at[:], 15, None, ALU.bitwise_and), Z["parts_ready"], r + 1)

            def choose(r, columns):
                dve.wait_ge(Z["converted"], r + 1 + FIRST)
                order(tt(hot[:], part_f[:].rearrange("p k a -> p a k").unsqueeze(3).to_broadcast(hots),
                         R["iota16"][:].unsqueeze(1).unsqueeze(1).to_broadcast(hots), ALU.is_equal))
                order(tt(hot[:], hot[:], top_f[:].unsqueeze(1).to_broadcast(hots), ALU.mult))
                ring(dve, dve.tensor_reduce(expert[:, columns], hot[:].rearrange("p a k b -> p a (k b)"), AX.X, ALU.add), Z["chosen"], r + 1)

            def reciprocal_sum(r):
                dve.wait_ge(Z["exp_ready"], r + 1 + FIRST)
                ring(dve, dve.reciprocal(total[:, 2:3], total[:, 1:2]), Z["sum_ready"], r + 1)

            def dot(c, n):
                lap = n // SLOTS
                dve.wait_ge(row_in[n % SLOTS], c * 32 + lap * 16 + 16)
                dve.wait_ge(Z["dot_done"], c * N + max(n - 1, 0) + FIRST)
                dve.scalar_tensor_tensor(out=prod[n % 2][:], in0=rows[:, n % SLOTS, 0:D], scalar=1.0, in1=xn[:], op0=ALU.mult, op1=ALU.mult,
                                         accum_out=dots[:, n:n + 1]).then_inc(Z["dot_done"], 1)

            def weigh(c, k, t=None):
                dve.wait_ge(Z["wts_ready"], c * GROUPS + k + 1 + FIRST)
                for n in (2 * k, 2 * k + 1):
                    sum_ = (acc, acc2)[n % 2]
                    row_v, weight = rows[:, n % SLOTS, D:2 * D], wts[:, n:n + 1]
                    dve.wait_ge(Z["acc_done"], c * N + max(n - 1, 0) + FIRST)
                    if t is not None and n == 0:
                        dve.wait_ge(h_in, t * 16 + 16)
                    if t is not None and n == 1:
                        ins = dve.tensor_scalar(sum_[:], row_v, weight, None, ALU.mult)
                    else:
                        ins = dve.scalar_tensor_tensor(out=sum_[:], in0=row_v, scalar=weight, in1=sum_[:] if t is None else hp[:], op0=ALU.mult, op1=ALU.add)
                    ins.then_inc(Z["acc_done"], 1)

            def reciprocal_rms(t):
                dve.wait_ge(Z["rms_ready"], t + 1 + FIRST)
                ring(dve, dve.reciprocal(rms[:, 2:3], rms[:, 1:2]), Z["rstd_ready"], t + 1)

            def output(t):
                dve.wait_ge(Z["sg_ready"], t + 1 + FIRST)
                dve.wait_ge(pp_in, t * 16 + 16)
                order(tt(o[:], o[:], hp[:], ALU.mult))
                ring(dve, tt(o[:], o[:], h2[:], ALU.add), Z["out_ready"], t + 1)

            def tile(t, before, after):
                def step(j):
                    c = t * PH + j
                    fixed = isinstance(j, int)
                    head, r = ahead(t, j)
                    searches = after or not (fixed and j >= PH - LEAD)
                    order.turn()
                    for k in range(GROUPS):
                        if k + 1 < GROUPS:
                            dot(c, 2 * k + 2)
                            dot(c, 2 * k + 3)
                        elif not (fixed and j == PH - 1):
                            dot(c + 1, 0)
                            dot(c + 1, 1)
                        weigh(c, k, t if fixed and j == 0 and k == 0 else None)
                        if k == 2 and before and fixed and j == 0:
                            reciprocal_rms(t - 1)
                        if k in (3, 4) and searches:
                            search(r, k - 3)
                        if k == 5 and searches:
                            pairs(r)
                        if k == 7 and before and fixed and j == 1:
                            output(t - 1)
                        if k == 7 and searches:
                            choose(r, part(head, 0, N))
                            reciprocal_sum(r)
                            order.hold()

                dve.wait_ge(Z["xn_ready"], t + 1 + FIRST)
                dot(t * PH, 0)
                dot(t * PH, 1)
                steps(dve, step)
                dve.wait_ge(Z["acc_done"], (t + 1) * NSEL + FIRST)
                order.turn()
                order(dve.tensor_copy(h2[:], acc[:]))
                ring(dve, tt(h2[:], h2[:], acc2[:], ALU.add), Z["h2_ready"], t + 1)

            for r in range(LEAD):
                order.turn()
                search(r, 0)
                search(r, 1)
                pairs(r)
                choose(r, part(r, 0, N))
                reciprocal_sum(r)
            tiles(dve, tile)
            reciprocal_rms(T - 1)
            output(T - 1)


SPILLS = {"xnt": [T, P, DC * P], "v": [T, P, RW], "kt": [T, P, RW], "yt": [T, P, 3 * RW], "pp": [T, P, D], "h": [T, P, D], "xn": [T, P, D]}


def build_program(nc, A, X=None):
    if X is None:
        X = {n: nc.dram_tensor(f"kept_{n}", s, F32).ap() for n, s in SPILLS.items()}
    with ExitStack() as ctx:
        R = {"semaphores": Semaphores()}
        for n, s, d in (("ident", [P, P], F32), ("eps", [P, 1], F32), ("col_mix", [P, DC], F32), ("col_ret", [P, RH], F32), ("col_ple", [P, DC], F32),
                        ("sink", [P, AH], F32), ("decays", [P, 40], F32), ("iota16", [P, TOPK], F32)):
            R[n] = ctx.enter_context(nc.sbuf_tensor("all_" + n, s, d))
        gates = ctx.enter_context(ExitStack())
        R["w_gates_first"] = gates.enter_context(nc.sbuf_tensor("gates_first", [P, DC, HB], F32))
        with ExitStack() as mixers:
            for n, s in (("decay_mask", [P, RH, P]), ("state_f", [P, T + 1, RW]), ("state_b", [P, T + 1, RW]), ("ka_t", [P, T + 2, P]), ("va", [P, T + 2, AKW]),
                         ("w_branches", [P, DC, KEPT * HB])):
                R[n] = mixers.enter_context(nc.sbuf_tensor("mix_" + n, s, F32))
            keys_stage(nc, A, R, X)
            R["semaphores"].clear(nc)
            branches_stage(nc, A, R, X)
            R["semaphores"].clear(nc)
        merge_stage(nc, A, R, X)
        gates.close()
        R["semaphores"].clear(nc)
        experts_stage(nc, A, R, X)


def constants():
    def rotary(dim):
        inv = (np.float32(1.0) / (np.float32(10000.0) ** (np.arange(0, dim, 2, dtype=np.float32) / np.float32(dim)))).astype(np.float32)
        ang = np.arange(S, dtype=np.float32)[:, None] * inv[None, :]
        return np.cos(ang).astype(np.float32), np.sin(ang).astype(np.float32)

    (cr, sr), (ca, sa) = rotary(RD), rotary(AD)
    scale = np.float32(RD ** -0.5)
    table = np.concatenate([cr, sr, cr * scale, sr * scale, ca, sa], axis=1).reshape(T, P, NR + NA)
    pos = np.arange(P)
    key = np.arange(WIN)
    near = np.abs(pos[:, None] + P - key[None, :]) <= P
    mask = np.empty((T, P, WIN), np.float32)
    for t in range(T):
        there = (t * P - P + key >= 0) & (t * P - P + key < S)
        mask[t] = np.where(near & there[None, :], 0.0, NEG)
    j, c = pos[:, None], pos[None, :]
    distance = np.stack([np.maximum(c - j, 0), np.maximum(j - c, 0)], axis=1).astype(np.float32)
    exponents = np.stack([P - 1 - pos, pos, pos + 1, P - pos], axis=1).astype(np.float32)
    return {"rotary": table, "window_mask": mask, "distance": distance, "exponent_col": exponents, "ident": np.eye(P, dtype=np.float32),
            "iota16": np.tile(np.arange(TOPK, dtype=np.float32), (P, 1))}


def layout(x, p, norm_mix, w_in, ret_decay, ret_norm, sgu_ln_g, sgu_ln_b, sgu_w, sgu_b, att_q_norm, att_k_norm, att_sink, w_proj_ret, w_proj_sgu,
           w_proj_att, w_out, norm_ffn, peer_wq, peer_keys, peer_u, peer_v, norm_ple, ple_gate, ple_proj):
    c = np.ascontiguousarray
    chunks = lambda w: c(np.asarray(w).reshape(-1, P, w.shape[-1]).transpose(1, 0, 2))
    col = lambda v: c(np.asarray(v).reshape(-1, P).T)
    w = np.asarray(w_in[0])
    offs = np.cumsum([0, RW, RW, RW, RW, G * GC, G * GC, AW, AKW, AKW, D, D, D])
    q_r, k_r, v_r, g_r, u_s, v_s, q_a, k_a, v_a, g0, g1, g2 = (w[:, offs[n]:offs[n + 1]] for n in range(12))
    heads = [n // 2 + (AH // AKV) * (n % 2) for n in range(AH)]
    by_head = [slice(n * AD, (n + 1) * AD) for n in heads]
    q_a = np.concatenate([q_a[:, s] for s in by_head], axis=1)
    wpa = np.concatenate([np.asarray(w_proj_att[0])[s] for s in by_head], axis=0)
    arrays = {
        "x": c(np.asarray(x[0]).reshape(T, P, D)),
        "p_t": c(np.asarray(p[0, 0]).reshape(T, P, 2, P).transpose(0, 3, 2, 1)),
        "w_keys": chunks(np.concatenate([k_r, v_r, k_a, v_a], axis=1)),
        "w_branches_kept": c(np.concatenate([q_a, q_r, v_s], axis=1).reshape(DC, P, KEPT * HB)), "w_branches_last": chunks(np.concatenate([u_s, g_r], axis=1)),
        "w_gates": chunks(np.concatenate([g0, g1, g2], axis=1)),
        "w_proj": chunks(np.concatenate([w_proj_ret[0], w_proj_sgu[0], wpa], axis=1)),
        "w_out": chunks(w_out[0]), "peer_wq": chunks(peer_wq[0]), "ple_gate": chunks(ple_gate[0]), "ple_proj": chunks(ple_proj[0]),
        "peer_keys_t": c(np.asarray(peer_keys[0]).reshape(2 * PH, PK, PC).transpose(2, 0, 1)),
        "peer_uv": np.concatenate([peer_u[0], peer_v[0]], axis=1),
        "norm_mix_col": col(norm_mix[0]), "ret_norm_col": col(ret_norm[0]), "norm_ple_col": col(norm_ple[0]), "norm_ffn": np.asarray(norm_ffn[0]),
        "ret_decay": np.asarray(ret_decay[0]).reshape(2 * RH), "att_sink": np.asarray(att_sink[0])[heads],
        "att_q_norm": np.asarray(att_q_norm[0]), "att_k_norm": np.asarray(att_k_norm[0]),
        "sgu_ln_g": np.asarray(sgu_ln_g[0]), "sgu_ln_b": np.asarray(sgu_ln_b[0]),
        "sgu_w_t": c(np.asarray(sgu_w[0]).transpose(2, 0, 1)), "sgu_b_col": c(np.asarray(sgu_b[0]).T),
    }
    return {n: c(a) for n, a in (arrays | constants()).items()}


def kernel(**inputs):
    import concourse.bacc as bacc
    from concourse.bass_utils import run_bass_kernel_spmd

    arrays = layout(**inputs)
    nc = bacc.Bacc("TRN2", target_bir_lowering=False, num_devices=1)
    A = {n: nc.dram_tensor(f"in_{n}", a.shape, mybir.dt.from_np(a.dtype), kind="ExternalInput").ap() for n, a in arrays.items()}
    A["out"] = nc.dram_tensor("out", (T, P, D), F32, kind="ExternalOutput").ap()
    build_program(nc, A)
    r = run_bass_kernel_spmd(nc, [{f"in_{n}": a for n, a in arrays.items()}], core_ids=[0])
    return r.results[0]["out"].reshape(1, S, D)
```
